# Optimizing a Trainium2 kernel written in Bass

```python
import jax, jax.numpy as jnp
from jax import lax
import numpy as np
import math

D_MODEL = 2048
BATCH = 1
SEQ = 256
DEPTH = 1

PLE_DIM = 256
BLK = 128
EPS = 1e-6

A_HEAD_DIM = 128
A_WIDTH = D_MODEL // 2
A_HEADS = A_WIDTH // A_HEAD_DIM
A_BRANCHES = ((128, 1), (512, 4), (2048, 16))

B_HEAD_DIM = 64
B_WIDTH = D_MODEL - A_WIDTH
B_HEADS = B_WIDTH // B_HEAD_DIM
B_GROUP = 8
B_KV_HEADS = B_HEADS // B_GROUP
B_WINDOW = 128

MIX_WIDTH = A_WIDTH + B_WIDTH
IN_COLS = 3 * A_WIDTH + B_WIDTH + 2 * B_KV_HEADS * B_HEAD_DIM

N_GROUPS = 4
EXPERTS_PER_GROUP = 8
N_EXPERTS = N_GROUPS * EXPERTS_PER_GROUP
TOP_K = 2
D_EXPERT = D_MODEL // 8


def rms_norm(x, g):
    xf = x.astype(jnp.float32)
    y = xf * lax.rsqrt(jnp.mean(xf * xf, axis=-1, keepdims=True) + EPS)
    return (y * g.astype(jnp.float32)).astype(x.dtype)

def alibi_slopes(n):
    return jnp.asarray(np.array([2.0 ** (-8.0 * (i + 1) / n) for i in range(n)], dtype=np.float32))

def _with_prev_block(xb):
    prev = jnp.pad(xb[:, :, :-1], ((0, 0), (0, 0), (1, 0), (0, 0), (0, 0)))
    return jnp.concatenate([prev, xb], axis=3)

def banded_attention(q, k, v, slopes, max_delta, stride, sinks=None):
    n, hkv, g, L, hd = q.shape
    nb = L // BLK
    qb = q.reshape(n, hkv, g, nb, BLK, hd)
    kb = _with_prev_block(k.reshape(n, hkv, nb, BLK, hd))
    vb = _with_prev_block(v.reshape(n, hkv, nb, BLK, hd))
    s = jnp.einsum('nkgbqd,nkbsd->nkgbqs', qb, kb,
                   preferred_element_type=jnp.float32) * (hd ** -0.5)
    qi = jnp.arange(L).reshape(nb, BLK)
    ki = qi[:, :1] - BLK + jnp.arange(2 * BLK)[None, :]
    delta = qi[:, :, None] - ki[:, None, :]
    valid = (delta >= 0) & (delta <= max_delta) & (ki[:, None, :] >= 0)
    s = s - slopes.astype(jnp.float32)[:, :, None, None, None] * (stride * delta).astype(jnp.float32)
    s = jnp.where(valid, s, -jnp.inf)
    m = jnp.max(s, axis=-1)
    if sinks is not None:
        sk = sinks.astype(jnp.float32)[:, :, None, None]
        m = jnp.maximum(m, sk)
    pr = jnp.exp(s - m[..., None])
    den = jnp.sum(pr, axis=-1)
    if sinks is not None:
        den = den + jnp.exp(sk - m)
    o = jnp.einsum('nkgbqs,nkbsd->nkgbqd', pr.astype(v.dtype), vb,
                   preferred_element_type=jnp.float32) / den[..., None]
    lse = m + jnp.log(den)
    return o.reshape(n, hkv, g, L, hd).astype(q.dtype), lse.reshape(n, hkv, g, L)

def dilated_branch(q, k, v, slopes, window, dilation):
    b, h, s, hd = q.shape
    span = dilation * BLK
    sp = -(-s // span) * span
    L = sp // dilation

    def to_residues(t):
        t = jnp.pad(t, ((0, 0), (0, 0), (0, sp - s), (0, 0)))
        t = t.reshape(b, h, L, dilation, hd).transpose(0, 3, 1, 2, 4)
        return t.reshape(b * dilation, h, L, hd)

    qr, kr, vr = to_residues(q), to_residues(k), to_residues(v)
    o, lse = banded_attention(qr[:, :, None], kr, vr, slopes[:, None], window // dilation, dilation)
    o = o[:, :, 0].reshape(b, dilation, h, L, hd).transpose(0, 2, 3, 1, 4).reshape(b, h, sp, hd)[:, :, :s]
    lse = lse[:, :, 0].reshape(b, dilation, h, L).transpose(0, 2, 3, 1).reshape(b, h, sp)[:, :, :s]
    return o, lse

def dilated_attention(q, k, v, slopes):
    outs, lses = [], []
    for window, dilation in A_BRANCHES:
        o, lse = dilated_branch(q, k, v, slopes, window, dilation)
        outs.append(o)
        lses.append(lse)
    w = jax.nn.softmax(jnp.stack(lses), axis=0)
    return jnp.einsum('rbhs,rbhsd->bhsd', w.astype(q.dtype), jnp.stack(outs))

def sink_window_attention(q, k, v, slopes, sinks):
    b, hq, s, hd = q.shape
    qg = q.reshape(b, B_KV_HEADS, B_GROUP, s, hd)
    o, _ = banded_attention(qg, k, v, slopes.reshape(B_KV_HEADS, B_GROUP), B_WINDOW - 1, 1,
                            sinks.reshape(B_KV_HEADS, B_GROUP))
    return o.reshape(b, hq, s, hd)

def hier_moe(x, w_grp, b_grp, w_exp, b_exp, w_gate, w_up, w_down):
    t = x.shape[0]
    grp_logits = jnp.dot(x, w_grp, preferred_element_type=jnp.float32) + b_grp.astype(jnp.float32)
    grp_prob = jax.nn.softmax(grp_logits, axis=-1)
    grp_idx = jnp.argmax(grp_logits, axis=-1)
    grp_w = jnp.take_along_axis(grp_prob, grp_idx[:, None], axis=-1)
    exp_logits = jnp.einsum('td,dge->tge', x, w_exp,
                            preferred_element_type=jnp.float32) + b_exp.astype(jnp.float32)
    in_grp = jnp.take_along_axis(exp_logits, grp_idx[:, None, None], axis=1)[:, 0]
    top_val, top_idx = lax.top_k(in_grp, TOP_K)
    top_w = jax.nn.softmax(top_val, axis=-1) * grp_w
    eid = grp_idx[:, None] * EXPERTS_PER_GROUP + top_idx
    combine = jnp.sum(jax.nn.one_hot(eid, N_EXPERTS, dtype=jnp.float32) * top_w[..., None], axis=1)
    hg = jnp.einsum('td,edf->tef', x, w_gate)
    hu = jnp.einsum('td,edf->tef', x, w_up)
    hid = jax.nn.silu(hg) * hu * combine.astype(x.dtype)[..., None]
    return jnp.einsum('tef,efd->td', hid, w_down)

def first_inputs(seed: int = 0) -> dict:
    key = jax.random.key(seed)
    ks = jax.random.split(key, 20)

    def nrm(k, shape, scale):
        return jax.random.normal(k, shape, jnp.float32) * scale

    return {
        "x": nrm(ks[0], (BATCH, SEQ, D_MODEL), 1.0),
        "p": nrm(ks[1], (DEPTH, BATCH, SEQ, PLE_DIM), 1.0),
        "w_in": nrm(ks[2], (DEPTH, D_MODEL, IN_COLS), D_MODEL ** -0.5),
        "w_out": nrm(ks[3], (DEPTH, MIX_WIDTH, D_MODEL), MIX_WIDTH ** -0.5),
        "sinks": nrm(ks[4], (DEPTH, B_HEADS), 1.0),
        "g_mix": 1.0 + nrm(ks[5], (DEPTH, D_MODEL), 0.02),
        "g_moe": 1.0 + nrm(ks[6], (DEPTH, D_MODEL), 0.02),
        "g_ple": 1.0 + nrm(ks[7], (DEPTH, D_MODEL), 0.02),
        "g_final": 1.0 + nrm(ks[8], (D_MODEL,), 0.02),
        "w_grp": nrm(ks[9], (DEPTH, D_MODEL, N_GROUPS), D_MODEL ** -0.5),
        "b_grp": nrm(ks[10], (DEPTH, N_GROUPS), 0.01),
        "w_exp": nrm(ks[11], (DEPTH, D_MODEL, N_GROUPS, EXPERTS_PER_GROUP), D_MODEL ** -0.5),
        "b_exp": nrm(ks[12], (DEPTH, N_GROUPS, EXPERTS_PER_GROUP), 0.01),
        "w_gate": nrm(ks[13], (DEPTH, N_EXPERTS, D_MODEL, D_EXPERT), D_MODEL ** -0.5),
        "w_up": nrm(ks[14], (DEPTH, N_EXPERTS, D_MODEL, D_EXPERT), D_MODEL ** -0.5),
        "w_down": nrm(ks[15], (DEPTH, N_EXPERTS, D_EXPERT, D_MODEL), D_EXPERT ** -0.5),
        "w_ple": nrm(ks[16], (DEPTH, PLE_DIM, D_MODEL), PLE_DIM ** -0.5),
        "w_ple_gate": nrm(ks[17], (DEPTH, D_MODEL, D_MODEL), D_MODEL ** -0.5),
    }

def first_block(x, p, w_in, w_out, sinks, g_mix, g_moe, g_ple, g_final, w_grp, b_grp,
              w_exp, b_exp, w_gate, w_up, w_down, w_ple, w_ple_gate):
    b, s, d = x.shape
    slopes_a = alibi_slopes(A_HEADS)
    slopes_b = alibi_slopes(B_HEADS)
    kv_w = B_KV_HEADS * B_HEAD_DIM
    splits = [A_WIDTH, 2 * A_WIDTH, 3 * A_WIDTH, 3 * A_WIDTH + B_WIDTH, 3 * A_WIDTH + B_WIDTH + kv_w]

    def heads(t, n, hd):
        return t.reshape(b, s, n, hd).transpose(0, 2, 1, 3)

    h = x
    for i in range(DEPTH):
        a = rms_norm(h, g_mix[i])
        proj = a @ w_in[i]
        qa, ka, va, qb, kb, vb = jnp.split(proj, splits, axis=-1)
        oa = dilated_attention(heads(qa, A_HEADS, A_HEAD_DIM), heads(ka, A_HEADS, A_HEAD_DIM),
                               heads(va, A_HEADS, A_HEAD_DIM), slopes_a)
        ob = sink_window_attention(heads(qb, B_HEADS, B_HEAD_DIM), heads(kb, B_KV_HEADS, B_HEAD_DIM),
                                   heads(vb, B_KV_HEADS, B_HEAD_DIM), slopes_b, sinks[i])
        mixed = jnp.concatenate([oa.transpose(0, 2, 1, 3).reshape(b, s, A_WIDTH),
                                 ob.transpose(0, 2, 1, 3).reshape(b, s, B_WIDTH)], axis=-1)
        h = h + mixed @ w_out[i]
        m = rms_norm(h, g_moe[i]).reshape(b * s, d)
        h = h + hier_moe(m, w_grp[i], b_grp[i], w_exp[i], b_exp[i],
                         w_gate[i], w_up[i], w_down[i]).reshape(b, s, d)
        n = rms_norm(h, g_ple[i])
        h = h + jax.nn.sigmoid(n @ w_ple_gate[i]) * (p[i] @ w_ple[i])
    return rms_norm(h, g_final)


DEPTH_2 = 2

N_REC = (DEPTH_2 + 1) // 2
N_ATT = DEPTH_2 // 2

RG_WIDTH = 2048
RG_HEADS = 8
RG_BLOCK = RG_WIDTH // RG_HEADS
CONV_WIDTH = 4
RG_C = 8.0

HG_HEADS = 16
HG_DK = 128
HG_DV = 128
HG_QK = HG_HEADS * HG_DK
HG_WIDTH = HG_HEADS * HG_DV
HG_CHUNK = 64

REC_IN = 2 * RG_WIDTH + 2 * HG_QK + 2 * HG_WIDTH
REC_OUT = RG_WIDTH + HG_WIDTH
REC_SPLITS = (RG_WIDTH, 2 * RG_WIDTH, 2 * RG_WIDTH + HG_QK,
              2 * RG_WIDTH + 2 * HG_QK, 2 * RG_WIDTH + 2 * HG_QK + HG_WIDTH)

ATT_HEADS = 8
ATT_DH = 128
ATT_QK = ATT_HEADS * 2 * ATT_DH
ATT_WIDTH = ATT_HEADS * 2 * ATT_DH
ATT_IN = 2 * ATT_QK + 2 * ATT_WIDTH
ATT_SPLITS = (ATT_QK, 2 * ATT_QK, 2 * ATT_QK + ATT_WIDTH)
ATT_BLOCK = 128
ROPE_DIM = ATT_DH // 4
ROPE_THETA = 500000.0

NORM_EPS = 1e-6
SUBLN_EPS = 1e-5


def rms_norm_2(x, g, eps=NORM_EPS):
    xf = x.astype(jnp.float32)
    y = xf * lax.rsqrt(jnp.mean(xf * xf, axis=-1, keepdims=True) + eps)
    return (y * g.astype(jnp.float32)).astype(x.dtype)

def causal_depthwise_conv(x, w, b):
    s = x.shape[1]
    xp = jnp.pad(x, ((0, 0), (CONV_WIDTH - 1, 0), (0, 0)))
    y = b
    for tap in range(CONV_WIDTH):
        y = y + xp[:, tap:tap + s] * w[tap]
    return y

def rg_lru(x, w_a, b_a, w_x, b_x, lam):
    bsz, s, _ = x.shape
    xb = x.reshape(bsz, s, RG_HEADS, RG_BLOCK)
    r = jax.nn.sigmoid(jnp.einsum('bshi,hij->bshj', xb, w_a).reshape(bsz, s, RG_WIDTH) + b_a)
    i = jax.nn.sigmoid(jnp.einsum('bshi,hij->bshj', xb, w_x).reshape(bsz, s, RG_WIDTH) + b_x)
    log_a = -RG_C * r.astype(jnp.float32) * jax.nn.softplus(-lam.astype(jnp.float32))
    a = jnp.exp(log_a)
    u = jnp.sqrt(-jnp.expm1(2.0 * log_a)) * (i * x).astype(jnp.float32)

    def combine(c1, c2):
        a1, u1 = c1
        a2, u2 = c2
        return a1 * a2, a2 * u1 + u2

    _, h = lax.associative_scan(combine, (a, u), axis=1)
    return h.astype(x.dtype)

def hgrn2_chunkwise(q, k, v, log_f):
    bsz, s, h, dk = q.shape
    dv = v.shape[-1]
    nc = s // HG_CHUNK

    def chunks(t):
        return t.reshape(bsz, nc, HG_CHUNK, h, t.shape[-1]).transpose(1, 0, 3, 2, 4)

    mask = jnp.tril(jnp.ones((HG_CHUNK, HG_CHUNK), dtype=bool))[:, :, None]

    def step(state, inp):
        qc, kc, vc, gc = inp
        b = jnp.cumsum(gc, axis=2)
        o_inter = jnp.einsum('bhtk,bhkv->bhtv', qc * jnp.exp(b), state)
        decay = jnp.exp(jnp.where(mask, b[:, :, :, None, :] - b[:, :, None, :, :], -jnp.inf))
        scores = jnp.einsum('bhtk,bhsk,bhtsk->bhts', qc, kc, decay)
        o = o_inter + jnp.einsum('bhts,bhsv->bhtv', scores, vc)
        b_last = b[:, :, -1:, :]
        state = (jnp.exp(b_last[:, :, 0, :, None]) * state
                 + jnp.einsum('bhsk,bhsv->bhkv', kc * jnp.exp(b_last - b), vc))
        return state, o

    s0 = jnp.zeros((bsz, h, dk, dv), jnp.float32)
    _, o = lax.scan(step, s0, (chunks(q), chunks(k), chunks(v), chunks(log_f)))
    return o.transpose(1, 0, 3, 2, 4).reshape(bsz, s, h, dv)

def partial_rope(x, pos):
    half = ROPE_DIM // 2
    inv_freq = ROPE_THETA ** (-jnp.arange(0, ROPE_DIM, 2, dtype=jnp.float32) / ROPE_DIM)
    ang = pos.astype(jnp.float32)[:, None] * inv_freq
    cos = jnp.cos(ang)[:, None, None, :]
    sin = jnp.sin(ang)[:, None, None, :]
    xr = x[..., :ROPE_DIM].astype(jnp.float32)
    x1, x2 = xr[..., :half], xr[..., half:]
    rot = jnp.concatenate([x1 * cos - x2 * sin, x2 * cos + x1 * sin], axis=-1)
    return jnp.concatenate([rot.astype(x.dtype), x[..., ROPE_DIM:]], axis=-1)

def diff_attention(q, k, v, lam):
    bsz, s, h, _, dh = q.shape
    nb = s // ATT_BLOCK
    scale = dh ** -0.5
    qb = q.reshape(bsz, nb, ATT_BLOCK, h, 2, dh).transpose(1, 0, 3, 4, 2, 5)
    kt = k.transpose(0, 2, 3, 1, 4)
    vt = v.transpose(0, 2, 1, 3)
    k_pos = jnp.arange(s)

    def one_block(args):
        q_blk, blk = args
        sc = jnp.einsum('bhiqd,bhikd->bhiqk', q_blk, kt).astype(jnp.float32) * scale
        q_pos = blk * ATT_BLOCK + jnp.arange(ATT_BLOCK)
        causal = k_pos[None, :] <= q_pos[:, None]
        p = jax.nn.softmax(jnp.where(causal, sc, -jnp.inf), axis=-1)
        attn = p[:, :, 0] - lam * p[:, :, 1]
        return jnp.einsum('bhqk,bhkv->bhqv', attn.astype(v.dtype), vt)

    o = lax.map(one_block, (qb, jnp.arange(nb)))
    return o.transpose(1, 0, 3, 2, 4).reshape(bsz, s, h, 2 * dh)

def second_inputs(seed: int = 0) -> dict:
    key = jax.random.key(seed)
    ks = jax.random.split(key, 24)
    f32 = jnp.float32

    def nrm(k, shape, scale):
        return jax.random.normal(k, shape, f32) * scale

    u = jax.random.uniform(ks[10], (N_REC, RG_WIDTH), f32, 0.9, 0.999)
    a0 = u ** (1.0 / RG_C)
    rg_lambda = jnp.log(a0) - jnp.log1p(-a0)
    return {
        'x': nrm(ks[0], (BATCH, SEQ, D_MODEL), 1.0),
        'rec_norm': 1.0 + nrm(ks[1], (N_REC, D_MODEL), 0.01),
        'rec_w_in': nrm(ks[2], (N_REC, D_MODEL, REC_IN), D_MODEL ** -0.5),
        'rg_conv_w': nrm(ks[3], (N_REC, CONV_WIDTH, RG_WIDTH), CONV_WIDTH ** -0.5),
        'rg_conv_b': nrm(ks[4], (N_REC, RG_WIDTH), 0.01),
        'rg_w_gate_a': nrm(ks[5], (N_REC, RG_HEADS, RG_BLOCK, RG_BLOCK), RG_BLOCK ** -0.5),
        'rg_b_gate_a': nrm(ks[6], (N_REC, RG_WIDTH), 0.01),
        'rg_w_gate_x': nrm(ks[7], (N_REC, RG_HEADS, RG_BLOCK, RG_BLOCK), RG_BLOCK ** -0.5),
        'rg_b_gate_x': nrm(ks[8], (N_REC, RG_WIDTH), 0.01),
        'rg_lambda': rg_lambda,
        'hg_lb': nrm(ks[11], (N_REC, HG_QK), 0.5),
        'hg_out_norm': 1.0 + nrm(ks[12], (N_REC, HG_DV), 0.01),
        'rec_w_out': nrm(ks[13], (N_REC, REC_OUT, D_MODEL), REC_OUT ** -0.5),
        'att_norm': 1.0 + nrm(ks[14], (N_ATT, D_MODEL), 0.01),
        'att_w_in': nrm(ks[15], (N_ATT, D_MODEL, ATT_IN), D_MODEL ** -0.5),
        'att_q_norm': 1.0 + nrm(ks[16], (N_ATT, ATT_DH), 0.01),
        'att_k_norm': 1.0 + nrm(ks[17], (N_ATT, ATT_DH), 0.01),
        'att_lambda': nrm(ks[18], (N_ATT, 4, ATT_DH), 0.1),
        'att_sub_norm': 1.0 + nrm(ks[19], (N_ATT, 2 * ATT_DH), 0.01),
        'att_w_out': nrm(ks[20], (N_ATT, ATT_WIDTH, D_MODEL), ATT_WIDTH ** -0.5),
    }

def second_block(x, rec_norm, rec_w_in, rg_conv_w, rg_conv_b, rg_w_gate_a, rg_b_gate_a,
              rg_w_gate_x, rg_b_gate_x, rg_lambda, hg_lb, hg_out_norm, rec_w_out,
              att_norm, att_w_in, att_q_norm, att_k_norm, att_lambda, att_sub_norm,
              att_w_out):
    bsz, s, _ = x.shape
    pos = jnp.arange(s)
    lb_all = jnp.cumsum(jax.nn.softmax(hg_lb.astype(jnp.float32), axis=0), axis=0)
    lb_all = lb_all - lb_all[0]

    for layer in range(DEPTH_2):
        j = layer // 2
        if layer % 2 == 0:
            h = rms_norm_2(x, rec_norm[j])
            proj = h @ rec_w_in[j]
            rg_x, rg_g, hg_q, hg_f, hg_i, hg_g = jnp.split(proj, REC_SPLITS, axis=-1)
            rg_x = causal_depthwise_conv(rg_x, rg_conv_w[j], rg_conv_b[j])
            rg_h = rg_lru(rg_x, rg_w_gate_a[j], rg_b_gate_a[j], rg_w_gate_x[j],
                          rg_b_gate_x[j], rg_lambda[j])
            y_a = rg_h * jax.nn.silu(rg_g)
            lb = lb_all[j]
            q = (jax.nn.silu(hg_q).astype(jnp.float32) * HG_DK ** -0.5).reshape(bsz, s, HG_HEADS, HG_DK)
            log_f = jnp.logaddexp(jnp.log(lb), jnp.log1p(-lb) + jax.nn.log_sigmoid(hg_f.astype(jnp.float32)))
            k = -jnp.expm1(log_f)
            o = hgrn2_chunkwise(q,
                                k.reshape(bsz, s, HG_HEADS, HG_DK),
                                hg_i.astype(jnp.float32).reshape(bsz, s, HG_HEADS, HG_DV),
                                log_f.reshape(bsz, s, HG_HEADS, HG_DK))
            o = rms_norm_2(o.astype(x.dtype), hg_out_norm[j])
            y_b = o.reshape(bsz, s, HG_WIDTH) * jax.nn.silu(hg_g)
            y = jnp.concatenate([y_a, y_b], axis=-1) @ rec_w_out[j]
        else:
            h = rms_norm_2(x, att_norm[j])
            proj = h @ att_w_in[j]
            q, k, v, g = jnp.split(proj, ATT_SPLITS, axis=-1)
            q = partial_rope(rms_norm_2(q.reshape(bsz, s, ATT_HEADS, 2, ATT_DH), att_q_norm[j]), pos)
            k = partial_rope(rms_norm_2(k.reshape(bsz, s, ATT_HEADS, 2, ATT_DH), att_k_norm[j]), pos)
            v = v.reshape(bsz, s, ATT_HEADS, 2 * ATT_DH)
            lam_init = 0.8 - 0.6 * math.exp(-0.3 * layer)
            lp = att_lambda[j].astype(jnp.float32)
            lam = jnp.exp(jnp.sum(lp[0] * lp[1])) - jnp.exp(jnp.sum(lp[2] * lp[3])) + lam_init
            o = diff_attention(q, k, v, lam)
            o = rms_norm_2(o, att_sub_norm[j], SUBLN_EPS) * (1.0 - lam_init)
            y = (o.reshape(bsz, s, ATT_WIDTH) * jax.nn.silu(g)) @ att_w_out[j]
        x = x + y.astype(x.dtype)
    return x


def setup_inputs(seed=0):
    out = dict(first_inputs(seed))
    for name, value in second_inputs(seed + 1).items():
        if name != "x":
            out[name + "_2"] = value
    return out


def reference(
    x, p, w_in, w_out, sinks, g_mix, g_moe, g_ple, g_final, w_grp, b_grp, w_exp, b_exp, w_gate,
    w_up, w_down, w_ple, w_ple_gate, rec_norm_2, rec_w_in_2, rg_conv_w_2, rg_conv_b_2,
    rg_w_gate_a_2, rg_b_gate_a_2, rg_w_gate_x_2, rg_b_gate_x_2, rg_lambda_2, hg_lb_2,
    hg_out_norm_2, rec_w_out_2, att_norm_2, att_w_in_2, att_q_norm_2, att_k_norm_2,
    att_lambda_2, att_sub_norm_2, att_w_out_2,
):
    x = first_block(
        x, p, w_in, w_out, sinks, g_mix, g_moe, g_ple, g_final, w_grp, b_grp, w_exp, b_exp,
        w_gate, w_up, w_down, w_ple, w_ple_gate,
    )
    return second_block(
        x, rec_norm_2, rec_w_in_2, rg_conv_w_2, rg_conv_b_2, rg_w_gate_a_2, rg_b_gate_a_2,
        rg_w_gate_x_2, rg_b_gate_x_2, rg_lambda_2, hg_lb_2, hg_out_norm_2, rec_w_out_2,
        att_norm_2, att_w_in_2, att_q_norm_2, att_k_norm_2, att_lambda_2, att_sub_norm_2,
        att_w_out_2,
    )


_drawn_inputs = setup_inputs


def setup_inputs(seed=0):
    import zlib

    import numpy as np

    out = dict(_drawn_inputs(seed))
    spreads = {}
    factors = {'g_ple': 8.0,
     'b_grp': 4.508,
     'b_exp': 3.9,
     'rec_norm_2': 7.664,
     'rg_conv_b_2': 3.224,
     'rg_b_gate_a_2': 8.0,
     'rg_b_gate_x_2': 8.0,
     'hg_out_norm_2': 8.0,
     'att_norm_2': 8.0,
     'att_q_norm_2': 8.0,
     'att_k_norm_2': 8.0,
     'att_sub_norm_2': 8.0}
    for name, (base, spread) in spreads.items():
        noise = np.random.default_rng([zlib.crc32(name.encode()), seed]).standard_normal(out[name].shape)
        drawn = base * np.exp(spread * noise) if base else spread * noise
        out[name] = __import__('jax').numpy.asarray(drawn.astype(out[name].dtype))
    for name, factor in factors.items():
        out[name] = (out[name] * factor).astype(out[name].dtype)
    return out
```

```python
from contextlib import ExitStack, contextmanager
import math

import numpy as np

import concourse.bass as bass
from concourse import mybir

F32 = mybir.dt.float32
F32R = mybir.dt.float32r
I32 = mybir.dt.int32
U32 = mybir.dt.uint32
ALU = mybir.AluOpType
ACT = mybir.ActivationFunctionType
AX = mybir.AxisListType

P = 128
D = 2048
T = 256
NT = T // P
KD = D // P
W = 512
UNIT_K = 2
RING = 4
UNITS = KD // UNIT_K
EPS = 1e-6
BIG = 1e30

A_HEADS = 8
A_DIM = 128
B_HEADS = 16
B_DIM = 64
B_GROUP = 8
N_GROUPS = 4
PER_GROUP = 8
N_EXPERTS = 32
D_EXPERT = 256
ROUTES = N_GROUPS + N_EXPERTS
PLE_DIM = 256
CONV = 4
ATT_LAYER = 1
LAM_INIT = 0.8 - 0.6 * math.exp(-0.3 * ATT_LAYER)
ROPE = 32
HALF = ROPE // 2
HG_CHUNK = 64
LEVELS = (1, 2, 4, 8, 16, 32, 64)
SCORE = 3 * P


def tables():
    p = np.arange(P)[:, None]
    parts = {}
    parts["ident"] = np.eye(P)
    parts["iota"] = np.broadcast_to(np.arange(P)[None, :], (P, P))
    parts["before"] = (p < np.arange(P)[None, :]).astype(float)
    parts["ones"] = np.ones((P, P))
    inv = 500000.0 ** (-np.arange(0, ROPE, 2, dtype=np.float32) / np.float32(ROPE))
    ang = np.stack([(p + t * P) * inv[None, :] for t in range(NT)], 1).astype(np.float32)
    parts["cos"] = np.cos(ang).reshape(P, -1)
    parts["sin"] = np.sin(ang).reshape(P, -1)
    parts["index"] = np.broadcast_to(np.arange(N_EXPERTS)[None, :], (P, N_EXPERTS))
    wide = P + p - np.arange(2 * P)[None, :]
    delta = np.concatenate([wide, wide[:, P:]], 1)
    seen = delta >= 0
    count = (seen & (delta <= 128)).astype(int) + (seen & (delta % 4 == 0)) + (seen & (delta % 16 == 0))
    parts["delta"] = delta
    parts["branches"] = np.where(count > 0, np.log(np.maximum(count, 1)), -BIG)
    parts["window"] = np.where(seen & (delta < 128), 0.0, -BIG)
    parts["causal"] = np.where(seen, 0.0, -BIG)
    s, t = p, np.arange(P)[None, :]
    for m in LEVELS:
        parts[f"level{m}"] = ((s // (2 * m) == t // (2 * m)) & (s % (2 * m) < m) & (t % (2 * m) >= m)).astype(float)
    parts["level0"] = np.eye(P)
    parts["reset"] = np.broadcast_to((np.arange(4 * T)[None, :] % HG_CHUNK != 0).astype(float), (P, 4 * T))
    at, n = {}, 0
    for name, a in parts.items():
        at[name] = (n, a.shape[1])
        n += a.shape[1]
    return np.concatenate([np.asarray(a, np.float32) for a in parts.values()], 1).astype(np.float32), at


class Flow:

    def __init__(self):
        self.u, self.c, self.terms = 0, 0, []

    def unit(self, j=0, scale=1):
        v = (self.u + j) * scale
        for reg, units, _ in self.terms:
            v = reg * (units * scale) + v
        return v

    def turn(self, j):
        v = 32 * ((self.u + j) // RING) + 32
        for reg, units, _ in self.terms:
            v = reg * (units // RING * 32) + v
        return v

    def chunk(self):
        v = self.c
        for reg, _, chunks in self.terms:
            v = reg * chunks + v
        return v

    def next(self, units):
        self.u += units
        self.c += 1

    @contextmanager
    def loop(self, eng, trips, units, chunks):
        assert units % RING == 0 and chunks % 2 == 0
        u, c = self.u, self.c
        with eng.Fori(0, trips) as i:
            self.terms.append((i, units, chunks))
            yield i
            self.terms.pop()
        assert (self.u - u, self.c - c) == (units, chunks), (self.u - u, self.c - c)
        self.u, self.c = u + trips * units, c + trips * chunks

    @contextmanager
    def optional(self, eng, flag, units, chunks):
        u, c = self.u, self.c
        with eng.If(flag > 0):
            yield
        assert (self.u - u, self.c - c) == (units, chunks)
        self.u, self.c = u, c
        self.terms.append((flag, units, chunks))


def program(nc, d, tab_at, out):
    ctx = ExitStack()
    with ctx:
        def sb(name, shape, dt=F32):
            return ctx.enter_context(nc.sbuf_tensor(name, shape, dt))

        def sem(name):
            return ctx.enter_context(nc.semaphore(name))

        raw = sb("raw", [P, RING, UNIT_K, W])
        w_hi = sb("w_hi", [P, RING, UNIT_K, W], F32R)
        w_lo = sb("w_lo", [P, RING, UNIT_K, W], F32R)
        x_hi = sb("x_hi", [P, KD, T], F32R)
        x_lo = sb("x_lo", [P, KD, T], F32R)
        y_hi = sb("y_hi", [P, KD, T], F32R)
        y_lo = sb("y_lo", [P, KD, T], F32R)
        e_hi = sb("e_hi", [P, D], F32R)
        e_lo = sb("e_lo", [P, D], F32R)
        select = sb("select", [P, NT, P], F32R)
        select_t = sb("select_t", [P, T], F32R)
        h = sb("h", [P, NT, D])
        work = sb("work", [P, 12800])
        keep_n = tab_at["delta"][0]
        keep = sb("keep", [P, keep_n])
        cols = sb("cols", [P, 208])
        rows = sb("rows", [P, 16 + 36 + 128 * 3 + 256])
        small = sb("small", [P, 96])
        ovf = sb("ovf", [P, 2], I32)
        out_ps = [ctx.enter_context(nc.psum_tensor(f"out_ps{i}", [P, 2, W], F32)) for i in range(2)]
        mix = ctx.enter_context(nc.psum_tensor("mix", [P, 4, W], F32))

        def kept(name):
            a, n = tab_at[name]
            return keep[:, a:a + n]

        ident = kept("ident")

        def wk(a, n):
            return work[:, a:a + n]

        def bank(b, a=0, n=W):
            return mix[:, b, a:a + n]

        vec_names = ["g_mix", "g_moe", "g_ple", "rec_norm_2", "att_norm_2", "rg_lambda_2", "rg_b_gate_a_2",
                     "rg_b_gate_x_2"]
        col = {n: cols[:, KD * i:KD * i + KD] for i, n in enumerate(vec_names)}
        conv_w = cols[:, 128:192].rearrange("p (t k) -> p t k", t=CONV)
        conv_b = cols[:, 192:208]
        sinks = rows[:, 0:16]
        route_b = rows[:, 16:52]
        hg_gain = rows[:, 52:180]
        q_gain = rows[:, 180:308]
        k_gain = rows[:, 308:436]
        sub_gain = rows[:, 436:692]

        raw_ready = [sem(f"raw_ready{i}") for i in range(RING)]
        low_ready = sem("low_ready")
        high_ready = sem("high_ready")
        unit_used = sem("unit_used")
        out_free = sem("out_free")
        start_loads = sem("start_loads")
        row_loads = sem("row_loads")
        vecs_turned = sem("vecs_turned")
        vecs_ready = sem("vecs_ready")

        def load_unit(sp, fl, j, sources):
            slot = (fl.u + j) % RING
            sp.wait_ge(low_ready, fl.unit(j) + 1)
            for r, (src, a, n) in enumerate(sources):
                sp.dma_start(raw[:, slot, r, a:a + n] if a is not None else raw[:, slot, :, n:n + D_EXPERT],
                             src).then_inc(raw_ready[slot], 16)

        def load_chunk(sp, fl, wt, row, c0, units=UNITS, n=W):
            for j in range(units):
                load_unit(sp, fl, j, [(wt[bass.ds(row + (UNIT_K * j + r) * P, P), bass.ds(c0, n)], 0, n)
                                      for r in range(UNIT_K)])
            fl.next(units)

        def high(act, fl, j, n=W):
            slot = (fl.u + j) % RING
            act.wait_ge(raw_ready[slot], fl.turn(j))
            act.wait_ge(unit_used, fl.unit(j) + 1)
            act.activation(w_hi[:, slot, :, 0:n], raw[:, slot, :, 0:n], ACT.Copy).then_inc(high_ready, 1)

        def low(dve, fl, j, n=W):
            slot = (fl.u + j) % RING
            dve.wait_ge(high_ready, fl.unit(j) + 1)
            dve.tensor_tensor(w_lo[:, slot, :, 0:n], raw[:, slot, :, 0:n], w_hi[:, slot, :, 0:n],
                              ALU.subtract).then_inc(low_ready, 1)

        def splits(part, eng, fl, units=UNITS, n=W, between=None):
            for j in range(units):
                if j == RING and between:
                    between()
                part(eng, fl, j, n)
            fl.next(units)

        def chunk_done(eng, fl, units_after=0):
            eng.wait_ge(unit_used, fl.unit(-units_after) + RING)

        def chunk_ps(fl, chunks_after=0):
            return out_ps[(fl.c - 1 - chunks_after) % 2]

        def product(pe, fl, acts, units=UNITS, n=W, tiles=NT, by_channel=False, after=()):
            ps = out_ps[fl.c % 2]
            pe.wait_ge(out_free, fl.chunk() + 1)
            last = UNIT_K * units - 1
            for j in range(units):
                for at, what in after:
                    if at == j:
                        what()
                slot = (fl.u + j) % RING
                pe.wait_ge(low_ready, fl.unit(j) + 1 + RING)
                for r in range(UNIT_K):
                    k = UNIT_K * j + r
                    for t in range(n // P if by_channel else tiles):
                        if by_channel:
                            o = ps[:, t // 2, (t % 2) * T:(t % 2) * T + T]
                            ws = slice(t * P, t * P + P)
                            pairs = [(w_hi[:, slot, r, ws], acts[0](k)), (w_hi[:, slot, r, ws], acts[1](k)),
                                     (w_lo[:, slot, r, ws], acts[0](k))]
                            first = k == 0 and t % 2 == 0
                        else:
                            o = ps[:, t, 0:n]
                            pairs = [(acts[0](k, t), w_hi[:, slot, r, 0:n]), (acts[0](k, t), w_lo[:, slot, r, 0:n]),
                                     (acts[1](k, t), w_hi[:, slot, r, 0:n])]
                            first = k == 0
                        for q, (lhs, rhs) in enumerate(pairs):
                            mm = pe.matmul(o, lhs, rhs, start=first and q == 0, stop=k == last and q == 2,
                                           skip_group_check=by_channel)
                mm.then_inc(unit_used, 1)
            fl.next(units)

        def tokens_of(hi, lo):
            return [lambda k, t=None, a=a: a[:, k, :] if t is None else a[:, k, t * P:t * P + P] for a in (hi, lo)]

        x_parts = tokens_of(x_hi, x_lo)
        y_parts = tokens_of(y_hi, y_lo)

        class Norm:

            def __init__(self, gain, squares, norms_before, rows_before, turns_before):
                self.gain, self.squares = gain, squares
                self.n, self.rows, self.turns = norms_before, rows_before, (turns_before or 0) * (KD // 2)

        norms = {"mix": Norm("g_mix", 4096, 0, 0, 0), "moe": Norm(None, 9216, 1, None, 1),
                 "ple": Norm("g_ple", 8704, 2, 1, 2), "final": Norm(None, 8704, 3, None, None),
                 "rec": Norm("rec_norm_2", 8704, 4, 2, 3), "att": Norm("att_norm_2", 4096, 5, 3, 4)}
        norm_s = {n: sem(f"norm_{n}") for n in ("h", "sums", "var", "root", "scale", "rows0", "rows1", "turned", "high",
                                           "low")}
        sum_sq, var, root, scale = (small[:, 2 * i:2 * i + 2] for i in range(4))
        xn = wk(0, NT * D).rearrange("p (t d) -> p t d", t=NT)

        def norm_stats_act(act, nm):
            act.wait_ge(norm_s["h"], nm.n + 1)
            for t in range(NT):
                act.activation(wk(nm.squares, D), h[:, t, :], ACT.Square, accum_out=sum_sq[:, t:t + 1])
                act.drain()
            act.drain().then_inc(norm_s["sums"], 1)
            act.wait_ge(norm_s["var"], nm.n + 1)
            act.activation(root, var, ACT.Sqrt).then_inc(norm_s["root"], 1)

        def norm_stats_dve(dve, nm):
            dve.drain().then_inc(norm_s["h"], 1)
            dve.wait_ge(norm_s["sums"], nm.n + 1)
            dve.tensor_scalar(var, sum_sq, 1.0 / D, EPS, ALU.mult, ALU.add).then_inc(norm_s["var"], 1)
            dve.wait_ge(norm_s["root"], nm.n + 1)
            dve.reciprocal(scale, root).then_inc(norm_s["scale"], 1)

        def norm_act(act, nm):
            norm_stats_act(act, nm)
            act.wait_ge(norm_s["scale"], nm.n + 1)
            act.activation(xn[:, 0, :], h[:, 0, :], ACT.Copy, scale=scale[:, 0:1]).then_inc(norm_s["rows0"], 1)
            for f in range(KD // 2):
                act.wait_ge(norm_s["turned"], nm.turns + f + 1)
                for kk in range(2):
                    k = 2 * f + kk
                    g = {"scale": col[nm.gain][:, k:k + 1]} if nm.gain else {}
                    i = act.activation(x_hi[:, k, :], bank(f % 4, kk * T, T), ACT.Copy, **g)
                i.then_inc(norm_s["high"], 1)

        def norm_dve(dve, nm):
            norm_stats_dve(dve, nm)
            dve.wait_ge(norm_s["scale"], nm.n + 1)
            dve.tensor_scalar(xn[:, 1, :], h[:, 1, :], scale[:, 1:2], None, ALU.mult).then_inc(norm_s["rows1"], 1)
            norm_low(dve, nm)

        def norm_low(dve, nm):
            for f in range(KD // 2):
                dve.wait_ge(norm_s["high"], nm.turns + f + 1)
                for kk in range(2):
                    k = 2 * f + kk
                    src = bank(f % 4, kk * T, T)
                    if nm.gain:
                        i = dve.scalar_tensor_tensor(x_lo[:, k, :], src, col[nm.gain][:, k:k + 1], x_hi[:, k, :],
                                                     ALU.mult, ALU.subtract)
                    else:
                        i = dve.tensor_tensor(x_lo[:, k, :], src, x_hi[:, k, :], ALU.subtract)
                i.then_inc(norm_s["low"], 1)

        def norm_pe(pe, nm, rows=None):
            for rows_of in [rows] if rows else [norm_s["rows0"], norm_s["rows1"]]:
                pe.wait_ge(rows_of, (nm.rows or 0) + 1)
            for f in range(KD // 2):
                if f >= 4:
                    pe.wait_ge(norm_s["low"], nm.turns + f - 3)
                for kk in range(2):
                    for t in range(NT):
                        k = 2 * f + kk
                        i = pe.transpose(bank(f % 4, kk * T + t * P, P), xn[:, t, k * P:k * P + P], ident)
                i.then_inc(norm_s["turned"], 1)
            pe.wait_ge(norm_s["low"], nm.turns + KD // 2)

        qk = wk(0, 16 * T).rearrange("p (n t) -> p n t", t=T)
        va = wk(4096, NT * 1024).rearrange("p (t n) -> p t n", t=NT)
        qb = wk(6144, 8 * T).rearrange("p (n t) -> p n t", t=T)
        kb = wk(8192, 2 * T).rearrange("p (n t) -> p n t", t=T)
        vb = wk(8704, NT * P).rearrange("p (t n) -> p t n", t=NT)
        bias_tabs = wk(8960, 3 * SCORE)
        t_delta, t_branches, t_window = (wk(8960 + SCORE * i, SCORE) for i in range(3))
        head_bias = wk(10112, SCORE)
        probs = [wk(10496 + SCORE * i, SCORE) for i in range(2)]
        probs_t = [wk(11264 + SCORE * i, SCORE) for i in range(2)]
        heads_o = [wk(12032 + T * i, T).rearrange("p (t n) -> p t n", t=NT) for i in range(2)]
        a_nmax, a_den, a_rden, a_sink = ([small[:, 8 + 4 * i + 2 * j:10 + 4 * i + 2 * j] for j in range(2)]
                                         for i in range(4))
        s_scores = sem("attn_scores")
        s_bank = sem("attn_scores_read")
        s_max = sem("attn_max")
        s_exp = sem("attn_probs")
        s_pt = sem("attn_turned")
        s_ptc = sem("attn_turned_copied")
        s_o = sem("attn_out")
        s_on = sem("attn_out_scaled")
        s_ot = sem("attn_out_turned")
        s_oh = sem("attn_out_high")
        s_ol = sem("attn_out_low")
        p1_copied = sem("proj_copied")
        keys_doubled = sem("keys_doubled")
        HEADS = [("a", i) for i in range(A_HEADS)] + [("b", i) for i in range(B_HEADS)]
        TILES_A = A_HEADS
        S_SCALE = {"a": A_DIM ** -0.5, "b": B_DIM ** -0.5}
        SLOPE = {"a": [2.0 ** (-8.0 * (i + 1) / A_HEADS) for i in range(A_HEADS)],
                 "b": [2.0 ** (-8.0 * (i + 1) / B_HEADS) for i in range(B_HEADS)]}

        def out_tile(n):
            kind, i = HEADS[n]
            if kind == "a":
                return i
            return TILES_A + i // 2 if i % 2 else None

        def attn_pe(pe):
            pe.wait_ge(p1_copied, 9)
            pe.wait_ge(keys_doubled, 32)
            tiles_out = 0

            def scores(n):
                kind, i = HEADS[n]
                if n >= 2:
                    pe.wait_ge(s_bank, n - 1)
                if kind == "a":
                    q, k, lo, hi = qk[:, i, :], qk[:, A_HEADS + i, :], 0, P
                else:
                    lo = B_DIM * (i % 2)
                    hi = lo + B_DIM
                    q, k = qb[:, i // 2, :], kb[:, i // B_GROUP, :]
                pe.matmul(bank(n % 2, 0, T), q[lo:hi, P:T], k[lo:hi, :], start=True, stop=True)
                pe.matmul(bank(n % 2, T, P), q[lo:hi, 0:P], k[lo:hi, 0:P], start=True,
                          stop=True).then_inc(s_scores, 1)

            scores(0)
            for n, (kind, i) in enumerate(HEADS):
                if n + 1 < len(HEADS):
                    scores(n + 1)
                pe.wait_ge(s_exp, n + 1)
                if n:
                    pe.wait_ge(s_ptc, n)
                for b in range(3):
                    m = pe.transpose(bank(2, b * P, P), probs[n % 2][:, b * P:b * P + P], ident)
                m.then_inc(s_pt, 1)
                pe.wait_ge(s_ptc, n + 1)
                pt = probs_t[n % 2]
                if n:
                    pe.wait_ge(s_on, n)
                if tiles_out:
                    pe.wait_ge(s_ol, tiles_out)
                if kind == "a":
                    v, w = va[:, :, i * A_DIM:(i + 1) * A_DIM], A_DIM
                else:
                    g = i // B_GROUP
                    v, w = vb[:, :, g * B_DIM:(g + 1) * B_DIM], B_DIM
                pe.matmul(bank(3, P, w), pt[:, 0:P], v[:, 0, :], start=True, stop=False)
                pe.matmul(bank(3, P, w), pt[:, P:T], v[:, 1, :], start=False, stop=True)
                pe.matmul(bank(3, 0, w), pt[:, T:SCORE], v[:, 0, :], start=True, stop=True).then_inc(s_o, 1)
                if out_tile(n) is not None:
                    pe.wait_ge(s_on, n + 1)
                    o = heads_o[out_tile(n) % 2]
                    for t in range(NT):
                        m = pe.transpose(bank(3, T + t * P, P), o[:, t, :], ident)
                    m.then_inc(s_ot, 1)
                    tiles_out += 1
            pe.wait_ge(s_ol, KD)

        def attn_act(act):
            for n, (kind, i) in enumerate(HEADS):
                pr, nm, den = probs[n % 2], a_nmax[n % 2], a_den[n % 2]
                act.wait_ge(s_max, n + 1)
                act.activation(pr[:, 0:T], pr[:, 0:T], ACT.Exp, bias=nm[:, 1:2], accum_out=den[:, 1:2])
                e = act.activation(pr[:, T:SCORE], pr[:, T:SCORE], ACT.Exp, bias=nm[:, 0:1],
                                   accum_out=den[:, 0:1])
                if kind == "b":
                    e = act.activation(a_sink[n % 2], nm, ACT.Exp, bias=sinks[:, i:i + 1])
                e.then_inc(s_exp, 1)
                act.wait_ge(s_pt, n + 1)
                act.activation(probs_t[n % 2], bank(2, 0, SCORE), ACT.Copy).then_inc(s_ptc, 1)
                tile = out_tile(n)
                if tile is not None:
                    act.wait_ge(s_ot, tile + 1)
                    act.activation(y_hi[:, tile, :], bank(3, T, T), ACT.Copy).then_inc(s_oh, 1)

        def attn_dve(dve):
            dve.wait_ge(row_loads, 16 * 8)

            def bias_and_max(n):
                kind, i = HEADS[n]
                b = n % 2
                dve.scalar_tensor_tensor(head_bias, t_delta, -SLOPE[kind][i],
                                         t_branches if kind == "a" else t_window, ALU.mult, ALU.add)
                dve.wait_ge(s_scores, n + 1)
                if n >= 2:
                    dve.wait_ge(s_pt, n - 1)
                dve.drain()
                dve.scalar_tensor_tensor(probs[b], bank(b, 0, SCORE), S_SCALE[kind], head_bias, ALU.mult,
                                         ALU.add).then_inc(s_bank, 1)
                dve.drain()
                nm = a_nmax[b]
                dve.tensor_reduce(nm[:, 1:2], probs[b][:, 0:T], AX.X, ALU.max)
                dve.tensor_reduce(nm[:, 0:1], probs[b][:, T:SCORE], AX.X, ALU.max)
                dve.drain()
                if kind == "b":
                    dve.tensor_scalar(nm, nm, sinks[:, i:i + 1], -1.0, ALU.max, ALU.mult)
                else:
                    dve.tensor_scalar(nm, nm, -1.0, None, ALU.mult)
                dve.drain().then_inc(s_max, 1)

            bias_and_max(0)
            for n, (kind, i) in enumerate(HEADS):
                b = n % 2
                if n + 1 < len(HEADS):
                    bias_and_max(n + 1)
                dve.wait_ge(s_exp, n + 1)
                if kind == "b":
                    dve.tensor_tensor(a_den[b], a_den[b], a_sink[b], ALU.add)
                    dve.drain()
                dve.reciprocal(a_rden[b], a_den[b])
                dve.drain()
                dve.wait_ge(s_o, n + 1)
                if kind == "a":
                    tile, lo, w = i, 0, A_DIM
                else:
                    tile, lo, w = TILES_A + i // 2, B_DIM * (i % 2), B_DIM
                o = heads_o[tile % 2]
                for t in range(NT):
                    m = dve.tensor_scalar(o[:, t, lo:lo + w], bank(3, t * P, w), a_rden[b][:, t:t + 1], None, ALU.mult)
                m.then_inc(s_on, 1)
                if out_tile(n) is not None:
                    dve.wait_ge(s_oh, tile + 1)
                    dve.tensor_tensor(y_lo[:, tile, :], bank(3, T, T), y_hi[:, tile, :],
                                      ALU.subtract).then_inc(s_ol, 1)

        def add_to_h(dve, fl, c, done=None):
            chunk_done(dve, fl)
            hs = h[:, :, c * W:(c + 1) * W]
            dve.tensor_tensor(hs, chunk_ps(fl)[:], hs, ALU.add).then_inc(out_free, 1)

        gain_row = wk(4096, D)
        route_raw = wk(6144, KD * ROUTES).rearrange("p (k n) -> p k n", n=ROUTES)
        route_hi = e_hi[:, 0:KD * ROUTES].rearrange("p (k n) -> p k n", n=ROUTES)
        route_lo = e_lo[:, 0:KD * ROUTES].rearrange("p (k n) -> p k n", n=ROUTES)

        def tile2(a, n):
            return wk(a, NT * n).rearrange("p (t n) -> p t n", t=NT)

        logits = tile2(6720, ROUTES)
        m_off = tile2(6792, ROUTES)
        em = tile2(6864, N_EXPERTS)
        em2 = tile2(6928, N_EXPERTS)
        eq = tile2(6992, N_EXPERTS)
        cand = tile2(7056, N_EXPERTS)
        oh1 = tile2(7120, N_EXPERTS)
        oh2 = tile2(7184, N_EXPERTS)
        combine = tile2(7248, N_EXPERTS)
        g_eq = tile2(7312, N_GROUPS)
        g_cand = tile2(7320, N_GROUPS)
        g_one = tile2(7328, N_GROUPS)
        g_exp = tile2(7336, N_GROUPS)
        (gmax, gidx, gsum, gw, m1, m2, c1, c2, dm, e2, den2, w1, w2, key, cur, rank) = (
            wk(7344 + 2 * i, 2) for i in range(16))
        counts, over4, over4i = wk(7376, 4), wk(7380, 4), wk(7384, 4)
        ovf_f, ovf_base = wk(7388, 2), wk(7390, 1)
        comb_rows = wk(7392, PER_GROUP)
        select_f = wk(7424, NT * P).rearrange("p (t n) -> p t n", t=NT)
        silu_g = [wk(7936 + D_EXPERT * i, D_EXPERT) for i in range(2)]
        hidden = [wk(8448 + D_EXPERT * i, D_EXPERT) for i in range(2)]
        xg_hi, xg_lo = (a[:].rearrange("p k t -> p (k t)") for a in (x_hi, x_lo))
        m_hi, m_lo = (a[:].rearrange("p k t -> p (k t)").rearrange("p (t d) -> p t d", t=NT) for a in (y_hi, y_lo))

        m_rows = sem("moe_rows")
        m_split_hi = sem("moe_rows_high")
        r_whi = sem("route_weights_high")
        r_wlo = sem("route_weights_low")
        moe_loads = sem("moe_loads")
        region_free = sem("attention_memory_free")
        r_out = sem("route_logits")
        r_gsub = sem("route_group_shifted")
        r_gexp = sem("route_group_exp")
        r_dm = sem("route_top_shifted")
        r_de = sem("route_top_exp")
        r_one = sem("route_one_hot")
        r_rank = sem("route_ranks")
        r_done = sem("route_done")
        sel_ready = sem("select_ready")
        sel_turned = sem("select_turned")
        sel_copied = sem("select_copied")
        comb_ready = sem("combine_rows_ready")
        g_done = sem("gathered")
        g_hi = sem("gathered_high")
        g_lo = sem("gathered_low")
        silu_done = sem("expert_silu")
        hid_ready = sem("expert_hidden")
        hid_turned = sem("expert_hidden_turned")
        hid_hi = sem("expert_hidden_high")
        hid_lo = sem("expert_hidden_low")
        dn_hi = sem("down_high")
        dn_lo = sem("down_low")
        sc_done = sem("scattered")
        sc_add = sem("scattered_added")

        MOE_UNITS = PER_GROUP * UNITS + D // W * UNITS
        MOE_CHUNKS = PER_GROUP + D // W

        def bc(ap, n):
            return ap.unsqueeze(2).to_broadcast([P, ap.shape[1], n])

        def route_dve(dve):
            dr = dve.drain
            lg, le = logits[:, :, 0:N_GROUPS], logits[:, :, N_GROUPS:ROUTES]
            idx = kept("index")
            idx_g = idx[:, 0:N_GROUPS].unsqueeze(1).to_broadcast([P, NT, N_GROUPS])
            idx_e = idx.unsqueeze(1).to_broadcast([P, NT, N_EXPERTS])
            dve.wait_ge(r_out, 1)
            for t in range(NT):
                dve.tensor_tensor(logits[:, t, :], bank(0, 64 * t, ROUTES), route_b, ALU.add)
            dr()

            def first_max(values, n, top, hit, cnd, at, one, idx_ap):
                dve.tensor_reduce(top, values, AX.X, ALU.max)
                dr()
                dve.tensor_tensor(hit, values, bc(top, n), ALU.is_equal)
                dr()
                dve.tensor_scalar(cnd, hit, -1000.0, 1000.0, ALU.mult, ALU.add)
                dr()
                dve.tensor_tensor(cnd, cnd, idx_ap, ALU.add)
                dr()
                dve.tensor_reduce(at, cnd, AX.X, ALU.min)
                dr()
                dve.tensor_tensor(one, cnd, bc(at, n), ALU.is_equal)
                dr()

            first_max(lg, N_GROUPS, gmax, g_eq, g_cand, gidx, g_one, idx_g)
            dve.drain().then_inc(r_one, 1)
            dve.tensor_tensor(g_exp, lg, bc(gmax, N_GROUPS), ALU.subtract)
            dve.drain().then_inc(r_gsub, 1)
            off = m_off[:, :, 0:N_GROUPS]
            dve.tensor_scalar(off, g_one, BIG, -BIG, ALU.mult, ALU.add)
            dr()
            for t in range(NT):
                dve.tensor_tensor(em[:, t, :].rearrange("p (g e) -> p g e", g=N_GROUPS),
                                  le[:, t, :].rearrange("p (g e) -> p g e", g=N_GROUPS),
                                  bc(off[:, t, :], PER_GROUP), ALU.add)
            dr()
            first_max(em, N_EXPERTS, m1, eq, cand, c1, oh1, idx_e)
            dve.scalar_tensor_tensor(em2, oh1, -3.0 * BIG, em, ALU.mult, ALU.add)
            dr()
            first_max(em2, N_EXPERTS, m2, eq, cand, c2, oh2, idx_e)
            dve.tensor_tensor(dm, m2, m1, ALU.subtract)
            dve.drain().then_inc(r_dm, 1)
            dve.wait_ge(r_gexp, 1)
            dve.tensor_reduce(gsum, g_exp, AX.X, ALU.add)
            dr()
            dve.reciprocal(gw, gsum)
            dve.wait_ge(r_de, 1)
            dve.tensor_scalar(den2, e2, 1.0, None, ALU.add)
            dr()
            dve.reciprocal(w1, den2)
            dr()
            dve.tensor_tensor(w1, w1, gw, ALU.mult)
            dr()
            dve.tensor_tensor(w2, w1, e2, ALU.mult)
            dr()
            dve.tensor_tensor(oh1, oh1, bc(w1, N_EXPERTS), ALU.mult)
            dve.tensor_tensor(oh2, oh2, bc(w2, N_EXPERTS), ALU.mult)
            dr()
            dve.tensor_tensor(combine, oh1, oh2, ALU.add)
            dve.wait_ge(r_rank, 1)
            for t in range(NT):
                dve.tensor_tensor(g_cand[:, t, :], bank(1, 8 * t, N_GROUPS), g_one[:, t, :], ALU.mult)
            dve.tensor_copy(counts, bank(1, 16, N_GROUPS))
            dr()
            dve.tensor_reduce(rank, g_cand, AX.X, ALU.add)
            dr()
            dve.scalar_tensor_tensor(key, gidx, 2.0 * P, rank, ALU.mult, ALU.add)
            dve.tensor_scalar(over4, counts, float(P), None, ALU.is_gt)
            dr()
            dve.tensor_tensor(over4i, over4, idx[:, 0:N_GROUPS], ALU.mult)
            dr()
            dve.tensor_reduce(ovf_f[:, 0:1], over4, AX.X, ALU.max)
            dve.tensor_reduce(ovf_f[:, 1:2], over4i, AX.X, ALU.max)
            dr()
            dve.tensor_scalar(ovf_base, ovf_f[:, 1:2], 2.0 * P, float(P), ALU.mult, ALU.add)
            dve.tensor_copy(ovf[:], ovf_f)
            dve.tensor_copy(cur, key)
            dve.drain().then_inc(r_done, 1)

        def route_act(act):
            act.wait_ge(r_gsub, 1)
            act.activation(g_exp, g_exp, ACT.Exp).then_inc(r_gexp, 1)
            act.wait_ge(r_dm, 1)
            act.activation(e2, dm, ACT.Exp).then_inc(r_de, 1)

        def route_pe(pe):
            pe.wait_ge(r_wlo, 1)
            for t in range(NT):
                for k in range(KD):
                    for q, (lhs, rhs) in enumerate(((x_hi, route_hi), (x_hi, route_lo), (x_lo, route_hi))):
                        m = pe.matmul(bank(0, 64 * t, ROUTES), lhs[:, k, t * P:t * P + P], rhs[:, k, :],
                                      start=k == 0 and q == 0, stop=k == KD - 1 and q == 2)
            m.then_inc(r_out, 1)
            pe.wait_ge(r_one, 1)
            before, ones = kept("before"), kept("ones")
            pe.matmul(bank(1, 0, N_GROUPS), before, g_one[:, 0, :], start=True, stop=True)
            pe.matmul(bank(1, 8, N_GROUPS), before, g_one[:, 1, :], start=True, stop=False)
            pe.matmul(bank(1, 8, N_GROUPS), ones, g_one[:, 0, :], start=False, stop=True)
            pe.matmul(bank(1, 16, N_GROUPS), ones, g_one[:, 0, :], start=True, stop=False)
            pe.matmul(bank(1, 16, N_GROUPS), ones, g_one[:, 1, :], start=False, stop=True).then_inc(r_rank, 1)

        def gath_bank(f):
            return 1 + f % 3

        def moe_pe(pe, fl, i):
            pe.wait_ge(sel_ready, i + 1)
            for t in range(NT):
                pe.transpose(bank(0, t * P, P), select_f[:, t, :], ident)
            for t in range(NT):
                m = pe.matmul(bank(0, T, N_EXPERTS), select_f[:, t, :], combine[:, t, :], start=t == 0, stop=t == 1)
            m.then_inc(sel_turned, 1)
            for f in range(8):
                b, part = f // 2, (m_hi, m_lo)[f % 2]
                if f >= 3:
                    pe.wait_ge((g_hi, g_lo)[(f - 3) % 2], i * 4 + (f - 3) // 2 + 1)
                for dd in range(4):
                    for t in range(NT):
                        m = pe.matmul(bank(gath_bank(f), dd * P, P), part[:, t, (4 * b + dd) * P:(4 * b + dd + 1) * P],
                                      select[:, t, :], start=t == 0, stop=t == 1)
                m.then_inc(g_done, 1)
            gathered = [lambda k, t, a=a: a[:, k * P:k * P + P] for a in (xg_hi, xg_lo)]
            hid = [lambda k, t, a=a: a[:, D + k * P:D + k * P + P] for a in (xg_hi, xg_lo)]

            with fl.loop(pe, PER_GROUP // 2, 2 * UNITS, 2) as ep:
                def turn_hidden(s):
                    pe.wait_ge(hid_ready, i * 8 + ep * 2 + s + 1)
                    pe.wait_ge(hid_lo, i * 8 + ep * 2 + s + 1)
                    for b in range(2):
                        m = pe.transpose(bank(0, b * P, P), hidden[s][:, b * P:b * P + P], ident)
                    m.then_inc(hid_turned, 1)

                pe.wait_ge(g_lo, i * 4 + 4)
                pe.wait_ge(g_hi, i * 4 + 4)
                product(pe, fl, gathered, tiles=1)
                product(pe, fl, gathered, tiles=1, after=[(5, lambda: turn_hidden(0))])
                turn_hidden(1)
            with fl.loop(pe, 2, 2 * UNITS, 2):
                pe.wait_ge(hid_lo, i * 8 + 8 + 1)
                for _ in range(2):
                    product(pe, fl, hid, tiles=1)
            pe.wait_ge(dn_lo, i * 4 + 4)
            for f in range(8):
                c, t = f // 2, f % 2
                if f >= 4:
                    pe.wait_ge(sc_add, i * 8 + f - 3)
                for q, part in enumerate((e_hi, e_lo)):
                    m = pe.matmul(bank(f % 4), select_t[:, t * P:t * P + P], part[:, c * W:(c + 1) * W],
                                  start=q == 0, stop=q == 1)
                m.then_inc(sc_done, 1)

        def moe_act(act, fl, i):
            act.wait_ge(sel_turned, i + 1)
            act.activation(select_t[:], bank(0, 0, T), ACT.Copy).then_inc(sel_copied, 1)
            for b in range(4):
                act.wait_ge(g_done, i * 8 + 2 * b + 1)
                act.activation(xg_hi[:, b * W:(b + 1) * W], bank(gath_bank(2 * b)), ACT.Copy).then_inc(g_hi, 1)
            with fl.loop(act, PER_GROUP // 2, 2 * UNITS, 2) as ep:
                def silu(s):
                    chunk_done(act, fl)
                    act.activation(silu_g[s], chunk_ps(fl)[:, 0, 0:D_EXPERT], ACT.Silu).then_inc(silu_done, 1)

                def hid_high(s):
                    act.wait_ge(hid_turned, i * 8 + ep * 2 + s + 1)
                    act.activation(xg_hi[:, bass.ds(ep * 512 + (D + s * T), T)], bank(0, 0, T),
                                   ACT.Copy).then_inc(hid_hi, 1)

                splits(high, act, fl)
                splits_two(high, act, fl, lambda: silu(0), lambda: hid_high(0))
                silu(1)
                hid_high(1)
            with fl.loop(act, 2, 2 * UNITS, 2) as cp:
                def down_high(s):
                    chunk_done(act, fl)
                    act.activation(e_hi[:, bass.ds(cp * (2 * W) + s * W, W)], chunk_ps(fl)[:, 0, :],
                                   ACT.Copy).then_inc(dn_hi, 1)

                splits(high, act, fl)
                splits(high, act, fl, between=lambda: down_high(0))
                down_high(1)

        def splits_two(part, eng, fl, first, second):
            for j in range(UNITS):
                if j == RING:
                    first()
                if j == RING + 2:
                    second()
                part(eng, fl, j)
            fl.next(UNITS)

        def moe_dve(dve, fl, i, overflow=False):
            if overflow:
                dve.tensor_scalar(cur, key, ovf_base, None, ALU.subtract)
                dve.drain()
            for t in range(NT):
                dve.tensor_scalar(select_f[:, t, :], kept("iota"), cur[:, t:t + 1], None, ALU.is_equal)
                dve.tensor_scalar(select[:, t, :], kept("iota"), cur[:, t:t + 1], None, ALU.is_equal)
            dve.drain().then_inc(sel_ready, 1)
            dve.tensor_scalar(cur, cur, -2.0 * P, None, ALU.add)
            dve.wait_ge(sel_copied, i + 1)
            dve.tensor_reduce(comb_rows, bank(0, T, N_EXPERTS).rearrange("p (g e) -> p e g", g=N_GROUPS), AX.X,
                              ALU.add).then_inc(comb_ready, 1)
            for b in range(4):
                dve.wait_ge(g_done, i * 8 + 2 * b + 2)
                dve.tensor_copy(xg_lo[:, b * W:(b + 1) * W], bank(gath_bank(2 * b + 1))).then_inc(g_lo, 1)
            with fl.loop(dve, PER_GROUP // 2, 2 * UNITS, 2) as ep:
                def gate(s):
                    dve.wait_ge(silu_done, i * 8 + ep * 2 + s + 1)
                    dve.scalar_tensor_tensor(hidden[s], chunk_ps(fl)[:, 0, D_EXPERT:2 * D_EXPERT],
                                             comb_rows[:, bass.ds(ep * 2 + s, 1)], silu_g[s], ALU.mult,
                                             ALU.mult).then_inc(hid_ready, 1)
                    dve.drain().then_inc(out_free, 1)

                def hid_low(s):
                    dve.wait_ge(hid_hi, i * 8 + ep * 2 + s + 1)
                    at = bass.ds(ep * 512 + (D + s * T), T)
                    dve.tensor_tensor(xg_lo[:, at], bank(0, 0, T), xg_hi[:, at], ALU.subtract).then_inc(hid_lo, 1)

                splits(low, dve, fl)
                splits_two(low, dve, fl, lambda: gate(0), lambda: hid_low(0))
                gate(1)
                hid_low(1)
            with fl.loop(dve, 2, 2 * UNITS, 2) as cp:
                def down_low(s):
                    dve.wait_ge(dn_hi, i * 4 + cp * 2 + s + 1)
                    at = bass.ds(cp * (2 * W) + s * W, W)
                    dve.tensor_tensor(e_lo[:, at], chunk_ps(fl)[:, 0, :], e_hi[:, at],
                                      ALU.subtract).then_inc(dn_lo, 1)
                    dve.drain().then_inc(out_free, 1)

                splits(low, dve, fl)
                splits(low, dve, fl, between=lambda: down_low(0))
                down_low(1)
            for f in range(8):
                c, t = f // 2, f % 2
                dve.wait_ge(sc_done, i * 8 + f + 1)
                hs = h[:, t, c * W:(c + 1) * W]
                dve.tensor_tensor(hs, bank(f % 4), hs, ALU.add).then_inc(sc_add, 1)

        def moe_sp(sp, fl, g):
            gates, ups = (d[n][0].rearrange("e k f -> (e k) f") for n in ("w_gate", "w_up"))
            downs = d["w_down"][0].rearrange("e f n -> (e f) n")
            with fl.loop(sp, PER_GROUP // 2, 2 * UNITS, 2) as ep:
                for s in range(2):
                    row = g * (PER_GROUP * D) + ep * (2 * D) + s * D
                    for j in range(UNITS):
                        load_unit(sp, fl, j, [
                            (m[bass.ds(row + j * UNIT_K * P, UNIT_K * P), :].rearrange("(r p) f -> p r f", p=P), None, a)
                            for m, a in ((gates, 0), (ups, D_EXPERT))])
                    fl.next(UNITS)
            with fl.loop(sp, 2, 2 * UNITS, 2) as cp:
                for s in range(2):
                    load_chunk(sp, fl, downs, g * (PER_GROUP * D_EXPERT), cp * (2 * W) + s * W)

        pp = wk(0, NT * D).rearrange("p (t d) -> p t d", t=NT)
        p_rows = wk(4096, NT * PLE_DIM).rearrange("p (t d) -> p t d", t=NT)
        sig = wk(4608, NT * W).rearrange("p (t d) -> p t d", t=NT)
        sig2 = wk(5632, NT * W).rearrange("p (t d) -> p t d", t=NT)
        final_gain = wk(6656, D)
        pt_hi, pt_lo = (a[:, 0:2 * T].rearrange("p (k t) -> p k t", k=2) for a in (e_hi, e_lo))
        ple_loads = sem("ple_loads")
        moe_memory_free = sem("moe_memory_free")
        pt_turned = sem("ple_turned")
        pt_high = sem("ple_high")
        pt_low = sem("ple_low")
        ple_sig = sem("ple_sigmoid")
        ple_used = sem("ple_sigmoid_used")
        first_done = sem("first_block_scaled")

        PAD = CONV - 1
        rg_x = wk(0, 4 * (T + PAD)).rearrange("p (n t) -> p n t", n=4)
        base = 1040
        (rg_c, rg_s, rg_r, rg_i, rg_a, rg_t, rg_u, rg_y) = (
            wk(base + 1024 * i, 1024).rearrange("p (n t) -> p n t", n=4) for i in range(8))
        decay = small[:, 32:48]
        wait_carrier = small[:, 95:96]
        sp_t = [small[:, 48 + 16 * i:64 + 16 * i] for i in range(3)]
        c_hi, c_lo = (a[:, 0:4 * T].rearrange("p (n t) -> p n t", n=4) for a in (e_hi, e_lo))
        rg = {n: sem("rg_" + n) for n in ("x", "conv", "chigh", "clow", "silu", "gates", "rate", "exp", "sq",
                                          "root", "y", "yhigh", "ylow", "lam")}

        def pe_rg(pe, fl):
            with fl.loop(pe, 2, 36, 8) as i:
                for s in range(2):
                    g = i * 2 + s
                    product(pe, fl, x_parts, by_channel=True)
                    product(pe, fl, x_parts, by_channel=True)
                    pe.wait_ge(rg["clow"], g + 1)
                    for hh in range(2):
                        product(pe, fl, [lambda k, a=a: a[:, 2 * hh + k, :] for a in (c_hi, c_lo)], units=1,
                                by_channel=True)

        def act_rg(act, fl):
            with fl.loop(act, 2, 36, 8) as i:
                for s in range(2):
                    g = i * 2 + s

                    def x_out():
                        chunk_done(act, fl)
                        act.activation(rg_x[:, :, PAD:PAD + T],
                                       chunk_ps(fl)[:].rearrange("p a b -> p (a b)").rearrange("p (n t) -> p n t", n=4),
                                       ACT.Copy).then_inc(out_free, 1)
                        act.drain().then_inc(rg["x"], 1)

                    splits(high, act, fl)
                    splits(high, act, fl, between=x_out)
                    for _ in range(2):
                        high(act, fl, 0)
                        fl.next(1)
                    act.wait_ge(rg["conv"], g + 1)
                    act.activation(c_hi, rg_c, ACT.Copy).then_inc(rg["chigh"], 1)
                    chunk_done(act, fl, 2)
                    act.activation(rg_s,
                                   chunk_ps(fl, 2)[:].rearrange("p a b -> p (a b)").rearrange("p (n t) -> p n t", n=4),
                                   ACT.Silu).then_inc(out_free, 1)
                    for hh in range(2):
                        chunk_done(act, fl, 1 - hh)
                        for q in range(4):
                            n = 2 * hh + q % 2
                            dst = (rg_r, rg_i)[q // 2][:, n, :]
                            b = col[("rg_b_gate_a_2", "rg_b_gate_x_2")[q // 2]]
                            m = act.activation(dst, chunk_ps(fl, 1 - hh)[:, q // 2, (q % 2) * T:(q % 2) * T + T],
                                               ACT.Sigmoid, bias=b[:, bass.ds(g * 4 + n, 1)])
                        m.then_inc(out_free, 1)
                    act.drain().then_inc(rg["gates"], 1)
                    act.wait_ge(rg["rate"], g + 1)
                    act.activation(rg_a, rg_r, ACT.Exp, scale=-1.0)
                    act.activation(rg_t, rg_r, ACT.Tanh).then_inc(rg["exp"], 1)
                    act.wait_ge(rg["sq"], g + 1)
                    act.activation(rg_t, rg_u, ACT.Sqrt).then_inc(rg["root"], 1)
                    act.wait_ge(rg["y"], g + 1)
                    act.activation(y_hi[:, bass.ds(g * 4, 4), :], rg_y, ACT.Copy).then_inc(rg["yhigh"], 1)

        def dve_rg(dve, fl):
            dve.memset(rg_x[:, :, 0:PAD], 0.0)
            with fl.loop(dve, 2, 36, 8) as i:
                for s in range(2):
                    g = i * 2 + s
                    splits(low, dve, fl)
                    splits(low, dve, fl)
                    low(dve, fl, 0)
                    fl.next(1)
                    low(dve, fl, 0)
                    fl.next(1)
                    dve.wait_ge(rg["x"], g + 1)
                    for tap in range(CONV - 1, -1, -1):
                        for n in range(4):
                            w = conv_w[:, tap, :][:, bass.ds(g * 4 + n, 1)]
                            src = rg_x[:, n, tap:tap + T]
                            if tap == CONV - 1:
                                dve.tensor_scalar(rg_c[:, n, :], src, w, conv_b[:, bass.ds(g * 4 + n, 1)], ALU.mult,
                                                  ALU.add)
                            else:
                                dve.scalar_tensor_tensor(rg_c[:, n, :], src, w, rg_c[:, n, :], ALU.mult, ALU.add)
                        dve.drain()
                    dve.drain().then_inc(rg["conv"], 1)
                    dve.wait_ge(rg["chigh"], g + 1)
                    dve.tensor_tensor(c_lo, rg_c, c_hi, ALU.subtract).then_inc(rg["clow"], 1)
                    dve.wait_ge(rg["gates"], g + 1)
                    for n in range(4):
                        dve.tensor_scalar(rg_r[:, n, :], rg_r[:, n, :], decay[:, bass.ds(g * 4 + n, 1)], None, ALU.mult)
                    dve.drain().then_inc(rg["rate"], 1)
                    dve.tensor_tensor(rg_i, rg_i, rg_c, ALU.mult)
                    dve.wait_ge(rg["exp"], g + 1)
                    dve.tensor_tensor(rg_u, rg_a, rg_a, ALU.mult)
                    dve.drain()
                    dve.scalar_tensor_tensor(rg_u, rg_u, 1.0, rg_t, ALU.add, ALU.mult)
                    dve.drain().then_inc(rg["sq"], 1)
                    dve.wait_ge(rg["root"], g + 1)
                    dve.tensor_tensor(rg_u, rg_t, rg_i, ALU.mult)
                    dve.drain()
                    for n in range(4):
                        dve.tensor_tensor_scan(rg_t[:, n, :], rg_a[:, n, :], rg_u[:, n, :], 0.0, ALU.mult, ALU.add)
                    dve.drain()
                    dve.tensor_tensor(rg_y, rg_t, rg_s, ALU.mult).then_inc(rg["y"], 1)
                    dve.wait_ge(rg["yhigh"], g + 1)
                    dve.tensor_tensor(y_lo[:, bass.ds(g * 4, 4), :], rg_y, y_hi[:, bass.ds(g * 4, 4), :],
                                      ALU.subtract).then_inc(rg["ylow"], 1)

        def sp_rg(sp, fl):
            w = d["rec_w_in_2"][0]
            ga, gx = (d[n][0].rearrange("h k n -> (h k) n") for n in ("rg_w_gate_a_2", "rg_w_gate_x_2"))
            with fl.loop(sp, 2, 36, 8) as i:
                for s in range(2):
                    g = i * 2 + s
                    load_chunk(sp, fl, w, 0, g * W)
                    load_chunk(sp, fl, w, 0, g * W + D)
                    for hh in range(2):
                        row = g * (2 * 256) + hh * 256
                        load_unit(sp, fl, 0, [
                            (m[bass.ds(row, 256), :].rearrange("(r p) f -> p r f", p=P), None, a)
                            for m, a in ((ga, 0), (gx, 256))])
                        fl.next(1)

        def hgv(a):
            return wk(a, 1024).rearrange("p (n t) -> p n t", n=4)

        hq, hk, hf, hb, hv, hs_, he, hqp, hkp, hst = (hgv(1024 * i) for i in range(10))
        hv_rows, hs_rows, hy_rows, hsq = (a.rearrange("p n t -> p (n t)").rearrange("p (t d) -> p t d", t=NT)
                                          for a in (hv, hs_, hf, he))
        hst8 = wk(9216, 1024).rearrange("p (n t) -> p n t", n=8)
        hsx = wk(10240, 512).rearrange("p (n t) -> p n t", n=4)
        n_masks = len(LEVELS) + 1
        masks = wk(10752, n_masks * P)
        reset = wk(11776, 1024)
        flat = lambda a: a.rearrange("p n t -> p (n t)")
        hg = {n: sem("hg_" + n) for n in ("loads", "free", "f", "abs", "ln", "logk", "kexp", "arg", "exp",
                                          "parts", "scores", "masked", "o", "sq", "var", "root", "y", "turned",
                                          "yhigh", "ylow")}
        h_ssq, h_var, h_root, h_scale = (small[:, 16 + 8 * i:24 + 8 * i] for i in range(4))

        NL = len(LEVELS) + 2

        def pe_hg(pe, fl):
            with fl.loop(pe, 4, 4 * UNITS, 4) as g:
                product(pe, fl, x_parts, by_channel=True)
                product(pe, fl, x_parts, by_channel=True)
                product(pe, fl, x_parts)
                product(pe, fl, x_parts)
                for l in range(NL):
                    pe.wait_ge(hg["parts"], g * NL + l + 1)
                    if l == 0:
                        pe.wait_ge(hg["kexp"], g + 1)
                    if l >= 2:
                        pe.wait_ge(hg["masked"], g * NL + l - 1)
                    kk, qq = (hk, hq) if l == 0 else (hkp, hqp)
                    for n in range(4):
                        if l == NL - 1:
                            m = pe.matmul(bank(2 * (l % 2), n * P, P), kk[:, n, 0:P], qq[:, n, P:T], start=True,
                                          stop=True)
                            continue
                        for t in range(NT):
                            q = n * NT + t
                            m = pe.matmul(bank(2 * (l % 2) + q // 4, (q % 4) * P, P), kk[:, n, t * P:t * P + P],
                                          qq[:, n, t * P:t * P + P], start=True, stop=True)
                    m.then_inc(hg["scores"], 1)
                pe.wait_ge(hg["masked"], g * NL + NL)
                for n in range(4):
                    ch = slice(n * P, n * P + P)
                    pe.matmul(bank(0, n * P, P), hst8[:, n * NT, :], hv_rows[:, 0, ch], start=True, stop=True)
                    pe.matmul(bank(1, n * P, P), hst8[:, n * NT + 1, :], hv_rows[:, 1, ch], start=True, stop=False)
                    m = pe.matmul(bank(1, n * P, P), hsx[:, n, :], hv_rows[:, 0, ch], start=False, stop=True)
                m.then_inc(hg["o"], 1)
                pe.wait_ge(hg["y"], g + 1)
                for n in range(4):
                    for t in range(NT):
                        m = pe.transpose(bank(2 + n // 2, (n % 2) * T + t * P, P), hy_rows[:, t, n * P:n * P + P], ident)
                m.then_inc(hg["turned"], 1)
                pe.wait_ge(hg["ylow"], g + 1)

        def act_hg(act, fl):
            with fl.loop(act, 4, 4 * UNITS, 4) as g:
                def ps_flat():
                    return chunk_ps(fl)[:].rearrange("p a b -> p (a b)")

                def q_out():
                    chunk_done(act, fl)
                    act.activation(flat(hq), ps_flat(), ACT.Silu).then_inc(out_free, 1)

                def f_out():
                    chunk_done(act, fl)
                    act.activation(flat(hf), ps_flat(), ACT.Copy).then_inc(out_free, 1)
                    act.drain().then_inc(hg["f"], 1)

                def v_out():
                    chunk_done(act, fl)
                    act.activation(hv_rows, chunk_ps(fl)[:], ACT.Copy).then_inc(out_free, 1)

                splits(high, act, fl)
                splits(high, act, fl, between=q_out)
                splits(high, act, fl, between=f_out)
                splits(high, act, fl, between=v_out)
                chunk_done(act, fl)
                act.activation(hs_rows, chunk_ps(fl)[:], ACT.Silu).then_inc(out_free, 1)
                act.wait_ge(hg["abs"], g + 1)
                act.activation(flat(he), flat(he), ACT.Exp)
                act.drain()
                act.activation(flat(he), flat(he), ACT.Ln, bias=1.0).then_inc(hg["ln"], 1)
                act.wait_ge(hg["logk"], g + 1)
                act.activation(flat(hk), flat(hk), ACT.Exp, scale=-1.0).then_inc(hg["kexp"], 1)
                for l in range(1, NL):
                    act.wait_ge(hg["arg"], g * (NL - 1) + l)
                    act.activation(flat(he), flat(he), ACT.Exp).then_inc(hg["exp"], 1)
                act.wait_ge(hg["o"], g + 1)
                for t in range(NT):
                    m = act.activation(hsq[:, t, :], bank(t), ACT.Square)
                m.then_inc(hg["sq"], 1)
                act.wait_ge(hg["var"], g + 1)
                act.activation(h_root, h_var, ACT.Sqrt).then_inc(hg["root"], 1)
                act.wait_ge(hg["turned"], g + 1)
                act.activation(y_hi[:, bass.ds(g * 4, 4), :], mix[:, 2:4, :].rearrange("p a (n t) -> p (a n) t", t=T),
                               ACT.Copy).then_inc(hg["yhigh"], 1)

        def dve_hg(dve, fl):
            dr = dve.drain
            dve.wait_ge(hg["loads"], 32)
            dve.memset(hst8, 0.0)
            dve.memset(hqp, 0.0)
            dve.memset(hkp, 0.0)
            dr()
            with fl.loop(dve, 4, 4 * UNITS, 4) as g:
                for _ in range(4):
                    splits(low, dve, fl)
                dve.wait_ge(hg["f"], g + 1)
                dve.scalar_tensor_tensor(flat(he), flat(hf), -1.0, flat(hf), ALU.mult, ALU.min).then_inc(hg["abs"], 1)
                dve.tensor_scalar(flat(hq), flat(hq), float(P) ** -0.5, None, ALU.mult)
                dve.wait_ge(hg["ln"], g + 1)
                dve.scalar_tensor_tensor(flat(hk), flat(hf), 0.0, flat(he), ALU.max, ALU.add).then_inc(hg["logk"], 1)
                dve.scalar_tensor_tensor(flat(hf), flat(hf), 0.0, flat(he), ALU.min, ALU.subtract)
                dr()
                dve.tensor_tensor_scan(flat(hb), reset, flat(hf), 0.0, ALU.mult, ALU.add)
                dr()
                dve.drain().then_inc(hg["parts"], 1)

                def masked(l):
                    dve.wait_ge(hg["scores"], g * NL + l + 1)
                    if l == NL - 1:
                        dve.tensor_copy(hsx, bank(2 * (l % 2)).rearrange("p (n t) -> p n t", n=4)).then_inc(
                            hg["masked"], 1)
                        return
                    mk = masks[:, (n_masks - 1 if l == 0 else l - 1) * P:][:, 0:P]
                    b0 = 2 * (l % 2)
                    dve.memset(wait_carrier, 0.0)
                    dve.copy_predicated(hst8, mk.bitcast(U32).unsqueeze(1).to_broadcast([P, 8, P]),
                                        mix[:, b0:b0 + 2, :].rearrange("p a (n t) -> p (a n) t", t=P)).then_inc(
                        hg["masked"], 1)

                for l in range(1, NL):
                    if l < NL - 1:
                        m_ = LEVELS[l - 1]
                        halves = lambda a: flat(a).rearrange("p (b s m) -> p b s m", s=2, m=m_)
                        bb, ee = halves(hb), halves(he)
                        nb = 1024 // (2 * m_)
                        edge = bb[:, :, 0, m_ - 1:m_].to_broadcast([P, nb, m_])
                        dve.tensor_tensor(ee[:, :, 0, :], edge, bb[:, :, 0, :], ALU.subtract)
                        if m_ < HG_CHUNK:
                            dve.tensor_tensor(ee[:, :, 1, :], bb[:, :, 1, :], edge, ALU.subtract)
                        else:
                            dve.tensor_copy(ee[:, :, 1, :], bb[:, :, 1, :])
                        dve.drain().then_inc(hg["arg"], 1)
                        q_out, q_in, k_out, k_in = (halves(a) for a in (hqp, hq, hkp, hk))
                        if l >= 2:
                            masked(l - 1)
                        if l == 1:
                            dve.wait_ge(hg["kexp"], g + 1)
                        dve.wait_ge(hg["exp"], g * (NL - 1) + l)
                        dve.tensor_tensor(q_out[:, :, 1, :], q_in[:, :, 1, :], ee[:, :, 1, :], ALU.mult)
                        dve.tensor_tensor(k_out[:, :, 0, :], k_in[:, :, 0, :], ee[:, :, 0, :], ALU.mult)
                        if l == 1:
                            masked(0)
                    else:
                        c4 = lambda a: flat(a).rearrange("p (n c m) -> p n c m", c=4, m=HG_CHUNK)
                        bb, ee = c4(hb), c4(he)
                        end = lambda c: bb[:, :, c, HG_CHUNK - 1:HG_CHUNK].to_broadcast([P, 4, HG_CHUNK])
                        for c in range(2):
                            dve.tensor_tensor(ee[:, :, c, :], end(c), bb[:, :, c, :], ALU.subtract)
                        dve.tensor_copy(ee[:, :, 2, :], bb[:, :, 2, :])
                        dve.tensor_tensor(ee[:, :, 3, :], bb[:, :, 3, :], end(2), ALU.add)
                        dr()
                        dve.tensor_tensor(ee[:, :, 0, :], ee[:, :, 0, :], end(1), ALU.add)
                        dve.drain().then_inc(hg["arg"], 1)
                        masked(l - 1)
                        dve.wait_ge(hg["exp"], g * (NL - 1) + l)
                        dve.tensor_tensor(hqp[:, :, P:T], hq[:, :, P:T], he[:, :, P:T], ALU.mult)
                        dve.tensor_tensor(hkp[:, :, 0:P], hk[:, :, 0:P], he[:, :, 0:P], ALU.mult)
                    dve.drain().then_inc(hg["parts"], 1)
                masked(NL - 1)
                dve.wait_ge(hg["sq"], g + 1)
                dve.tensor_reduce(h_ssq.rearrange("p (t n) -> p t n", t=NT), hsq.rearrange("p t (n d) -> p t n d", d=P),
                                  AX.X, ALU.add)
                dr()
                dve.tensor_scalar(h_var, h_ssq, 1.0 / P, EPS, ALU.mult, ALU.add).then_inc(hg["var"], 1)
                dve.wait_ge(hg["root"], g + 1)
                dve.reciprocal(h_scale, h_root)
                dr()
                for t in range(NT):
                    v = lambda a: a[:, t, :].rearrange("p (n d) -> p n d", d=P)
                    dve.tensor_tensor(v(hy_rows), bank(t).rearrange("p (n d) -> p n d", d=P),
                                      bc(h_scale[:, 4 * t:4 * t + 4], P), ALU.mult)
                    dve.tensor_tensor(v(hs_rows), v(hs_rows), hg_gain.unsqueeze(1).to_broadcast([P, 4, P]), ALU.mult)
                dr()
                dve.tensor_tensor(hy_rows, hy_rows, hs_rows, ALU.mult).then_inc(hg["y"], 1)
                dve.wait_ge(hg["yhigh"], g + 1)
                dve.tensor_tensor(y_lo[:, bass.ds(g * 4, 4), :], mix[:, 2:4, :].rearrange("p a (n t) -> p (a n) t", t=T),
                                  y_hi[:, bass.ds(g * 4, 4), :], ALU.subtract).then_inc(hg["ylow"], 1)

        t_raw, t_sq = (wk(1024 * i, 1024).rearrange("p (t d) -> p t d", t=NT) for i in range(2))
        t_v, t_s = (wk(2048 + 1024 * i, 1024).rearrange("p (t d) -> p t d", t=NT) for i in range(2))
        t_q, t_k = (wk(4096 + 1024 * i, 1024).rearrange("p (n t) -> p n t", n=4) for i in range(2))
        t_p = [wk(6144 + SCORE * i, SCORE) for i in range(4)]
        t_a = [wk(7680 + SCORE * i, SCORE) for i in range(2)]
        t_pt = [wk(8448 + SCORE * i, SCORE) for i in range(2)]
        t_y = wk(9216, 512).rearrange("p (t d) -> p t d", t=NT)
        t_mask = wk(9728, SCORE)
        lam_rows = wk(10112, 512)
        t_raws = (t_raw, wk(11264, 1024).rearrange("p (t d) -> p t d", t=NT))
        rope_t = [wk(10752 + P * i, P).rearrange("p (a n) -> p a n", n=HALF) for i in range(4)]
        at = {n: sem("att_" + n) for n in ("loads", "free", "lam", "lamexp", "sq", "var", "root", "rows",
                                           "turned", "copied", "scores", "read", "max", "exp", "mixed", "pturned",
                                           "pcopied", "o", "osq", "ovar", "oroot", "y", "yturned", "yhigh", "ylow",
                                           "v")}
        lam2, lam = small[:, 48:50], small[:, 50:51]
        t_ssq, t_scale = small[:, 16:24], small[:, 24:32]
        t_var = [small[:, 32 + 8 * i:40 + 8 * i] for i in range(2)]
        t_root = [small[:, 8 * i:8 + 8 * i] for i in range(2)]
        t_nm = [small[:, 52 + 2 * i:54 + 2 * i] for i in range(4)]
        t_den = [small[:, 60 + 2 * i:62 + 2 * i] for i in range(4)]
        t_r = [small[:, 68 + 2 * i:70 + 2 * i] for i in range(4)]
        o_ssq, o_var, o_root, o_scale = (small[:, 76 + 2 * i:78 + 2 * i] for i in range(4))

        def pe_att(pe, fl):
            with fl.loop(pe, 4, 4 * UNITS, 4) as g:
                def turn(n):
                    pe.wait_ge(at["rows"], g * 2 + n + 1)
                    if n:
                        pe.wait_ge(at["copied"], g * 2 + 1)
                    for q in range(4):
                        for t in range(NT):
                            m = pe.transpose(bank(2 + q // 2, (q % 2) * T + t * P, P),
                                             t_raws[n][:, t, q * P:q * P + P], ident)
                    m.then_inc(at["turned"], 1)

                product(pe, fl, x_parts)
                product(pe, fl, x_parts)
                product(pe, fl, x_parts)
                product(pe, fl, x_parts)
                turn(0)
                turn(1)
                pe.wait_ge(at["copied"], g * 2 + 2)
                pe.wait_ge(at["v"], g + 1)
                for hh in range(2):
                    for i in range(2):
                        n = 2 * hh + i
                        if hh:
                            pe.wait_ge(at["read"], g * 4 + n - 1)
                        pe.matmul(bank(i, 0, T), t_q[:, n, P:T], t_k[:, n, :], start=True, stop=True)
                        pe.matmul(bank(i, T, P), t_q[:, n, 0:P], t_k[:, n, 0:P], start=True, stop=True).then_inc(
                            at["scores"], 1)
                for hh in range(2):
                    pe.wait_ge(at["mixed"], g * 2 + hh + 1)
                    for b in range(3):
                        m = pe.transpose(bank(2, b * P, P), t_a[hh][:, b * P:b * P + P], ident)
                    m.then_inc(at["pturned"], 1)
                    pe.wait_ge(at["pcopied"], g * 2 + hh + 1)
                    ch = slice(hh * T, hh * T + T)
                    pt = t_pt[hh]
                    pe.matmul(bank(3, T, T), pt[:, 0:P], t_v[:, 0, ch], start=True, stop=False)
                    pe.matmul(bank(3, T, T), pt[:, P:T], t_v[:, 1, ch], start=False, stop=True)
                    pe.matmul(bank(3, 0, T), pt[:, T:SCORE], t_v[:, 0, ch], start=True, stop=True).then_inc(at["o"], 1)
                    pe.wait_ge(at["y"], g * 2 + hh + 1)
                    for q in range(2):
                        for t in range(NT):
                            m = pe.transpose(bank(2, q * T + t * P, P), t_y[:, t, q * P:q * P + P], ident)
                    m.then_inc(at["yturned"], 1)
                    pe.wait_ge(at["ylow"], g * 2 + hh + 1)

        def act_att(act, fl):
            act.wait_ge(at["lam"], 1)
            act.activation(lam2, lam2, ACT.Exp).then_inc(at["lamexp"], 1)
            with fl.loop(act, 4, 4 * UNITS, 4) as g:
                def head_rows(n):
                    chunk_done(act, fl)
                    if n:
                        act.wait_ge(at["var"], g * 2 + 1)
                    act.activation(t_raws[n], chunk_ps(fl)[:], ACT.Copy)
                    act.activation(t_sq, chunk_ps(fl)[:], ACT.Square).then_inc(out_free, 1)
                    act.drain().then_inc(at["sq"], 1)

                def head_root(n):
                    act.wait_ge(at["var"], g * 2 + n + 1)
                    act.activation(t_root[n], t_var[n], ACT.Sqrt).then_inc(at["root"], 1)

                def copy_turned(n):
                    act.wait_ge(at["turned"], g * 2 + n + 1)
                    act.activation((t_q, t_k)[n], mix[:, 2:4, :].rearrange("p a (n t) -> p (a n) t", t=T),
                                   ACT.Copy).then_inc(at["copied"], 1)

                def v_out():
                    chunk_done(act, fl)
                    act.activation(t_v, chunk_ps(fl)[:], ACT.Copy).then_inc(out_free, 1)

                splits(high, act, fl)
                splits(high, act, fl, between=lambda: head_rows(0))
                splits(high, act, fl, between=lambda: head_rows(1))
                splits(high, act, fl, between=v_out)
                head_root(0)
                head_root(1)
                chunk_done(act, fl)
                act.activation(t_s, chunk_ps(fl)[:], ACT.Silu).then_inc(out_free, 1)
                act.drain().then_inc(at["v"], 1)
                copy_turned(0)
                copy_turned(1)
                for n in range(4):
                    act.wait_ge(at["max"], g * 4 + n + 1)
                    act.activation(t_p[n][:, 0:T], t_p[n][:, 0:T], ACT.Exp, bias=t_nm[n][:, 1:2],
                                   accum_out=t_den[n][:, 1:2])
                    act.activation(t_p[n][:, T:SCORE], t_p[n][:, T:SCORE], ACT.Exp, bias=t_nm[n][:, 0:1],
                                   accum_out=t_den[n][:, 0:1]).then_inc(at["exp"], 1)
                for hh in range(2):
                    act.wait_ge(at["pturned"], g * 2 + hh + 1)
                    act.activation(t_pt[hh], bank(2, 0, SCORE), ACT.Copy).then_inc(at["pcopied"], 1)
                    act.wait_ge(at["o"], g * 2 + hh + 1)
                    for t in range(NT):
                        act.activation(t_sq[:, t, 0:T], bank(3, t * T, T), ACT.Square, accum_out=o_ssq[:, t:t + 1])
                    act.drain().then_inc(at["osq"], 1)
                    act.wait_ge(at["ovar"], g * 2 + hh + 1)
                    act.activation(o_root, o_var, ACT.Sqrt).then_inc(at["oroot"], 1)
                    act.wait_ge(at["yturned"], g * 2 + hh + 1)
                    act.activation(y_hi[:, bass.ds(g * 4 + 2 * hh, 2), :],
                                   bank(2).rearrange("p (n t) -> p n t", t=T), ACT.Copy).then_inc(at["yhigh"], 1)

        def dve_att(dve, fl):
            dr = dve.drain
            dve.wait_ge(at["loads"], 32)
            lr = lam_rows.rearrange("p (a b d) -> p a b d", a=2, b=2)
            pr = wk(0, 256).rearrange("p (a d) -> p a d", a=2)
            dve.tensor_tensor(pr, lr[:, :, 0, :], lr[:, :, 1, :], ALU.mult)
            dr()
            dve.tensor_reduce(lam2, pr, AX.X, ALU.add)
            dve.drain().then_inc(at["lam"], 1)
            dve.wait_ge(at["lamexp"], 1)
            dve.tensor_tensor(lam, lam2[:, 1:2], lam2[:, 0:1], ALU.subtract)
            dr()
            dve.tensor_scalar(lam, lam, -LAM_INIT, None, ALU.add)
            dr()
            cos, sin = (kept(n).rearrange("p (t a) -> p t a", t=NT) for n in ("cos", "sin"))
            with fl.loop(dve, 4, 4 * UNITS, 4) as g:
                def head_scale(n):
                    dve.wait_ge(at["sq"], g * 2 + n + 1)
                    dve.tensor_reduce(t_ssq.rearrange("p (t n) -> p t n", t=NT),
                                      t_sq.rearrange("p t (n d) -> p t n d", d=P), AX.X, ALU.add)
                    dr()
                    dve.tensor_scalar(t_var[n], t_ssq, 1.0 / P, EPS, ALU.mult, ALU.add).then_inc(at["var"], 1)

                def head_norm(n):
                    gain = (q_gain, k_gain)[n]
                    dve.wait_ge(at["root"], g * 2 + n + 1)
                    dve.reciprocal(t_scale, t_root[n])
                    dr()
                    for t in range(NT):
                        v = t_raws[n][:, t, :].rearrange("p (n d) -> p n d", d=P)
                        dve.tensor_tensor(v, v, bc(t_scale[:, 4 * t:4 * t + 4], P), ALU.mult)
                    dr()
                    for t in range(NT):
                        v = t_raws[n][:, t, :].rearrange("p (n d) -> p n d", d=P)
                        dve.tensor_tensor(v, v, gain.unsqueeze(1).to_broadcast([P, 4, P]), ALU.mult)
                    dr()
                    for t in range(NT):
                        v = t_raws[n][:, t, :].rearrange("p (n d) -> p n d", d=P)
                        x1, x2 = v[:, :, 0:HALF], v[:, :, HALF:ROPE]
                        cc, ss = (a[:, t, :].unsqueeze(1).to_broadcast([P, 4, HALF]) for a in (cos, sin))
                        r4 = [a[:, 4 * t:4 * t + 4, :] for a in rope_t]
                        dve.tensor_tensor(r4[0], x1, cc, ALU.mult)
                        dve.tensor_tensor(r4[1], x2, ss, ALU.mult)
                        dve.tensor_tensor(r4[2], x2, cc, ALU.mult)
                        dve.tensor_tensor(r4[3], x1, ss, ALU.mult)
                    dr()
                    for t in range(NT):
                        v = t_raws[n][:, t, :].rearrange("p (n d) -> p n d", d=P)
                        r4 = [a[:, 4 * t:4 * t + 4, :] for a in rope_t]
                        dve.tensor_tensor(v[:, :, 0:HALF], r4[0], r4[1], ALU.subtract)
                        dve.tensor_tensor(v[:, :, HALF:ROPE], r4[2], r4[3], ALU.add)
                    dve.drain().then_inc(at["rows"], 1)

                splits(low, dve, fl)
                splits(low, dve, fl)
                splits(low, dve, fl, between=lambda: head_scale(0))
                splits(low, dve, fl, between=lambda: head_scale(1))
                head_norm(0)
                head_norm(1)
                dve.wait_ge(at["v"], g + 1)
                for t in range(NT):
                    v = t_s[:, t, :].rearrange("p (a d) -> p a d", d=2 * P)
                    dve.scalar_tensor_tensor(v, v, 1.0 - LAM_INIT, sub_gain.unsqueeze(1).to_broadcast([P, 2, 2 * P]),
                                             ALU.mult, ALU.mult)
                for n in range(4):
                    dve.wait_ge(at["scores"], g * 4 + n + 1)
                    dve.scalar_tensor_tensor(t_p[n], bank(n % 2, 0, SCORE), float(P) ** -0.5, t_mask, ALU.mult,
                                             ALU.add).then_inc(at["read"], 1)
                    dr()
                    dve.tensor_reduce(t_nm[n][:, 1:2], t_p[n][:, 0:T], AX.X, ALU.max)
                    dve.tensor_reduce(t_nm[n][:, 0:1], t_p[n][:, T:SCORE], AX.X, ALU.max)
                    dr()
                    dve.tensor_scalar(t_nm[n], t_nm[n], -1.0, None, ALU.mult)
                    dve.drain().then_inc(at["max"], 1)
                for hh in range(2):
                    dve.wait_ge(at["exp"], g * 4 + 2 * hh + 2)
                    n0, n1 = 2 * hh, 2 * hh + 1
                    dve.reciprocal(t_r[n0], t_den[n0])
                    dve.reciprocal(t_r[n1], t_den[n1])
                    dr()
                    dve.tensor_scalar(t_r[n1], t_r[n1], lam, None, ALU.mult)
                    for t, (a, b) in enumerate(((T, SCORE), (0, T))):
                        dve.tensor_scalar(t_a[hh][:, a:b], t_p[n0][:, a:b], t_r[n0][:, t:t + 1], None, ALU.mult)
                    dr()
                    for t, (a, b) in enumerate(((T, SCORE), (0, T))):
                        dve.scalar_tensor_tensor(t_a[hh][:, a:b], t_p[n1][:, a:b], t_r[n1][:, t:t + 1],
                                                 t_a[hh][:, a:b], ALU.mult, ALU.add)
                    dve.drain().then_inc(at["mixed"], 1)
                    dve.wait_ge(at["osq"], g * 2 + hh + 1)
                    dve.tensor_scalar(o_var, o_ssq, 1.0 / (2 * P), 1e-5, ALU.mult, ALU.add).then_inc(at["ovar"], 1)
                    dve.wait_ge(at["oroot"], g * 2 + hh + 1)
                    dve.reciprocal(o_scale, o_root)
                    dr()
                    for t in range(NT):
                        m = dve.scalar_tensor_tensor(t_y[:, t, :], bank(3, t * T, T), o_scale[:, t:t + 1],
                                                     t_s[:, t, hh * T:hh * T + T], ALU.mult, ALU.mult)
                    m.then_inc(at["y"], 1)
                    dve.wait_ge(at["yhigh"], g * 2 + hh + 1)
                    ys = bass.ds(g * 4 + 2 * hh, 2)
                    dve.tensor_tensor(y_lo[:, ys, :], bank(2).rearrange("p (n t) -> p n t", t=T), y_hi[:, ys, :],
                                      ALU.subtract).then_inc(at["ylow"], 1)

        def sum_pe(pe, fl):
            for _ in range(D // W):
                product(pe, fl, y_parts)

        def sum_act(act, fl):
            for _ in range(D // W):
                splits(high, act, fl)

        def sum_dve(dve, fl):
            for c in range(D // W):
                splits(low, dve, fl, between=(lambda c=c: add_to_h(dve, fl, c - 1)) if c else None)
            add_to_h(dve, fl, D // W - 1)

        def sum_sp(sp, fl, wt, row):
            for c in range(D // W):
                load_chunk(sp, fl, wt, row, c * W)

        fin_ready = sem("h_ready")
        fin_sum = sem("stored")
        block = ctx.enter_context(nc.Block())

        @block.sync
        def _(sp):
            fl = Flow()
            sp.dma_start(h[:], d["x"][0].rearrange("(t p) n -> p t n", p=P)).then_inc(start_loads, 16)
            sp.dma_start(keep[:], d["tables"][:, 0:keep_n]).then_inc(start_loads, 16)
            vrows = wk(9000, 2 * P).rearrange("p (a b) -> p a b", a=2)
            for i, n in enumerate(vec_names):
                sp.dma_start(vrows[16 * i:16 * i + 16, 0, :], d[n].rearrange("a (k p) -> (a k) p", p=P)).then_inc(
                    start_loads, 16)
            sp.dma_start(vrows[0:64, 1, :], d["rg_conv_w_2"][0].rearrange("t (k p) -> (t k) p", p=P)).then_inc(
                start_loads, 16)
            sp.dma_start(vrows[64:80, 1, :], d["rg_conv_b_2"].rearrange("a (k p) -> (a k) p", p=P)).then_inc(
                start_loads, 16)
            w = d["w_in"][0]
            with fl.loop(sp, 4, 2 * UNITS, 2) as i:
                for s in range(2):
                    load_chunk(sp, fl, w, 0, i * (2 * W) + s * W)
            load_chunk(sp, fl, w, 0, 8 * W, n=256)
            sum_sp(sp, fl, d["w_out"][0], 0)
            sp.wait_ge(r_done, 1)
            flag = sp.value_load(ovf[0:1, 0:1], min_val=0, max_val=1)
            over = sp.value_load(ovf[0:1, 1:2], min_val=0, max_val=N_GROUPS - 1)
            with fl.loop(sp, N_GROUPS, MOE_UNITS, MOE_CHUNKS) as g:
                moe_sp(sp, fl, g)
            with fl.optional(sp, flag, MOE_UNITS, MOE_CHUNKS):
                moe_sp(sp, fl, over)
            for c in range(D // W):
                load_chunk(sp, fl, d["w_ple"][0], 0, c * W, units=1)
            sum_sp(sp, fl, d["w_ple_gate"][0], 0)
            sp_rg(sp, fl)
            sum_sp(sp, fl, d["rec_w_out_2"][0], 0)
            with fl.loop(sp, 4, 4 * UNITS, 4) as g:
                for n in range(4):
                    load_chunk(sp, fl, d["rec_w_in_2"][0], 0, g * W + (2 + n) * D)
            sum_sp(sp, fl, d["rec_w_out_2"][0], D)
            with fl.loop(sp, 4, 4 * UNITS, 4) as g:
                for n in range(4):
                    load_chunk(sp, fl, d["att_w_in_2"][0], 0, g * W + n * D)
            sum_sp(sp, fl, d["att_w_out_2"][0], 0)
            sp.wait_ge(fin_ready, 1)
            sp.dma_start(out[0].rearrange("(t p) n -> p t n", p=P), h[:]).then_inc(fin_sum, 16)
            sp.wait_ge(fin_sum, 16)

        @block.gpsimd
        def _(pool):
            pool.dma_start(sinks, d["sinks"][0].partition_broadcast(P)).then_inc(row_loads, 16)
            pool.dma_start(route_b[:, 0:N_GROUPS], d["b_grp"][0].partition_broadcast(P)).then_inc(row_loads, 16)
            pool.dma_start(route_b[:, N_GROUPS:], d["b_exp"][0].rearrange("g e -> (g e)").partition_broadcast(P)
                           ).then_inc(row_loads, 16)
            for dst, n in ((hg_gain, "hg_out_norm_2"), (q_gain, "att_q_norm_2"), (k_gain, "att_k_norm_2"),
                           (sub_gain, "att_sub_norm_2")):
                pool.dma_start(dst, d[n][0].partition_broadcast(P)).then_inc(row_loads, 16)
            a = tab_at["delta"][0]
            pool.wait_ge(vecs_turned, 1)
            pool.dma_start(bias_tabs, d["tables"][:, a:a + 3 * SCORE]).then_inc(row_loads, 16)
            pool.wait_ge(p1_copied, 9)
            pool.dma_start(kb[B_DIM:P, 0, :], kb[0:B_DIM, 0, :]).then_inc(keys_doubled, 16)
            pool.dma_start(kb[0:B_DIM, 1, :], kb[B_DIM:P, 1, :]).then_inc(keys_doubled, 16)
            pool.wait_ge(region_free, 1)
            pool.dma_start(gain_row, d["g_moe"][0].partition_broadcast(P)).then_inc(moe_loads, 16)
            with nc.allow_non_contiguous_dma(reason="router weights have short rows"):
                pool.dma_start(route_raw[:, :, 0:N_GROUPS],
                               d["w_grp"][0].rearrange("(k p) g -> p k g", p=P)).then_inc(moe_loads, 16)
                pool.dma_start(route_raw[:, :, N_GROUPS:],
                               d["w_exp"][0].rearrange("(k p) g e -> p k (g e)", p=P)).then_inc(moe_loads, 16)
            pool.wait_ge(moe_memory_free, 1)
            pool.dma_start(p_rows, d["p"][0, 0].rearrange("(t p) n -> p t n", p=P)).then_inc(ple_loads, 16)
            pool.dma_start(final_gain, d["g_final"].partition_broadcast(P)).then_inc(ple_loads, 16)
            pool.wait_ge(hg["free"], 1)
            a = tab_at["level1"][0]
            pool.dma_start(masks, d["tables"][:, a:a + n_masks * P]).then_inc(hg["loads"], 16)
            a = tab_at["reset"][0]
            pool.dma_start(reset, d["tables"][:, a:a + 1024]).then_inc(hg["loads"], 16)
            pool.wait_ge(at["free"], 1)
            a = tab_at["causal"][0]
            pool.dma_start(t_mask, d["tables"][:, a:a + SCORE]).then_inc(at["loads"], 16)
            pool.dma_start(lam_rows, d["att_lambda_2"][0].rearrange("a d -> (a d)").partition_broadcast(P)).then_inc(
                at["loads"], 16)

        vrows2 = wk(9000, 2 * P).rearrange("p (a b) -> p a b", a=2)

        @block.tensor
        def _(pe):
            fl = Flow()
            pe.nop().then_inc(unit_used, RING)
            pe.wait_ge(start_loads, 16 * 12)
            pe.transpose(bank(3, 0, P), vrows2[:, 0, :], ident)
            pe.transpose(bank(3, P, 80), vrows2[0:80, 1, :], ident[0:80, 0:80]).then_inc(vecs_turned, 1)
            pe.wait_ge(vecs_ready, 1)
            norm_pe(pe, norms["mix"])
            with fl.loop(pe, 2, 2 * UNITS, 2):
                for s in range(2):
                    product(pe, fl, x_parts, by_channel=True)
            for _ in range(2):
                product(pe, fl, x_parts)
            for _ in range(2):
                product(pe, fl, x_parts, by_channel=True)
            ps = out_ps[fl.c % 2]
            pe.wait_ge(out_free, fl.chunk() + 1)
            for j in range(UNITS):
                slot = (fl.u + j) % RING
                pe.wait_ge(low_ready, fl.unit(j) + 1 + RING)
                for r in range(UNIT_K):
                    k = UNIT_K * j + r
                    keys = slice(0, P)
                    for q, (wp, xp) in enumerate(((w_hi, x_hi), (w_hi, x_lo), (w_lo, x_hi))):
                        pe.matmul(ps[:, 0, 0:T], wp[:, slot, r, keys], xp[:, k, :], start=k == 0 and q == 0,
                                  stop=k == KD - 1 and q == 2, skip_group_check=True)
                    for t in range(NT):
                        for q, (xp, wp) in enumerate(((x_hi, w_hi), (x_hi, w_lo), (x_lo, w_hi))):
                            m = pe.matmul(ps[:, 1, t * P:t * P + P], xp[:, k, t * P:t * P + P],
                                          wp[:, slot, r, P:2 * P], start=k == 0 and t == 0 and q == 0,
                                          stop=k == KD - 1 and q == 2, skip_group_check=True)
                m.then_inc(unit_used, 1)
            fl.next(UNITS)
            attn_pe(pe)
            sum_pe(pe, fl)
            norm_pe(pe, norms["moe"], rows=m_rows)
            route_pe(pe)
            pe.wait_ge(r_done, 1)
            flag = pe.value_load(ovf[0:1, 0:1], min_val=0, max_val=1)
            with fl.loop(pe, N_GROUPS, MOE_UNITS, MOE_CHUNKS) as g:
                moe_pe(pe, fl, g)
            with fl.optional(pe, flag, MOE_UNITS, MOE_CHUNKS):
                moe_pe(pe, fl, N_GROUPS)
            norm_pe(pe, norms["ple"])
            pe.wait_ge(ple_loads, 32)
            for k in range(2):
                for t in range(NT):
                    m = pe.transpose(bank(0, k * T + t * P, P), p_rows[:, t, k * P:k * P + P], ident)
            m.then_inc(pt_turned, 1)
            pe.wait_ge(pt_low, 1)
            for _ in range(D // W):
                product(pe, fl, tokens_of(pt_hi, pt_lo), units=1)
            for _ in range(D // W):
                product(pe, fl, x_parts)
            norm_pe(pe, norms["rec"])
            pe_rg(pe, fl)
            pe.wait_ge(rg["ylow"], 4)
            sum_pe(pe, fl)
            pe_hg(pe, fl)
            sum_pe(pe, fl)
            norm_pe(pe, norms["att"])
            pe_att(pe, fl)
            sum_pe(pe, fl)

        @block.scalar
        def _(act):
            fl = Flow()
            act.wait_ge(vecs_turned, 1)
            act.activation(cols[:], bank(3, 0, 208), ACT.Copy)
            act.drain().then_inc(vecs_ready, 1)
            norm_act(act, norms["mix"])
            flat_ps = lambda: chunk_ps(fl)[:].rearrange("p a b -> p (a b)")

            def qk_out(i, s):
                chunk_done(act, fl)
                act.activation(qk[:, bass.ds(i * 8 + 4 * s, 4), :].rearrange("p n t -> p (n t)"), flat_ps(), ACT.Copy).then_inc(p1_copied, 1)
                act.drain().then_inc(out_free, 1)

            with fl.loop(act, 2, 2 * UNITS, 2) as i:
                splits(high, act, fl)
                splits(high, act, fl, between=lambda: qk_out(i, 0))
                qk_out(i, 1)

            def copy_out(dst, src):
                chunk_done(act, fl)
                act.activation(dst, src, ACT.Copy).then_inc(p1_copied, 1)
                act.drain().then_inc(out_free, 1)

            splits(high, act, fl)
            splits(high, act, fl, between=lambda: copy_out(va[:, :, 0:W], chunk_ps(fl)[:]))
            splits(high, act, fl, between=lambda: copy_out(va[:, :, W:2 * W], chunk_ps(fl)[:]))
            splits(high, act, fl, between=lambda: copy_out(qb[:, 0:4, :].rearrange("p n t -> p (n t)"), flat_ps()))
            splits(high, act, fl, n=256,
                   between=lambda: copy_out(qb[:, 4:8, :].rearrange("p n t -> p (n t)"), flat_ps()))
            chunk_done(act, fl)
            for g in range(2):
                lo_, hi_ = g * B_DIM, (g + 1) * B_DIM
                act.activation(kb[lo_:hi_, g, :], chunk_ps(fl)[lo_:hi_, 0, 0:T], ACT.Copy)
            act.activation(vb.rearrange("p n t -> p (n t)"), chunk_ps(fl)[:, 1, 0:T], ACT.Copy).then_inc(p1_copied, 1)
            act.drain().then_inc(out_free, 1)
            act.wait_ge(row_loads, 16 * 8)
            attn_act(act)
            sum_act(act, fl)
            act.wait_ge(moe_loads, 48)
            act.activation(route_hi, route_raw, ACT.Copy).then_inc(r_whi, 1)
            nm = norms["moe"]
            norm_stats_act(act, nm)
            act.wait_ge(m_rows, 1)
            act.activation(m_hi, xn, ACT.Copy).then_inc(m_split_hi, 1)
            for f in range(KD // 2):
                act.wait_ge(norm_s["turned"], nm.turns + f + 1)
                act.activation(x_hi[:, 2 * f:2 * f + 2, :], bank(f % 4).rearrange("p (n t) -> p n t", t=T),
                               ACT.Copy).then_inc(norm_s["high"], 1)
            route_act(act)
            act.wait_ge(r_done, 1)
            flag = act.value_load(ovf[0:1, 0:1], min_val=0, max_val=1)
            with fl.loop(act, N_GROUPS, MOE_UNITS, MOE_CHUNKS) as g:
                moe_act(act, fl, g)
            with fl.optional(act, flag, MOE_UNITS, MOE_CHUNKS):
                moe_act(act, fl, N_GROUPS)
            norm_act(act, norms["ple"])
            act.wait_ge(pt_turned, 1)
            act.activation(pt_hi, bank(0).rearrange("p (n t) -> p n t", t=T), ACT.Copy).then_inc(pt_high, 1)

            def pp_out(c):
                chunk_done(act, fl)
                act.activation(pp[:, :, c * W:(c + 1) * W], chunk_ps(fl)[:], ACT.Copy)
                act.drain().then_inc(out_free, 1)

            def sig_out(c):
                chunk_done(act, fl)
                if c:
                    act.wait_ge(ple_used, c)
                act.activation(sig, chunk_ps(fl)[:], ACT.Sigmoid).then_inc(ple_sig, 1)
                act.drain().then_inc(out_free, 1)

            for c in range(D // W):
                splits(high, act, fl, units=1)
                pp_out(c)
            for c in range(D // W):
                splits(high, act, fl, between=(lambda c=c: sig_out(c - 1)) if c else None)
            sig_out(D // W - 1)
            norm_stats_act(act, norms["final"])
            act.wait_ge(vecs_ready, 1)
            act.activation(sp_t[0], col["rg_lambda_2"], ACT.Abs)
            act.drain()
            act.activation(sp_t[0], sp_t[0], ACT.Exp, scale=-1.0).then_inc(rg["lam"], 1)
            norm_act(act, norms["rec"])
            act_rg(act, fl)
            sum_act(act, fl)
            act_hg(act, fl)
            sum_act(act, fl)
            norm_act(act, norms["att"])
            act_att(act, fl)
            sum_act(act, fl)

        @block.vector
        def _(dve):
            fl = Flow()
            dve.nop().then_inc(low_ready, RING)
            dve.nop().then_inc(out_free, 2)
            dve.nop().then_inc(hid_lo, 1)
            dve.wait_ge(start_loads, 16 * 12)
            dve.wait_ge(vecs_ready, 1)
            norm_dve(dve, norms["mix"])
            with fl.loop(dve, 4, 2 * UNITS, 2):
                for s in range(2):
                    splits(low, dve, fl)
            splits(low, dve, fl, n=256)
            attn_dve(dve)
            dve.drain().then_inc(region_free, 1)
            sum_dve(dve, fl)
            dve.wait_ge(moe_loads, 48)
            dve.wait_ge(r_whi, 1)
            dve.tensor_tensor(route_lo, route_raw, route_hi, ALU.subtract).then_inc(r_wlo, 1)
            nm = norms["moe"]
            norm_stats_dve(dve, nm)
            dve.wait_ge(norm_s["scale"], nm.n + 1)
            for t in range(NT):
                dve.scalar_tensor_tensor(xn[:, t, :], h[:, t, :], scale[:, t:t + 1], gain_row, ALU.mult, ALU.mult)
            dve.drain().then_inc(m_rows, 1)
            dve.wait_ge(m_split_hi, 1)
            dve.tensor_tensor(m_lo, xn, m_hi, ALU.subtract)
            norm_low(dve, nm)
            route_dve(dve)
            flag = dve.value_load(ovf[0:1, 0:1], min_val=0, max_val=1)
            with fl.loop(dve, N_GROUPS, MOE_UNITS, MOE_CHUNKS) as g:
                moe_dve(dve, fl, g)
            with fl.optional(dve, flag, MOE_UNITS, MOE_CHUNKS):
                moe_dve(dve, fl, N_GROUPS, overflow=True)
            dve.drain().then_inc(moe_memory_free, 1)
            norm_dve(dve, norms["ple"])
            dve.wait_ge(pt_high, 1)
            dve.tensor_tensor(pt_lo, bank(0).rearrange("p (n t) -> p n t", t=T), pt_hi, ALU.subtract).then_inc(pt_low, 1)

            def gate_out(c):
                dve.wait_ge(ple_sig, c + 1)
                at_ = slice(c * W, (c + 1) * W)
                dve.tensor_tensor(sig2, sig, pp[:, :, at_], ALU.mult).then_inc(ple_used, 1)
                dve.drain()
                dve.tensor_tensor(h[:, :, at_], h[:, :, at_], sig2, ALU.add)

            for c in range(D // W):
                splits(low, dve, fl, units=1)
            for c in range(D // W):
                splits(low, dve, fl, between=(lambda c=c: gate_out(c - 1)) if c else None)
            gate_out(D // W - 1)
            norm_stats_dve(dve, norms["final"])
            dve.wait_ge(norm_s["scale"], norms["final"].n + 1)
            dve.wait_ge(ple_loads, 32)
            for t in range(NT):
                dve.scalar_tensor_tensor(h[:, t, :], h[:, t, :], scale[:, t:t + 1], final_gain, ALU.mult, ALU.mult)
            dve.wait_ge(rg["lam"], 1)
            x_, z_, s_ = sp_t
            dve.tensor_scalar(z_, x_, 2.0, None, ALU.add)
            dve.drain()
            dve.reciprocal(s_, z_)
            dve.drain()
            dve.tensor_tensor(z_, x_, s_, ALU.mult)
            dve.drain()
            dve.tensor_tensor(x_, z_, z_, ALU.mult)
            dve.memset(s_, 1.0 / 17)
            dve.drain()
            for n in range(15, 0, -2):
                dve.tensor_tensor(s_, s_, x_, ALU.mult)
                dve.drain()
                dve.tensor_scalar(s_, s_, 1.0 / n, None, ALU.add)
                dve.drain()
            dve.tensor_tensor(s_, s_, z_, ALU.mult)
            dve.tensor_scalar(x_, col["rg_lambda_2"], -1.0, 0.0, ALU.mult, ALU.max)
            dve.drain()
            dve.scalar_tensor_tensor(s_, s_, 2.0, x_, ALU.mult, ALU.add)
            dve.drain()
            dve.tensor_scalar(decay, s_, 8.0, None, ALU.mult)
            norm_dve(dve, norms["rec"])
            dve_rg(dve, fl)
            dve.drain().then_inc(hg["free"], 1)
            sum_dve(dve, fl)
            dve_hg(dve, fl)
            dve.drain().then_inc(at["free"], 1)
            sum_dve(dve, fl)
            norm_dve(dve, norms["att"])
            dve_att(dve, fl)
            sum_dve(dve, fl)
            dve.drain().then_inc(fin_ready, 1)


_IN = ["x", "p", "w_in", "w_out", "sinks", "g_mix", "g_moe", "g_ple", "g_final", "w_grp", "b_grp", "w_exp", "b_exp",
       "w_gate", "w_up", "w_down", "w_ple", "w_ple_gate", "rec_norm_2", "rec_w_in_2", "rg_conv_w_2", "rg_conv_b_2",
       "rg_w_gate_a_2", "rg_b_gate_a_2", "rg_w_gate_x_2", "rg_b_gate_x_2", "rg_lambda_2", "hg_out_norm_2",
       "rec_w_out_2", "att_norm_2", "att_w_in_2", "att_q_norm_2", "att_k_norm_2", "att_lambda_2", "att_sub_norm_2",
       "att_w_out_2"]


def kernel(**inputs):
    import concourse.bacc as bacc
    from concourse.bass_utils import run_bass_kernel_spmd

    nc = bacc.Bacc("TRN2", target_bir_lowering=False, num_devices=1)
    table, tab_at = tables()
    arrays = {n: np.ascontiguousarray(inputs[n]) for n in _IN}
    arrays["tables"] = table
    d = {n: nc.dram_tensor(n, a.shape, F32, kind="ExternalInput").ap() for n, a in arrays.items()}
    out = nc.dram_tensor("out", (1, T, D), F32, kind="ExternalOutput").ap()
    program(nc, d, tab_at, out)
    r = run_bass_kernel_spmd(nc, [arrays], core_ids=[0])
    return r.results[0]["out"]
```

```python
from contextlib import ExitStack, contextmanager
import math

import numpy as np

import concourse.bass as bass
from concourse import mybir

F32 = mybir.dt.float32
F32R = mybir.dt.float32r
I32 = mybir.dt.int32
U32 = mybir.dt.uint32
ALU = mybir.AluOpType
ACT = mybir.ActivationFunctionType
AX = mybir.AxisListType

P = 128
D = 2048
T = 256
NT = T // P
KD = D // P
W = 512
UNIT_K = 2
RING = 4
UNITS = KD // UNIT_K
EPS = 1e-6
BIG = 1e30

A_HEADS = 8
A_DIM = 128
B_HEADS = 16
B_DIM = 64
B_GROUP = 8
N_GROUPS = 4
PER_GROUP = 8
N_EXPERTS = 32
D_EXPERT = 256
ROUTES = N_GROUPS + N_EXPERTS
PLE_DIM = 256
CONV = 4
ATT_LAYER = 1
LAM_INIT = 0.8 - 0.6 * math.exp(-0.3 * ATT_LAYER)
ROPE = 32
HALF = ROPE // 2
HG_CHUNK = 64
LEVELS = (1, 2, 4, 8, 16, 32, 64)
SCORE = 3 * P


def tables():
    p = np.arange(P)[:, None]
    parts = {}
    parts["ident"] = np.eye(P)
    parts["iota"] = np.broadcast_to(np.arange(P)[None, :], (P, P))
    parts["before"] = (p < np.arange(P)[None, :]).astype(float)
    parts["ones"] = np.ones((P, P))
    inv = 500000.0 ** (-np.arange(0, ROPE, 2, dtype=np.float32) / np.float32(ROPE))
    ang = np.stack([(p + t * P) * inv[None, :] for t in range(NT)], 1).astype(np.float32)
    parts["cos"] = np.cos(ang).reshape(P, -1)
    parts["sin"] = np.sin(ang).reshape(P, -1)
    parts["index"] = np.broadcast_to(np.arange(N_EXPERTS)[None, :], (P, N_EXPERTS))
    wide = P + p - np.arange(2 * P)[None, :]
    delta = np.concatenate([wide, wide[:, P:]], 1)
    seen = delta >= 0
    count = (seen & (delta <= 128)).astype(int) + (seen & (delta % 4 == 0)) + (seen & (delta % 16 == 0))
    parts["delta"] = delta
    parts["branches"] = np.where(count > 0, np.log(np.maximum(count, 1)), -BIG)
    parts["window"] = np.where(seen & (delta < 128), 0.0, -BIG)
    parts["causal"] = np.where(seen, 0.0, -BIG)
    s, t = p, np.arange(P)[None, :]
    for m in LEVELS:
        parts[f"level{m}"] = ((s // (2 * m) == t // (2 * m)) & (s % (2 * m) < m) & (t % (2 * m) >= m)).astype(float)
    parts["level0"] = np.eye(P)
    parts["reset"] = np.broadcast_to((np.arange(4 * T)[None, :] % HG_CHUNK != 0).astype(float), (P, 4 * T))
    at, n = {}, 0
    for name, a in parts.items():
        at[name] = (n, a.shape[1])
        n += a.shape[1]
    return np.concatenate([np.asarray(a, np.float32) for a in parts.values()], 1).astype(np.float32), at


class Flow:

    def __init__(self):
        self.u, self.c, self.terms = 0, 0, []

    def unit(self, j=0, scale=1):
        v = (self.u + j) * scale
        for reg, units, _ in self.terms:
            v = reg * (units * scale) + v
        return v

    def turn(self, j):
        v = 32 * ((self.u + j) // RING) + 32
        for reg, units, _ in self.terms:
            v = reg * (units // RING * 32) + v
        return v

    def chunk(self):
        v = self.c
        for reg, _, chunks in self.terms:
            v = reg * chunks + v
        return v

    def next(self, units):
        self.u += units
        self.c += 1

    @contextmanager
    def loop(self, eng, trips, units, chunks):
        assert units % RING == 0 and chunks % 2 == 0
        u, c = self.u, self.c
        with eng.Fori(0, trips) as i:
            self.terms.append((i, units, chunks))
            yield i
            self.terms.pop()
        assert (self.u - u, self.c - c) == (units, chunks), (self.u - u, self.c - c)
        self.u, self.c = u + trips * units, c + trips * chunks

    @contextmanager
    def optional(self, eng, flag, units, chunks):
        u, c = self.u, self.c
        with eng.If(flag > 0):
            yield
        assert (self.u - u, self.c - c) == (units, chunks)
        self.u, self.c = u, c
        self.terms.append((flag, units, chunks))


def program(nc, d, tab_at, out):
    ctx = ExitStack()
    with ctx:
        def sb(name, shape, dt=F32):
            return ctx.enter_context(nc.sbuf_tensor(name, shape, dt))

        def sem(name):
            return ctx.enter_context(nc.semaphore(name))

        raw = sb("raw", [P, RING, UNIT_K, W])
        w_hi = sb("w_hi", [P, RING, UNIT_K, W], F32R)
        w_lo = sb("w_lo", [P, RING, UNIT_K, W], F32R)
        x_hi = sb("x_hi", [P, KD, T], F32R)
        x_lo = sb("x_lo", [P, KD, T], F32R)
        y_hi = sb("y_hi", [P, KD, T], F32R)
        y_lo = sb("y_lo", [P, KD, T], F32R)
        e_hi = sb("e_hi", [P, D], F32R)
        e_lo = sb("e_lo", [P, D], F32R)
        select = sb("select", [P, NT, P], F32R)
        select_t = sb("select_t", [P, T], F32R)
        h = sb("h", [P, NT, D])
        work = sb("work", [P, 12800])
        keep_n = tab_at["delta"][0]
        keep = sb("keep", [P, keep_n])
        cols = sb("cols", [P, 208])
        rows = sb("rows", [P, 16 + 36 + 128 * 3 + 256])
        small = sb("small", [P, 96])
        ovf = sb("ovf", [P, 2], I32)
        out_ps = [ctx.enter_context(nc.psum_tensor(f"out_ps{i}", [P, 2, W], F32)) for i in range(2)]
        mix = ctx.enter_context(nc.psum_tensor("mix", [P, 4, W], F32))

        def kept(name):
            a, n = tab_at[name]
            return keep[:, a:a + n]

        ident = kept("ident")

        def wk(a, n):
            return work[:, a:a + n]

        def bank(b, a=0, n=W):
            return mix[:, b, a:a + n]

        vec_names = ["g_mix", "g_moe", "g_ple", "rec_norm_2", "att_norm_2", "rg_lambda_2", "rg_b_gate_a_2",
                     "rg_b_gate_x_2"]
        col = {n: cols[:, KD * i:KD * i + KD] for i, n in enumerate(vec_names)}
        conv_w = cols[:, 128:192].rearrange("p (t k) -> p t k", t=CONV)
        conv_b = cols[:, 192:208]
        sinks = rows[:, 0:16]
        route_b = rows[:, 16:52]
        hg_gain = rows[:, 52:180]
        q_gain = rows[:, 180:308]
        k_gain = rows[:, 308:436]
        sub_gain = rows[:, 436:692]

        raw_ready = [sem(f"raw_ready{i}") for i in range(RING)]
        low_ready = sem("low_ready")
        high_ready = sem("high_ready")
        unit_used = sem("unit_used")
        out_free = sem("out_free")
        start_loads = sem("start_loads")
        row_loads = sem("row_loads")
        vecs_turned = sem("vecs_turned")
        vecs_ready = sem("vecs_ready")

        def load_unit(sp, fl, j, sources):
            slot = (fl.u + j) % RING
            sp.wait_ge(low_ready, fl.unit(j) + 1)
            for r, (src, a, n) in enumerate(sources):
                sp.dma_start(raw[:, slot, r, a:a + n] if a is not None else raw[:, slot, :, n:n + D_EXPERT],
                             src).then_inc(raw_ready[slot], 16)

        def load_chunk(sp, fl, wt, row, c0, units=UNITS, n=W):
            for j in range(units):
                load_unit(sp, fl, j, [(wt[bass.ds(row + (UNIT_K * j + r) * P, P), bass.ds(c0, n)], 0, n)
                                      for r in range(UNIT_K)])
            fl.next(units)

        def high(act, fl, j):
            slot = (fl.u + j) % RING
            act.wait_ge(raw_ready[slot], fl.turn(j))
            act.wait_ge(unit_used, fl.unit(j) + 1)
            act.activation(w_hi[:, slot], raw[:, slot], ACT.Copy).then_inc(high_ready, 1)

        def low(dve, fl, j):
            slot = (fl.u + j) % RING
            dve.wait_ge(high_ready, fl.unit(j) + 1)
            dve.tensor_tensor(w_lo[:, slot], raw[:, slot], w_hi[:, slot], ALU.subtract).then_inc(low_ready, 1)

        def splits(part, eng, fl, units=UNITS, hooks=None, last=False):
            for j in range(units):
                if hooks and j in hooks:
                    hooks[j]()
                if not last or j + RING < units:
                    part(eng, fl, j + RING)
            fl.next(units)

        def chunk_done(eng, fl, units_after=0):
            eng.wait_ge(unit_used, fl.unit(-units_after) + RING)

        def chunk_ps(fl, chunks_after=0):
            return out_ps[(fl.c - 1 - chunks_after) % 2]

        def product(pe, fl, acts, units=UNITS, n=W, tiles=NT, by_channel=False, hooks=None):
            ps = out_ps[fl.c % 2]
            pe.wait_ge(out_free, fl.chunk() + 1)
            last = UNIT_K * units - 1
            for j in range(units):
                if hooks and j in hooks:
                    hooks[j]()
                slot = (fl.u + j) % RING
                pe.wait_ge(low_ready, fl.unit(j) + 1 + RING)
                for r in range(UNIT_K):
                    k = UNIT_K * j + r
                    for t in range(n // P if by_channel else tiles):
                        if by_channel:
                            o = ps[:, t // 2, (t % 2) * T:(t % 2) * T + T]
                            ws = slice(t * P, t * P + P)
                            pairs = [(w_hi[:, slot, r, ws], acts[0](k)), (w_hi[:, slot, r, ws], acts[1](k)),
                                     (w_lo[:, slot, r, ws], acts[0](k))]
                            first = k == 0 and t % 2 == 0
                        else:
                            o = ps[:, t, 0:n]
                            pairs = [(acts[0](k, t), w_hi[:, slot, r, 0:n]), (acts[0](k, t), w_lo[:, slot, r, 0:n]),
                                     (acts[1](k, t), w_hi[:, slot, r, 0:n])]
                            first = k == 0
                        for q, (lhs, rhs) in enumerate(pairs):
                            mm = pe.matmul(o, lhs, rhs, start=first and q == 0, stop=k == last and q == 2,
                                           skip_group_check=by_channel)
                mm.then_inc(unit_used, 1)
            fl.next(units)

        def tokens_of(hi, lo):
            return [lambda k, t=None, a=a: a[:, k, :] if t is None else a[:, k, t * P:t * P + P] for a in (hi, lo)]

        x_parts = tokens_of(x_hi, x_lo)
        y_parts = tokens_of(y_hi, y_lo)

        class Norm:

            def __init__(self, gain, squares, norms_before, rows_before, turns_before):
                self.gain, self.squares = gain, squares
                self.n, self.rows, self.turns = norms_before, rows_before, (turns_before or 0) * (KD // 2)

        norms = {"mix": Norm("g_mix", 4096, 0, 0, 0), "moe": Norm(None, 9216, 1, None, 1),
                 "ple": Norm("g_ple", 8704, 2, 1, 2), "final": Norm(None, 8704, 3, None, None),
                 "rec": Norm("rec_norm_2", 8704, 4, 2, 3), "att": Norm("att_norm_2", 4096, 5, 3, 4)}
        norm_s = {n: sem(f"norm_{n}") for n in ("h", "sums", "var", "root", "scale", "rows0", "rows1", "turned", "high",
                                           "low")}
        sum_sq, var, root, scale = (small[:, 2 * i:2 * i + 2] for i in range(4))
        xn = wk(0, NT * D).rearrange("p (t d) -> p t d", t=NT)

        def norm_stats_act(act, nm):
            act.wait_ge(norm_s["h"], nm.n + 1)
            for t in range(NT):
                act.activation(wk(nm.squares, D), h[:, t, :], ACT.Square, accum_out=sum_sq[:, t:t + 1])
                act.drain()
            act.drain().then_inc(norm_s["sums"], 1)
            act.wait_ge(norm_s["var"], nm.n + 1)
            act.activation(root, var, ACT.Sqrt).then_inc(norm_s["root"], 1)

        def norm_stats_dve(dve, nm):
            dve.drain().then_inc(norm_s["h"], 1)
            dve.wait_ge(norm_s["sums"], nm.n + 1)
            dve.tensor_scalar(var, sum_sq, 1.0 / D, EPS, ALU.mult, ALU.add).then_inc(norm_s["var"], 1)
            dve.wait_ge(norm_s["root"], nm.n + 1)
            dve.reciprocal(scale, root).then_inc(norm_s["scale"], 1)

        def norm_act(act, nm):
            norm_stats_act(act, nm)
            act.wait_ge(norm_s["scale"], nm.n + 1)
            act.activation(xn[:, 0, :], h[:, 0, :], ACT.Copy, scale=scale[:, 0:1]).then_inc(norm_s["rows0"], 1)
            for f in range(KD // 2):
                act.wait_ge(norm_s["turned"], nm.turns + f + 1)
                for kk in range(2):
                    k = 2 * f + kk
                    g = {"scale": col[nm.gain][:, k:k + 1]} if nm.gain else {}
                    i = act.activation(x_hi[:, k, :], bank(f % 4, kk * T, T), ACT.Copy, **g)
                i.then_inc(norm_s["high"], 1)

        def norm_dve(dve, nm):
            norm_stats_dve(dve, nm)
            dve.wait_ge(norm_s["scale"], nm.n + 1)
            dve.tensor_scalar(xn[:, 1, :], h[:, 1, :], scale[:, 1:2], None, ALU.mult).then_inc(norm_s["rows1"], 1)
            norm_low(dve, nm)

        def norm_low(dve, nm):
            for f in range(KD // 2):
                dve.wait_ge(norm_s["high"], nm.turns + f + 1)
                for kk in range(2):
                    k = 2 * f + kk
                    src = bank(f % 4, kk * T, T)
                    if nm.gain:
                        i = dve.scalar_tensor_tensor(x_lo[:, k, :], src, col[nm.gain][:, k:k + 1], x_hi[:, k, :],
                                                     ALU.mult, ALU.subtract)
                    else:
                        i = dve.tensor_tensor(x_lo[:, k, :], src, x_hi[:, k, :], ALU.subtract)
                i.then_inc(norm_s["low"], 1)

        def norm_fill(pe, nm, f):
            if f >= 4:
                pe.wait_ge(norm_s["low"], nm.turns + f - 3)
            for kk in range(2):
                for t in range(NT):
                    k = 2 * f + kk
                    i = pe.transpose(bank(f % 4, kk * T + t * P, P), xn[:, t, k * P:k * P + P], ident)
            i.then_inc(norm_s["turned"], 1)

        def norm_pe(pe, nm, rows=None, fills=KD // 2):
            for rows_of in [rows] if rows else [norm_s["rows0"], norm_s["rows1"]]:
                pe.wait_ge(rows_of, (nm.rows or 0) + 1)
            for f in range(fills):
                norm_fill(pe, nm, f)
            if fills == KD // 2:
                pe.wait_ge(norm_s["low"], nm.turns + KD // 2)

        FIRST_FILLS = 6

        def norm_hooks(pe, nm):
            def at_unit(j):
                if j == 1:
                    for f in range(FIRST_FILLS, KD // 2):
                        norm_fill(pe, nm, f)
                pe.wait_ge(norm_s["low"], nm.turns + j + 1)

            return {j: lambda j=j: at_unit(j) for j in range(UNITS)}

        qk = wk(0, 16 * T).rearrange("p (n t) -> p n t", t=T)
        va = wk(4096, NT * 1024).rearrange("p (t n) -> p t n", t=NT)
        qb = wk(6144, 8 * T).rearrange("p (n t) -> p n t", t=T)
        kb = wk(8192, 2 * T).rearrange("p (n t) -> p n t", t=T)
        vb = wk(8704, NT * P).rearrange("p (t n) -> p t n", t=NT)
        bias_tabs = wk(8960, 3 * SCORE)
        t_delta, t_branches, t_window = (wk(8960 + SCORE * i, SCORE) for i in range(3))
        head_bias = wk(10112, SCORE)
        probs = [wk(10496 + SCORE * i, SCORE) for i in range(2)]
        probs_t = [wk(11264 + SCORE * i, SCORE) for i in range(2)]
        heads_o = [wk(12032 + T * i, T).rearrange("p (t n) -> p t n", t=NT) for i in range(2)]
        a_nmax, a_den, a_rden, a_sink = ([small[:, 8 + 4 * i + 2 * j:10 + 4 * i + 2 * j] for j in range(2)]
                                         for i in range(4))
        s_scores = sem("attn_scores")
        s_bank = sem("attn_scores_read")
        s_max = sem("attn_max")
        s_exp = sem("attn_probs")
        s_pt = sem("attn_turned")
        s_ptc = sem("attn_turned_copied")
        s_o = sem("attn_out")
        s_on = sem("attn_out_scaled")
        s_ot = sem("attn_out_turned")
        s_oh = sem("attn_out_high")
        s_ol = sem("attn_out_low")
        p1_copied = sem("proj_copied")
        keys_doubled = sem("keys_doubled")
        HEADS = [("b", i) for i in range(B_HEADS)] + [("a", i) for i in range(A_HEADS)]
        N_HEADS = len(HEADS)
        S_SCALE = {"a": A_DIM ** -0.5, "b": B_DIM ** -0.5}
        SLOPE = {"a": [2.0 ** (-8.0 * (i + 1) / A_HEADS) for i in range(A_HEADS)],
                 "b": [2.0 ** (-8.0 * (i + 1) / B_HEADS) for i in range(B_HEADS)]}
        W_IN = [("qb0", 6), ("kvb", 8), ("qb1", 7), ("qa0", 0), ("ka0", 2), ("va0", 4), ("qa1", 1), ("ka1", 3),
                ("va1", 5)]
        PROJ = {name: i + 1 for i, (name, _) in enumerate(W_IN)}
        STEP_AT = [1 + 2 * n for n in range(17)] + [36, 40, 44, 49]

        def out_tile(n):
            kind, i = HEADS[n]
            if kind == "a":
                return i
            return A_HEADS + i // 2 if i % 2 else None

        def tiles_until(n):
            return sum(out_tile(m) is not None for m in range(n + 1))

        def attn_hooks(chunk, first, step_a, step_b):
            hooks = {0: first} if first else {}
            for n, p in enumerate(STEP_AT):
                for q, step in ((p, step_a), (p + 1, step_b)):
                    j = q - UNITS * (chunk - 2)
                    if 0 <= j < UNITS:
                        hooks[j] = lambda n=n, step=step, before=hooks.get(j): (before and before(), step(n))
            return hooks

        def attn_rest(step_a, step_b):
            for n in range(len(STEP_AT), N_HEADS + 2):
                step_a(n)
                step_b(n)

        def pe_attn_a(pe):
            def scores(n):
                kind, i = HEADS[n]
                pe.wait_ge(p1_copied, PROJ[("qb1" if i >= B_HEADS // 2 else "kvb") if kind == "b" else
                                           ("ka1" if i >= A_HEADS // 2 else "ka0")])
                if kind == "b":
                    pe.wait_ge(keys_doubled, 32)
                if n >= 2:
                    pe.wait_ge(s_bank, n - 1)
                if kind == "a":
                    q, k, lo, hi = qk[:, i, :], qk[:, A_HEADS + i, :], 0, P
                else:
                    lo = B_DIM * (i % 2)
                    hi = lo + B_DIM
                    q, k = qb[:, i // 2, :], kb[:, i // B_GROUP, :]
                pe.matmul(bank(n % 2, 0, T), q[lo:hi, P:T], k[lo:hi, :], start=True, stop=True)
                pe.matmul(bank(n % 2, T, P), q[lo:hi, 0:P], k[lo:hi, 0:P], start=True,
                          stop=True).then_inc(s_scores, 1)

            def turn_probs(n):
                pe.wait_ge(s_exp, n + 1)
                if n:
                    pe.wait_ge(s_ptc, n)
                for b in range(3):
                    m = pe.transpose(bank(2, b * P, P), probs[n % 2][:, b * P:b * P + P], ident)
                m.then_inc(s_pt, 1)

            def turn_out(n):
                pe.wait_ge(s_on, n + 1)
                o = heads_o[out_tile(n) % 2]
                for t in range(NT):
                    m = pe.transpose(bank(3, T + t * P, P), o[:, t, :], ident)
                m.then_inc(s_ot, 1)

            def step(n):
                if n >= 2 and out_tile(n - 2) is not None:
                    turn_out(n - 2)
                if 1 <= n <= N_HEADS:
                    turn_probs(n - 1)
                if n < N_HEADS:
                    scores(n)

            return step

        def pe_attn_b(pe):
            def step(n):
                n -= 1
                if not 0 <= n < N_HEADS:
                    return
                kind, i = HEADS[n]
                pe.wait_ge(s_ptc, n + 1)
                pt = probs_t[n % 2]
                if n:
                    pe.wait_ge(s_on, n)
                    if tiles_until(n - 1):
                        pe.wait_ge(s_ol, tiles_until(n - 1))
                if kind == "a":
                    pe.wait_ge(p1_copied, PROJ["va1" if i >= A_HEADS // 2 else "va0"])
                    v, w = va[:, :, i * A_DIM:(i + 1) * A_DIM], A_DIM
                else:
                    g = i // B_GROUP
                    v, w = vb[:, :, g * B_DIM:(g + 1) * B_DIM], B_DIM
                pe.matmul(bank(3, P, w), pt[:, 0:P], v[:, 0, :], start=True, stop=False)
                pe.matmul(bank(3, P, w), pt[:, P:T], v[:, 1, :], start=False, stop=True)
                pe.matmul(bank(3, 0, w), pt[:, T:SCORE], v[:, 0, :], start=True, stop=True).then_inc(s_o, 1)

            return step

        def act_attn_a(act):
            def step(n):
                if n >= 2 and out_tile(n - 2) is not None:
                    act.wait_ge(s_ot, tiles_until(n - 2))
                    act.activation(y_hi[:, out_tile(n - 2), :], bank(3, T, T), ACT.Copy).then_inc(s_oh, 1)
                if 1 <= n <= N_HEADS:
                    act.wait_ge(s_pt, n)
                    act.activation(probs_t[(n - 1) % 2], bank(2, 0, SCORE), ACT.Copy).then_inc(s_ptc, 1)

            return step

        def act_attn_b(act):
            def step(n):
                if n >= N_HEADS:
                    return
                kind, i = HEADS[n]
                pr, nm, den = probs[n % 2], a_nmax[n % 2], a_den[n % 2]
                act.wait_ge(s_max, n + 1)
                act.activation(pr[:, 0:T], pr[:, 0:T], ACT.Exp, bias=nm[:, 1:2], accum_out=den[:, 1:2])
                e = act.activation(pr[:, T:SCORE], pr[:, T:SCORE], ACT.Exp, bias=nm[:, 0:1],
                                   accum_out=den[:, 0:1])
                if kind == "b":
                    e = act.activation(a_sink[n % 2], nm, ACT.Exp, bias=sinks[:, i:i + 1])
                e.then_inc(s_exp, 1)

            return step

        def dve_attn_a(dve):
            def bias_and_max(n):
                kind, i = HEADS[n]
                b = n % 2
                dve.scalar_tensor_tensor(head_bias, t_delta, -SLOPE[kind][i],
                                         t_branches if kind == "a" else t_window, ALU.mult, ALU.add)
                dve.wait_ge(s_scores, n + 1)
                if n >= 2:
                    dve.wait_ge(s_pt, n - 1)
                dve.drain()
                dve.scalar_tensor_tensor(probs[b], bank(b, 0, SCORE), S_SCALE[kind], head_bias, ALU.mult,
                                         ALU.add).then_inc(s_bank, 1)
                dve.drain()
                nm = a_nmax[b]
                dve.tensor_reduce(nm[:, 1:2], probs[b][:, 0:T], AX.X, ALU.max)
                dve.tensor_reduce(nm[:, 0:1], probs[b][:, T:SCORE], AX.X, ALU.max)
                dve.drain()
                if kind == "b":
                    dve.tensor_scalar(nm, nm, sinks[:, i:i + 1], -1.0, ALU.max, ALU.mult)
                else:
                    dve.tensor_scalar(nm, nm, -1.0, None, ALU.mult)
                dve.drain().then_inc(s_max, 1)

            def step(n):
                if n >= 2 and out_tile(n - 2) is not None:
                    tile = out_tile(n - 2)
                    dve.wait_ge(s_oh, tiles_until(n - 2))
                    dve.tensor_tensor(y_lo[:, tile, :], bank(3, T, T), y_hi[:, tile, :],
                                      ALU.subtract).then_inc(s_ol, 1)
                if n < N_HEADS:
                    bias_and_max(n)

            return step

        def dve_attn_b(dve):
            def step(n):
                n -= 1
                if not 0 <= n < N_HEADS:
                    return
                kind, i = HEADS[n]
                b = n % 2
                dve.wait_ge(s_exp, n + 1)
                if kind == "b":
                    dve.tensor_tensor(a_den[b], a_den[b], a_sink[b], ALU.add)
                    dve.drain()
                dve.reciprocal(a_rden[b], a_den[b])
                dve.drain()
                dve.wait_ge(s_o, n + 1)
                if kind == "a":
                    tile, lo, w = i, 0, A_DIM
                else:
                    tile, lo, w = A_HEADS + i // 2, B_DIM * (i % 2), B_DIM
                o = heads_o[tile % 2]
                for t in range(NT):
                    m = dve.tensor_scalar(o[:, t, lo:lo + w], bank(3, t * P, w), a_rden[b][:, t:t + 1], None, ALU.mult)
                m.then_inc(s_on, 1)

            return step

        def add_to_h(dve, fl, c, last=False):
            chunk_done(dve, fl)
            hs = h[:, :, c * W:(c + 1) * W]
            dve.tensor_tensor(hs, chunk_ps(fl)[:], hs, ALU.add).then_inc(out_free, 1)
            if last:
                dve.drain().then_inc(fin_ready, 1)

        gain_row = wk(4096, D)
        route_raw = wk(6144, KD * ROUTES).rearrange("p (k n) -> p k n", n=ROUTES)
        route_hi = e_hi[:, 0:KD * ROUTES].rearrange("p (k n) -> p k n", n=ROUTES)
        route_lo = e_lo[:, 0:KD * ROUTES].rearrange("p (k n) -> p k n", n=ROUTES)

        def tile2(a, n):
            return wk(a, NT * n).rearrange("p (t n) -> p t n", t=NT)

        logits = tile2(6720, ROUTES)
        m_off = tile2(6792, ROUTES)
        em = tile2(6864, N_EXPERTS)
        em2 = tile2(6928, N_EXPERTS)
        eq = tile2(6992, N_EXPERTS)
        cand = tile2(7056, N_EXPERTS)
        oh1 = tile2(7120, N_EXPERTS)
        oh2 = tile2(7184, N_EXPERTS)
        combine = tile2(7248, N_EXPERTS)
        g_eq = tile2(7312, N_GROUPS)
        g_cand = tile2(7320, N_GROUPS)
        g_one = tile2(7328, N_GROUPS)
        g_exp = tile2(7336, N_GROUPS)
        (gmax, gidx, gsum, gw, m1, m2, c1, c2, dm, e2, den2, w1, w2, key, cur, rank) = (
            wk(7344 + 2 * i, 2) for i in range(16))
        counts, over4, over4i = wk(7376, 4), wk(7380, 4), wk(7384, 4)
        ovf_f = wk(7388, 2)
        bases = wk(8960, N_GROUPS + 2)
        comb_rows = wk(7392, PER_GROUP)
        select_f = wk(7424, NT * P).rearrange("p (t n) -> p t n", t=NT)
        silu_g = [wk(7936 + D_EXPERT * i, D_EXPERT) for i in range(2)]
        hidden = [wk(8448 + D_EXPERT * i, D_EXPERT) for i in range(2)]
        xg_hi, xg_lo = (a[:].rearrange("p k t -> p (k t)") for a in (x_hi, x_lo))
        m_hi, m_lo = (a[:].rearrange("p k t -> p (k t)").rearrange("p (t d) -> p t d", t=NT) for a in (y_hi, y_lo))

        m_rows = sem("moe_rows")
        m_split_hi = sem("moe_rows_high")
        r_whi = sem("route_weights_high")
        r_wlo = sem("route_weights_low")
        moe_loads = sem("moe_loads")
        region_free = sem("attention_memory_free")
        r_out = sem("route_logits")
        r_gsub = sem("route_group_shifted")
        r_gexp = sem("route_group_exp")
        r_dm = sem("route_top_shifted")
        r_de = sem("route_top_exp")
        r_one = sem("route_one_hot")
        r_rank = sem("route_ranks")
        r_done = sem("route_done")
        sel_ready = sem("select_ready")
        sel_turned = sem("select_turned")
        sel_copied = sem("select_copied")
        comb_ready = sem("combine_rows_ready")
        g_done = sem("gathered")
        g_hi = sem("gathered_high")
        g_lo = sem("gathered_low")
        silu_done = sem("expert_silu")
        hid_ready = sem("expert_hidden")
        hid_turned = sem("expert_hidden_turned")
        hid_hi = sem("expert_hidden_high")
        hid_lo = sem("expert_hidden_low")
        dn_hi = sem("down_high")
        dn_lo = sem("down_low")
        sc_done = sem("scattered")
        sc_add = sem("scattered_added")

        MOE_UNITS = PER_GROUP * UNITS + D // W * UNITS
        MOE_CHUNKS = PER_GROUP + D // W

        def bc(ap, n):
            return ap.unsqueeze(2).to_broadcast([P, ap.shape[1], n])

        def route_dve(dve):
            dr = dve.drain
            lg, le = logits[:, :, 0:N_GROUPS], logits[:, :, N_GROUPS:ROUTES]
            idx = kept("index")
            idx_g = idx[:, 0:N_GROUPS].unsqueeze(1).to_broadcast([P, NT, N_GROUPS])
            idx_e = idx.unsqueeze(1).to_broadcast([P, NT, N_EXPERTS])
            dve.wait_ge(r_out, 1)
            for t in range(NT):
                dve.tensor_tensor(logits[:, t, :], bank(0, 64 * t, ROUTES), route_b, ALU.add)
            dr()

            def first_max(values, n, top, hit, cnd, at, one, idx_ap):
                dve.tensor_reduce(top, values, AX.X, ALU.max)
                dr()
                dve.tensor_tensor(hit, values, bc(top, n), ALU.is_equal)
                dr()
                dve.tensor_scalar(cnd, hit, -1000.0, 1000.0, ALU.mult, ALU.add)
                dr()
                dve.tensor_tensor(cnd, cnd, idx_ap, ALU.add)
                dr()
                dve.tensor_reduce(at, cnd, AX.X, ALU.min)
                dr()
                dve.tensor_tensor(one, cnd, bc(at, n), ALU.is_equal)
                dr()

            first_max(lg, N_GROUPS, gmax, g_eq, g_cand, gidx, g_one, idx_g)
            dve.drain().then_inc(r_one, 1)
            dve.tensor_tensor(g_exp, lg, bc(gmax, N_GROUPS), ALU.subtract)
            dve.drain().then_inc(r_gsub, 1)
            off = m_off[:, :, 0:N_GROUPS]
            dve.tensor_scalar(off, g_one, BIG, -BIG, ALU.mult, ALU.add)
            dr()
            for t in range(NT):
                dve.tensor_tensor(em[:, t, :].rearrange("p (g e) -> p g e", g=N_GROUPS),
                                  le[:, t, :].rearrange("p (g e) -> p g e", g=N_GROUPS),
                                  bc(off[:, t, :], PER_GROUP), ALU.add)
            dr()
            first_max(em, N_EXPERTS, m1, eq, cand, c1, oh1, idx_e)
            dve.scalar_tensor_tensor(em2, oh1, -3.0 * BIG, em, ALU.mult, ALU.add)
            dr()
            first_max(em2, N_EXPERTS, m2, eq, cand, c2, oh2, idx_e)
            dve.tensor_tensor(dm, m2, m1, ALU.subtract)
            dve.drain().then_inc(r_dm, 1)
            dve.wait_ge(r_gexp, 1)
            dve.tensor_reduce(gsum, g_exp, AX.X, ALU.add)
            dr()
            dve.reciprocal(gw, gsum)
            dve.wait_ge(r_de, 1)
            dve.tensor_scalar(den2, e2, 1.0, None, ALU.add)
            dr()
            dve.reciprocal(w1, den2)
            dr()
            dve.tensor_tensor(w1, w1, gw, ALU.mult)
            dr()
            dve.tensor_tensor(w2, w1, e2, ALU.mult)
            dr()
            dve.tensor_tensor(oh1, oh1, bc(w1, N_EXPERTS), ALU.mult)
            dve.tensor_tensor(oh2, oh2, bc(w2, N_EXPERTS), ALU.mult)
            dr()
            dve.tensor_tensor(combine, oh1, oh2, ALU.add)
            dve.wait_ge(r_rank, 1)
            for t in range(NT):
                dve.tensor_tensor(g_cand[:, t, :], bank(1, 8 * t, N_GROUPS), g_one[:, t, :], ALU.mult)
            dve.tensor_copy(counts, bank(1, 16, N_GROUPS))
            dr()
            dve.tensor_reduce(rank, g_cand, AX.X, ALU.add)
            dr()
            dve.scalar_tensor_tensor(key, gidx, 2.0 * P, rank, ALU.mult, ALU.add)
            dve.tensor_scalar(over4, counts, float(P), None, ALU.is_gt)
            dr()
            dve.tensor_tensor(over4i, over4, idx[:, 0:N_GROUPS], ALU.mult)
            dr()
            dve.tensor_reduce(ovf_f[:, 0:1], over4, AX.X, ALU.max)
            dve.tensor_reduce(ovf_f[:, 1:2], over4i, AX.X, ALU.max)
            dr()
            dve.tensor_scalar(bases[:, 0:N_GROUPS], idx[:, 0:N_GROUPS], 2.0 * P, None, ALU.mult)
            dve.tensor_scalar(bases[:, N_GROUPS:N_GROUPS + 1], ovf_f[:, 1:2], 2.0 * P, float(P), ALU.mult, ALU.add)
            dve.memset(bases[:, N_GROUPS + 1:], 16.0 * P)
            dve.tensor_copy(ovf[:], ovf_f)
            dve.drain().then_inc(r_done, 1)

        def route_act(act):
            act.wait_ge(r_gsub, 1)
            act.activation(g_exp, g_exp, ACT.Exp).then_inc(r_gexp, 1)
            act.wait_ge(r_dm, 1)
            act.activation(e2, dm, ACT.Exp).then_inc(r_de, 1)

        def route_pe(pe):
            pe.wait_ge(r_wlo, 1)
            for t in range(NT):
                for k in range(KD):
                    for q, (lhs, rhs) in enumerate(((x_hi, route_hi), (x_hi, route_lo), (x_lo, route_hi))):
                        m = pe.matmul(bank(0, 64 * t, ROUTES), lhs[:, k, t * P:t * P + P], rhs[:, k, :],
                                      start=k == 0 and q == 0, stop=k == KD - 1 and q == 2)
            m.then_inc(r_out, 1)
            pe.wait_ge(r_one, 1)
            before, ones = kept("before"), kept("ones")
            pe.matmul(bank(1, 0, N_GROUPS), before, g_one[:, 0, :], start=True, stop=True)
            pe.matmul(bank(1, 8, N_GROUPS), before, g_one[:, 1, :], start=True, stop=False)
            pe.matmul(bank(1, 8, N_GROUPS), ones, g_one[:, 0, :], start=False, stop=True)
            pe.matmul(bank(1, 16, N_GROUPS), ones, g_one[:, 0, :], start=True, stop=False)
            pe.matmul(bank(1, 16, N_GROUPS), ones, g_one[:, 1, :], start=False, stop=True).then_inc(r_rank, 1)

        gathered = [lambda k, t, a=a: a[:, k * P:k * P + P] for a in (xg_hi, xg_lo)]
        hid = [lambda k, t, a=a: a[:, D + k * P:D + k * P + P] for a in (xg_hi, xg_lo)]

        def gather_pe(pe, i, f):
            b, part = f // 2, (m_hi, m_lo)[f % 2]
            if f == 0:
                pe.wait_ge(sel_ready, i + 1)
            if f >= 2:
                pe.wait_ge((g_hi, g_lo)[f % 2], i * 4 + (f - 2) // 2 + 1)
            for dd in range(4):
                for t in range(NT):
                    m = pe.matmul(bank(2 + f % 2, dd * P, P), part[:, t, (4 * b + dd) * P:(4 * b + dd + 1) * P],
                                  select[:, t, :], start=t == 0, stop=t == 1)
            m.then_inc(g_done, 1)

        def gather_act(act, i, b):
            act.wait_ge(g_done, i * 8 + 2 * b + 1)
            act.activation(xg_hi[:, b * W:(b + 1) * W], bank(2), ACT.Copy).then_inc(g_hi, 1)

        def gather_dve(dve, i, b):
            dve.wait_ge(g_done, i * 8 + 2 * b + 2)
            dve.tensor_copy(xg_lo[:, b * W:(b + 1) * W], bank(3)).then_inc(g_lo, 1)

        def select_dve(dve, i):
            dve.tensor_scalar(cur, key, bases[:, bass.ds(i, 1)], None, ALU.subtract)
            dve.drain()
            for t in range(NT):
                dve.tensor_scalar(select_f[:, t, :], kept("iota"), cur[:, t:t + 1], None, ALU.is_equal)
                dve.tensor_scalar(select[:, t, :], kept("iota"), cur[:, t:t + 1], None, ALU.is_equal)
            dve.drain().then_inc(sel_ready, 1)

        def moe_pe(pe, fl, i):
            def turn_select():
                pe.wait_ge(sc_add, i * 8 + 1)
                for t in range(NT):
                    pe.transpose(bank(0, t * P, P), select_f[:, t, :], ident)
                for t in range(NT):
                    m = pe.matmul(bank(0, T, N_EXPERTS), select_f[:, t, :], combine[:, t, :], start=t == 0,
                                  stop=t == 1)
                m.then_inc(sel_turned, 1)

            def turn_hidden(e, s):
                pe.wait_ge(comb_ready, i + 1)
                pe.wait_ge(hid_lo, i * 8 + e + 1)
                pe.wait_ge(hid_ready, i * 8 + e + 1)
                for b in range(2):
                    m = pe.transpose(bank(0, b * P, P), hidden[s][:, b * P:b * P + P], ident)
                m.then_inc(hid_turned, 1)

            def scatter(f):
                c, t = f // 2, f % 2
                pe.wait_ge(dn_lo, i * 4 + c + 1)
                if f >= 2:
                    pe.wait_ge(sc_add, i * 8 + f)
                for q, part in enumerate((e_hi, e_lo)):
                    m = pe.matmul(bank(f % 2), select_t[:, t * P:t * P + P], part[:, c * W:(c + 1) * W],
                                  start=q == 0, stop=q == 1)
                m.then_inc(sc_done, 1)

            pe.wait_ge(g_lo, i * 4 + 4)
            pe.wait_ge(g_hi, i * 4 + 4)
            product(pe, fl, gathered, tiles=1, hooks={1: turn_select})
            with fl.loop(pe, PER_GROUP // 2 - 1, 2 * UNITS, 2) as ep:
                for s in range(2):
                    product(pe, fl, gathered, tiles=1, hooks={3: lambda: turn_hidden(ep * 2 + s, s)})
            product(pe, fl, gathered, tiles=1, hooks={3: lambda: turn_hidden(PER_GROUP - 2, 0)})
            pe.wait_ge(hid_lo, i * 8 + PER_GROUP)
            product(pe, fl, hid, tiles=1, hooks={
                3: lambda: turn_hidden(PER_GROUP - 1, 1),
                7: lambda: pe.wait_ge(hid_lo, i * 8 + PER_GROUP + 1)})
            fill = lambda f: lambda: gather_pe(pe, i + 1, f)
            put = lambda f: lambda: scatter(f)
            product(pe, fl, hid, tiles=1, hooks={2: fill(0), 3: put(0), 4: fill(1), 5: put(1), 6: fill(2), 7: fill(3)})
            product(pe, fl, hid, tiles=1, hooks={2: fill(4), 3: put(2), 4: fill(5), 5: put(3), 6: fill(6), 7: fill(7)})
            product(pe, fl, hid, tiles=1, hooks={3: put(4), 5: put(5)})
            scatter(6)
            scatter(7)

        def moe_act(act, fl, i):
            def select_high():
                act.wait_ge(sel_turned, i + 1)
                act.activation(select_t[:], bank(0, 0, T), ACT.Copy).then_inc(sel_copied, 1)

            def silu(e, s):
                chunk_done(act, fl)
                act.activation(silu_g[s], chunk_ps(fl)[:, 0, 0:D_EXPERT], ACT.Silu).then_inc(silu_done, 1)

            def hid_high(e, s):
                act.wait_ge(hid_turned, i * 8 + e + 1)
                act.activation(xg_hi[:, bass.ds(e * T + D, T)], bank(0, 0, T), ACT.Copy).then_inc(hid_hi, 1)

            def down_high(c):
                chunk_done(act, fl)
                act.activation(e_hi[:, c * W:(c + 1) * W], chunk_ps(fl)[:, 0, :], ACT.Copy).then_inc(dn_hi, 1)

            splits(high, act, fl, hooks={2: select_high})
            with fl.loop(act, PER_GROUP // 2 - 1, 2 * UNITS, 2) as ep:
                for s in range(2):
                    splits(high, act, fl, hooks={0: lambda: silu(ep * 2 + s, s), 4: lambda: hid_high(ep * 2 + s, s)})
            for e, s in ((PER_GROUP - 2, 0), (PER_GROUP - 1, 1)):
                splits(high, act, fl, hooks={0: lambda: silu(e, s), 4: lambda: hid_high(e, s)})
            row = lambda b: lambda: gather_act(act, i + 1, b)
            splits(high, act, fl, hooks={0: lambda: down_high(0), 3: row(0), 7: row(1)})
            splits(high, act, fl, hooks={0: lambda: down_high(1), 3: row(2), 7: row(3)})
            splits(high, act, fl, hooks={0: lambda: down_high(2)})
            down_high(3)

        def moe_dve(dve, fl, i):
            def combine_rows():
                dve.wait_ge(sel_copied, i + 1)
                dve.tensor_reduce(comb_rows, bank(0, T, N_EXPERTS).rearrange("p (g e) -> p e g", g=N_GROUPS), AX.X,
                                  ALU.add).then_inc(comb_ready, 1)

            def gate(e, s):
                dve.wait_ge(silu_done, i * 8 + e + 1)
                dve.scalar_tensor_tensor(hidden[s], chunk_ps(fl)[:, 0, D_EXPERT:2 * D_EXPERT],
                                         comb_rows[:, bass.ds(e, 1)], silu_g[s], ALU.mult,
                                         ALU.mult).then_inc(hid_ready, 1)
                dve.drain().then_inc(out_free, 1)

            def hid_low(e, s):
                dve.wait_ge(hid_hi, i * 8 + e + 1)
                at = bass.ds(e * T + D, T)
                dve.tensor_tensor(xg_lo[:, at], bank(0, 0, T), xg_hi[:, at], ALU.subtract).then_inc(hid_lo, 1)

            def down_low(c):
                dve.wait_ge(dn_hi, i * 4 + c + 1)
                at = slice(c * W, (c + 1) * W)
                dve.tensor_tensor(e_lo[:, at], chunk_ps(fl)[:, 0, :], e_hi[:, at], ALU.subtract).then_inc(dn_lo, 1)
                dve.drain().then_inc(out_free, 1)

            def add_rows(f):
                c, t = f // 2, f % 2
                dve.wait_ge(sc_done, i * 8 + f + 1)
                hs = h[:, t, c * W:(c + 1) * W]
                dve.tensor_tensor(hs, bank(f % 2), hs, ALU.add).then_inc(sc_add, 1)

            splits(low, dve, fl, hooks={2: combine_rows})
            with fl.loop(dve, PER_GROUP // 2 - 1, 2 * UNITS, 2) as ep:
                for s in range(2):
                    splits(low, dve, fl, hooks={0: lambda: gate(ep * 2 + s, s), 4: lambda: hid_low(ep * 2 + s, s)})
            splits(low, dve, fl, hooks={0: lambda: gate(PER_GROUP - 2, 0), 4: lambda: hid_low(PER_GROUP - 2, 0)})
            splits(low, dve, fl, hooks={0: lambda: gate(PER_GROUP - 1, 1), 4: lambda: hid_low(PER_GROUP - 1, 1),
                                        6: lambda: select_dve(dve, i + 1)})
            row = lambda b: lambda: gather_dve(dve, i + 1, b)
            add = lambda f: lambda: add_rows(f)
            splits(low, dve, fl, hooks={0: lambda: down_low(0), 4: add(0), 5: row(0), 6: add(1)})
            splits(low, dve, fl, hooks={0: lambda: (row(1)(), down_low(1)), 4: add(2), 5: row(2), 6: add(3)})
            splits(low, dve, fl, hooks={0: lambda: (row(3)(), down_low(2)), 4: add(4), 6: add(5)})
            down_low(3)
            add_rows(6)
            add_rows(7)

        def moe_sp(sp, fl, g):
            gates, ups = (d[n][0].rearrange("e k f -> (e k) f") for n in ("w_gate", "w_up"))
            downs = d["w_down"][0].rearrange("e f n -> (e f) n")
            with fl.loop(sp, PER_GROUP // 2, 2 * UNITS, 2) as ep:
                for s in range(2):
                    row = g * (PER_GROUP * D) + ep * (2 * D) + s * D
                    for j in range(UNITS):
                        load_unit(sp, fl, j, [
                            (m[bass.ds(row + j * UNIT_K * P, UNIT_K * P), :].rearrange("(r p) f -> p r f", p=P), None, a)
                            for m, a in ((gates, 0), (ups, D_EXPERT))])
                    fl.next(UNITS)
            with fl.loop(sp, 2, 2 * UNITS, 2) as cp:
                for s in range(2):
                    load_chunk(sp, fl, downs, g * (PER_GROUP * D_EXPERT), cp * (2 * W) + s * W)

        pp = wk(0, NT * D).rearrange("p (t d) -> p t d", t=NT)
        p_rows = wk(4096, NT * PLE_DIM).rearrange("p (t d) -> p t d", t=NT)
        sig = wk(4608, NT * W).rearrange("p (t d) -> p t d", t=NT)
        sig2 = wk(5632, NT * W).rearrange("p (t d) -> p t d", t=NT)
        final_gain = wk(6656, D)
        pt_hi, pt_lo = (a[:, 0:2 * T].rearrange("p (k t) -> p k t", k=2) for a in (e_hi, e_lo))
        ple_loads = sem("ple_loads")
        moe_memory_free = sem("moe_memory_free")
        pt_turned = sem("ple_turned")
        pt_high = sem("ple_high")
        pt_low = sem("ple_low")
        ple_sig = sem("ple_sigmoid")
        ple_used = sem("ple_sigmoid_used")
        first_done = sem("first_block_scaled")

        PAD = CONV - 1
        rg_x = wk(0, 4 * (T + PAD)).rearrange("p (n t) -> p n t", n=4)
        base = 1040
        (rg_c, rg_s, rg_r, rg_i, rg_a, rg_t, rg_u, rg_y) = (
            wk(base + 1024 * i, 1024).rearrange("p (n t) -> p n t", n=4) for i in range(8))
        decay = small[:, 32:48]
        wait_carrier = small[:, 95:96]
        sp_t = [small[:, 48 + 16 * i:64 + 16 * i] for i in range(3)]
        c_hi, c_lo = (a[:, 0:4 * T].rearrange("p (n t) -> p n t", n=4) for a in (e_hi, e_lo))
        rg = {n: sem("rg_" + n) for n in ("x", "conv", "chigh", "clow", "silu", "gates", "rate", "exp", "sq",
                                          "root", "y", "yhigh", "ylow", "lam")}

        def pe_rg(pe, fl):
            for g in range(4):
                product(pe, fl, x_parts, by_channel=True, hooks=None if g else norm_hooks(pe, norms["rec"]))
                product(pe, fl, x_parts, by_channel=True)
                pe.wait_ge(rg["clow"], g + 1)
                for hh in range(2):
                    product(pe, fl, [lambda k, a=a: a[:, 2 * hh + k, :] for a in (c_hi, c_lo)], units=1,
                            by_channel=True)

        def act_rg(act, fl):
            def x_out(g):
                chunk_done(act, fl)
                act.activation(rg_x[:, :, PAD:PAD + T], by_channel(fl), ACT.Copy).then_inc(out_free, 1)
                act.drain().then_inc(rg["x"], 1)

            def conv_high(g):
                act.wait_ge(rg["conv"], g + 1)
                act.activation(c_hi, rg_c, ACT.Copy).then_inc(rg["chigh"], 1)

            def gates(g, hh):
                chunk_done(act, fl)
                for q in range(4):
                    n = 2 * hh + q % 2
                    dst = (rg_r, rg_i)[q // 2][:, n, :]
                    b = col[("rg_b_gate_a_2", "rg_b_gate_x_2")[q // 2]]
                    m = act.activation(dst, chunk_ps(fl)[:, q // 2, (q % 2) * T:(q % 2) * T + T], ACT.Sigmoid,
                                       bias=b[:, bass.ds(g * 4 + n, 1)])
                m.then_inc(out_free, 1)
                if hh:
                    act.drain().then_inc(rg["gates"], 1)

            def rate_exp(g):
                act.wait_ge(rg["rate"], g + 1)
                act.activation(rg_a, rg_r, ACT.Exp, scale=-1.0)
                act.activation(rg_t, rg_r, ACT.Tanh).then_inc(rg["exp"], 1)

            def root(g):
                act.wait_ge(rg["sq"], g + 1)
                act.activation(rg_t, rg_u, ACT.Sqrt).then_inc(rg["root"], 1)

            def y_high(g):
                act.wait_ge(rg["y"], g + 1)
                act.activation(y_hi[:, bass.ds(g * 4, 4), :], rg_y, ACT.Copy).then_inc(rg["yhigh"], 1)

            recurrence = lambda g: {0: lambda: gates(g, 1), 2: lambda: rate_exp(g), 3: lambda: root(g),
                                    5: lambda: y_high(g)}
            for g in range(4):
                splits(high, act, fl, hooks=recurrence(g - 1) if g else None)
                splits(high, act, fl, hooks={0: lambda: x_out(g), 4: lambda: conv_high(g)})
                chunk_done(act, fl)
                act.activation(rg_s, by_channel(fl), ACT.Silu).then_inc(out_free, 1)
                splits(high, act, fl, units=1)
                gates(g, 0)
                splits(high, act, fl, units=1)
            return recurrence(3)

        def by_channel(fl):
            return chunk_ps(fl)[:].rearrange("p a (b t) -> p (a b) t", t=T)

        def dve_rg(dve, fl):
            dve.memset(rg_x[:, :, 0:PAD], 0.0)
            def conv(g):
                dve.wait_ge(rg["x"], g + 1)
                for tap in range(CONV - 1, -1, -1):
                    for n in range(4):
                        w = conv_w[:, tap, :][:, bass.ds(g * 4 + n, 1)]
                        src = rg_x[:, n, tap:tap + T]
                        if tap == CONV - 1:
                            dve.tensor_scalar(rg_c[:, n, :], src, w, conv_b[:, bass.ds(g * 4 + n, 1)], ALU.mult,
                                              ALU.add)
                        else:
                            dve.scalar_tensor_tensor(rg_c[:, n, :], src, w, rg_c[:, n, :], ALU.mult, ALU.add)
                    dve.drain()
                dve.drain().then_inc(rg["conv"], 1)

            def conv_low(g):
                dve.wait_ge(rg["chigh"], g + 1)
                dve.tensor_tensor(c_lo, rg_c, c_hi, ALU.subtract).then_inc(rg["clow"], 1)

            def rates(g):
                dve.wait_ge(rg["gates"], g + 1)
                for n in range(4):
                    dve.tensor_scalar(rg_r[:, n, :], rg_r[:, n, :], decay[:, bass.ds(g * 4 + n, 1)], None, ALU.mult)
                dve.drain().then_inc(rg["rate"], 1)
                dve.tensor_tensor(rg_i, rg_i, rg_c, ALU.mult)

            def squares(g):
                dve.wait_ge(rg["exp"], g + 1)
                dve.tensor_tensor(rg_u, rg_a, rg_a, ALU.mult)
                dve.drain()
                dve.scalar_tensor_tensor(rg_u, rg_u, 1.0, rg_t, ALU.add, ALU.mult)
                dve.drain().then_inc(rg["sq"], 1)

            def scan(g):
                dve.wait_ge(rg["root"], g + 1)
                dve.tensor_tensor(rg_u, rg_t, rg_i, ALU.mult)
                dve.drain()
                for n in range(4):
                    dve.tensor_tensor_scan(rg_t[:, n, :], rg_a[:, n, :], rg_u[:, n, :], 0.0, ALU.mult, ALU.add)
                dve.drain()
                dve.tensor_tensor(rg_y, rg_t, rg_s, ALU.mult).then_inc(rg["y"], 1)

            def y_low(g):
                dve.wait_ge(rg["yhigh"], g + 1)
                dve.tensor_tensor(y_lo[:, bass.ds(g * 4, 4), :], rg_y, y_hi[:, bass.ds(g * 4, 4), :],
                                  ALU.subtract).then_inc(rg["ylow"], 1)

            recurrence = lambda g: {1: lambda: rates(g), 3: lambda: squares(g), 4: lambda: scan(g),
                                    6: lambda: y_low(g)}
            for g in range(4):
                splits(low, dve, fl, hooks=recurrence(g - 1) if g else None)
                splits(low, dve, fl, hooks={1: lambda: conv(g), 5: lambda: conv_low(g)})
                splits(low, dve, fl, units=1)
                splits(low, dve, fl, units=1)
            return recurrence(3)

        def sp_rg(sp, fl):
            w = d["rec_w_in_2"][0]
            ga, gx = (d[n][0].rearrange("h k n -> (h k) n") for n in ("rg_w_gate_a_2", "rg_w_gate_x_2"))
            for g in range(4):
                load_chunk(sp, fl, w, 0, g * W)
                load_chunk(sp, fl, w, 0, g * W + D)
                for hh in range(2):
                    row = g * (2 * 256) + hh * 256
                    load_unit(sp, fl, 0, [
                        (m[bass.ds(row, 256), :].rearrange("(r p) f -> p r f", p=P), None, a)
                        for m, a in ((ga, 0), (gx, 256))])
                    fl.next(1)

        def hgv(a):
            return wk(a, 1024).rearrange("p (n t) -> p n t", n=4)

        hq, hk, hf, hb, hv, hs_, he, hqp, hkp, hst = (hgv(1024 * i) for i in range(10))
        hv_rows, hs_rows, hy_rows, hsq = (a.rearrange("p n t -> p (n t)").rearrange("p (t d) -> p t d", t=NT)
                                          for a in (hv, hs_, hf, he))
        hst8 = wk(9216, 1024).rearrange("p (n t) -> p n t", n=8)
        hsx = wk(10240, 512).rearrange("p (n t) -> p n t", n=4)
        n_masks = len(LEVELS) + 1
        masks = wk(10752, n_masks * P)
        reset = wk(11776, 1024)
        flat = lambda a: a.rearrange("p n t -> p (n t)")
        hg = {n: sem("hg_" + n) for n in ("loads", "free", "f", "abs", "ln", "logk", "kexp", "arg", "exp",
                                          "parts", "scores", "masked", "o", "sq", "var", "root", "y", "turned",
                                          "yhigh", "ylow")}
        h_ssq, h_var, h_root, h_scale = (small[:, 16 + 8 * i:24 + 8 * i] for i in range(4))

        NL = len(LEVELS) + 2

        LEVEL_AT = {False: tuple(range(2, 20, 2)), True: (2, 3, 5, 6, 8, 9, 11, 12, 14)}
        SCORES_AFTER = {False: 2, True: 1}
        TAIL_AT = {False: 20, True: 16}

        def hg_hooks(chunk, last, shift, level, others):
            hooks = {p - UNITS * chunk: f for p, f in others.items() if p // UNITS == chunk}
            for l, p in enumerate(LEVEL_AT[last]):
                if (p + shift) // UNITS == chunk:
                    j = p + shift - UNITS * chunk
                    hooks[j] = lambda l=l, first=hooks.get(j): (first and first(), level(l))
            return hooks

        def hg_groups(eng, fl, first, group):
            first()
            with fl.loop(eng, 3, 4 * UNITS, 4) as g:
                group(g, False)
            return group(3, True)

        def pe_hg(pe, fl):
            def scores(g, l):
                pe.wait_ge(hg["parts"], g * NL + l + 1)
                if l == 0:
                    pe.wait_ge(hg["kexp"], g + 1)
                if l >= 2:
                    pe.wait_ge(hg["masked"], g * NL + l - 1)
                kk, qq = (hk, hq) if l == 0 else (hkp, hqp)
                for n in range(4):
                    if l == NL - 1:
                        m = pe.matmul(bank(2 * (l % 2), n * P, P), kk[:, n, 0:P], qq[:, n, P:T], start=True,
                                      stop=True)
                        continue
                    for t in range(NT):
                        q = n * NT + t
                        m = pe.matmul(bank(2 * (l % 2) + q // 4, (q % 4) * P, P), kk[:, n, t * P:t * P + P],
                                      qq[:, n, t * P:t * P + P], start=True, stop=True)
                m.then_inc(hg["scores"], 1)

            def outputs(g):
                pe.wait_ge(hg["masked"], g * NL + NL)
                for n in range(4):
                    ch = slice(n * P, n * P + P)
                    pe.matmul(bank(0, n * P, P), hst8[:, n * NT, :], hv_rows[:, 0, ch], start=True, stop=True)
                    pe.matmul(bank(1, n * P, P), hst8[:, n * NT + 1, :], hv_rows[:, 1, ch], start=True, stop=False)
                    m = pe.matmul(bank(1, n * P, P), hsx[:, n, :], hv_rows[:, 0, ch], start=False, stop=True)
                m.then_inc(hg["o"], 1)

            def turn(g):
                pe.wait_ge(hg["y"], g + 1)
                for n in range(4):
                    for t in range(NT):
                        m = pe.transpose(bank(2 + n // 2, (n % 2) * T + t * P, P), hy_rows[:, t, n * P:n * P + P], ident)
                m.then_inc(hg["turned"], 1)

            def group(g, last):
                at_ = TAIL_AT[last]
                tail = {at_ + SCORES_AFTER[last]: lambda: outputs(g), at_ + (5 if last else 7): lambda: turn(g)}
                if last:
                    tail[at_ + 6] = lambda: pe.wait_ge(hg["ylow"], g + 1)
                hooks = lambda chunk: hg_hooks(chunk, last, SCORES_AFTER[last], lambda l: scores(g, l), tail)
                product(pe, fl, x_parts, hooks=hooks(0))
                product(pe, fl, x_parts, hooks=hooks(1))
                if last:
                    return hooks(2)
                product(pe, fl, x_parts, by_channel=True, hooks=hooks(2))
                product(pe, fl, x_parts, by_channel=True, hooks=hooks(3))
                pe.wait_ge(hg["ylow"], g + 1)

            def first():
                for _ in range(2):
                    product(pe, fl, x_parts, by_channel=True)

            return hg_groups(pe, fl, first, group)

        def act_hg(act, fl):
            def q_out(g):
                chunk_done(act, fl)
                act.activation(hq, by_channel(fl), ACT.Silu).then_inc(out_free, 1)

            def f_out(g):
                chunk_done(act, fl)
                act.activation(hf, by_channel(fl), ACT.Copy).then_inc(out_free, 1)
                act.drain().then_inc(hg["f"], 1)

            def v_out(g):
                chunk_done(act, fl)
                act.activation(hv_rows, chunk_ps(fl)[:], ACT.Copy).then_inc(out_free, 1)

            def s_out(g):
                chunk_done(act, fl)
                act.activation(hs_rows, chunk_ps(fl)[:], ACT.Silu).then_inc(out_free, 1)

            def log_part(g):
                act.wait_ge(hg["abs"], g + 1)
                act.activation(flat(he), flat(he), ACT.Exp)
                act.drain()
                act.activation(flat(he), flat(he), ACT.Ln, bias=1.0).then_inc(hg["ln"], 1)

            def level(g, l):
                if l == 0:
                    act.wait_ge(hg["logk"], g + 1)
                    act.activation(flat(hk), flat(hk), ACT.Exp, scale=-1.0).then_inc(hg["kexp"], 1)
                else:
                    act.wait_ge(hg["arg"], g * (NL - 1) + l)
                    act.activation(flat(he), flat(he), ACT.Exp).then_inc(hg["exp"], 1)

            def out_squares(g):
                act.wait_ge(hg["o"], g + 1)
                for t in range(NT):
                    m = act.activation(hsq[:, t, :], bank(t), ACT.Square)
                m.then_inc(hg["sq"], 1)

            def out_root(g):
                act.wait_ge(hg["var"], g + 1)
                act.activation(h_root, h_var, ACT.Sqrt).then_inc(hg["root"], 1)

            def y_high(g):
                act.wait_ge(hg["turned"], g + 1)
                act.activation(y_hi[:, bass.ds(g * 4, 4), :], mix[:, 2:4, :].rearrange("p a (n t) -> p (a n) t", t=T),
                               ACT.Copy).then_inc(hg["yhigh"], 1)

            def group(g, last):
                at_ = TAIL_AT[last]
                others = {0: lambda: f_out(g), 1: lambda: log_part(g), 8: lambda: v_out(g), 16: lambda: s_out(g),
                          at_ + 2: lambda: out_squares(g), at_ + 3: lambda: out_root(g),
                          at_ + (6 if last else 7): lambda: y_high(g)}
                if not last:
                    others[24] = lambda: q_out(g)
                hooks = lambda chunk: hg_hooks(chunk, last, 0, lambda l: level(g, l), others)
                splits(high, act, fl, hooks=hooks(0))
                splits(high, act, fl, hooks=hooks(1))
                if last:
                    return hooks(2)
                splits(high, act, fl, hooks=hooks(2))
                splits(high, act, fl, hooks=hooks(3))

            def first():
                splits(high, act, fl)
                splits(high, act, fl, hooks={0: lambda: q_out(0)})

            return hg_groups(act, fl, first, group)

        def dve_hg(dve, fl):
            dr = dve.drain
            dve.wait_ge(hg["loads"], 32)
            dve.memset(hst8, 0.0)
            dve.memset(hqp, 0.0)
            dve.memset(hkp, 0.0)
            dr()

            def log_part(g):
                dve.wait_ge(hg["f"], g + 1)
                dve.scalar_tensor_tensor(flat(he), flat(hf), -1.0, flat(hf), ALU.mult, ALU.min).then_inc(hg["abs"], 1)
                dve.tensor_scalar(flat(hq), flat(hq), float(P) ** -0.5, None, ALU.mult)
                dve.wait_ge(hg["ln"], g + 1)
                dve.scalar_tensor_tensor(flat(hk), flat(hf), 0.0, flat(he), ALU.max, ALU.add).then_inc(hg["logk"], 1)
                dve.scalar_tensor_tensor(flat(hf), flat(hf), 0.0, flat(he), ALU.min, ALU.subtract)
                dr()
                dve.tensor_tensor_scan(flat(hb), reset, flat(hf), 0.0, ALU.mult, ALU.add)

            def masked(g, l):
                dve.wait_ge(hg["scores"], g * NL + l + 1)
                if l == NL - 1:
                    dve.tensor_copy(hsx, bank(2 * (l % 2)).rearrange("p (n t) -> p n t", n=4)).then_inc(
                        hg["masked"], 1)
                    return
                mk = masks[:, (n_masks - 1 if l == 0 else l - 1) * P:][:, 0:P]
                b0 = 2 * (l % 2)
                dve.memset(wait_carrier, 0.0)
                dve.copy_predicated(hst8, mk.bitcast(U32).unsqueeze(1).to_broadcast([P, 8, P]),
                                    mix[:, b0:b0 + 2, :].rearrange("p a (n t) -> p (a n) t", t=P)).then_inc(
                    hg["masked"], 1)

            def level(g, l):
                if l == 0:
                    dve.drain().then_inc(hg["parts"], 1)
                    return
                if l < NL - 1:
                    m_ = LEVELS[l - 1]
                    halves = lambda a: flat(a).rearrange("p (b s m) -> p b s m", s=2, m=m_)
                    bb, ee = halves(hb), halves(he)
                    nb = 1024 // (2 * m_)
                    edge = bb[:, :, 0, m_ - 1:m_].to_broadcast([P, nb, m_])
                    dve.tensor_tensor(ee[:, :, 0, :], edge, bb[:, :, 0, :], ALU.subtract)
                    if m_ < HG_CHUNK:
                        dve.tensor_tensor(ee[:, :, 1, :], bb[:, :, 1, :], edge, ALU.subtract)
                    else:
                        dve.tensor_copy(ee[:, :, 1, :], bb[:, :, 1, :])
                    dve.drain().then_inc(hg["arg"], 1)
                    q_out, q_in, k_out, k_in = (halves(a) for a in (hqp, hq, hkp, hk))
                    if l >= 2:
                        masked(g, l - 1)
                    if l == 1:
                        dve.wait_ge(hg["kexp"], g + 1)
                    dve.wait_ge(hg["exp"], g * (NL - 1) + l)
                    dve.tensor_tensor(q_out[:, :, 1, :], q_in[:, :, 1, :], ee[:, :, 1, :], ALU.mult)
                    dve.tensor_tensor(k_out[:, :, 0, :], k_in[:, :, 0, :], ee[:, :, 0, :], ALU.mult)
                    if l == 1:
                        masked(g, 0)
                else:
                    c4 = lambda a: flat(a).rearrange("p (n c m) -> p n c m", c=4, m=HG_CHUNK)
                    bb, ee = c4(hb), c4(he)
                    end = lambda c: bb[:, :, c, HG_CHUNK - 1:HG_CHUNK].to_broadcast([P, 4, HG_CHUNK])
                    for c in range(2):
                        dve.tensor_tensor(ee[:, :, c, :], end(c), bb[:, :, c, :], ALU.subtract)
                    dve.tensor_copy(ee[:, :, 2, :], bb[:, :, 2, :])
                    dve.tensor_tensor(ee[:, :, 3, :], bb[:, :, 3, :], end(2), ALU.add)
                    dr()
                    dve.tensor_tensor(ee[:, :, 0, :], ee[:, :, 0, :], end(1), ALU.add)
                    dve.drain().then_inc(hg["arg"], 1)
                    masked(g, l - 1)
                    dve.wait_ge(hg["exp"], g * (NL - 1) + l)
                    dve.tensor_tensor(hqp[:, :, P:T], hq[:, :, P:T], he[:, :, P:T], ALU.mult)
                    dve.tensor_tensor(hkp[:, :, 0:P], hk[:, :, 0:P], he[:, :, 0:P], ALU.mult)
                dve.drain().then_inc(hg["parts"], 1)

            def out_var(g):
                dve.wait_ge(hg["sq"], g + 1)
                dve.tensor_reduce(h_ssq.rearrange("p (t n) -> p t n", t=NT), hsq.rearrange("p t (n d) -> p t n d", d=P),
                                  AX.X, ALU.add)
                dr()
                dve.tensor_scalar(h_var, h_ssq, 1.0 / P, EPS, ALU.mult, ALU.add).then_inc(hg["var"], 1)

            def y_rows(g):
                dve.wait_ge(hg["root"], g + 1)
                dve.reciprocal(h_scale, h_root)
                dr()
                for t in range(NT):
                    v = lambda a: a[:, t, :].rearrange("p (n d) -> p n d", d=P)
                    dve.tensor_tensor(v(hy_rows), bank(t).rearrange("p (n d) -> p n d", d=P),
                                      bc(h_scale[:, 4 * t:4 * t + 4], P), ALU.mult)
                    dve.tensor_tensor(v(hs_rows), v(hs_rows), hg_gain.unsqueeze(1).to_broadcast([P, 4, P]), ALU.mult)
                dr()
                dve.tensor_tensor(hy_rows, hy_rows, hs_rows, ALU.mult).then_inc(hg["y"], 1)

            def y_low(g):
                dve.wait_ge(hg["yhigh"], g + 1)
                dve.tensor_tensor(y_lo[:, bass.ds(g * 4, 4), :], mix[:, 2:4, :].rearrange("p a (n t) -> p (a n) t", t=T),
                                  y_hi[:, bass.ds(g * 4, 4), :], ALU.subtract).then_inc(hg["ylow"], 1)

            def group(g, last):
                at_ = TAIL_AT[last]
                others = {1: lambda: log_part(g), at_: lambda: masked(g, NL - 1), at_ + 2: lambda: out_var(g),
                          at_ + 3: lambda: y_rows(g), at_ + (6 if last else 7): lambda: y_low(g)}
                hooks = lambda chunk: hg_hooks(chunk, last, 0, lambda l: level(g, l), others)
                splits(low, dve, fl, hooks=hooks(0))
                splits(low, dve, fl, hooks=hooks(1))
                if last:
                    return hooks(2)
                splits(low, dve, fl, hooks=hooks(2))
                splits(low, dve, fl, hooks=hooks(3))

            def first():
                for _ in range(2):
                    splits(low, dve, fl)

            return hg_groups(dve, fl, first, group)

        def sp_hg(sp, fl):
            w = d["rec_w_in_2"][0]

            def group(g, last):
                for n in (4, 5):
                    load_chunk(sp, fl, w, 0, g * W + n * D)
                if not last:
                    for n in (2, 3):
                        load_chunk(sp, fl, w, 0, g * W + (W + n * D))

            def first():
                for n in (2, 3):
                    load_chunk(sp, fl, w, 0, n * D)

            hg_groups(sp, fl, first, group)

        t_raw, t_sq = (wk(1024 * i, 1024).rearrange("p (t d) -> p t d", t=NT) for i in range(2))
        t_v, t_s = (wk(2048 + 1024 * i, 1024).rearrange("p (t d) -> p t d", t=NT) for i in range(2))
        t_q, t_k = (wk(4096 + 1024 * i, 1024).rearrange("p (n t) -> p n t", n=4) for i in range(2))
        t_p = [wk(6144 + SCORE * i, SCORE) for i in range(4)]
        t_a = [wk(7680 + SCORE * i, SCORE) for i in range(2)]
        t_pt = [wk(8448 + SCORE * i, SCORE) for i in range(2)]
        t_ys = [wk(a, 512).rearrange("p (t d) -> p t d", t=NT) for a in (9216, 12288)]
        t_mask = wk(9728, SCORE)
        lam_rows = wk(10112, 512)
        t_raws = (t_raw, wk(11264, 1024).rearrange("p (t d) -> p t d", t=NT))
        rope_t = [wk(10752 + P * i, P).rearrange("p (a n) -> p a n", n=HALF) for i in range(4)]
        at = {n: sem("att_" + n) for n in ("loads", "free", "lam", "lamexp", "sq", "var", "root", "rows",
                                           "turned", "copied", "scores", "read", "max", "exp", "mixed", "pturned",
                                           "pcopied", "o", "osq", "ovar", "oroot", "y", "yturned", "yhigh", "ylow",
                                           "s")}
        lam2, lam = small[:, 48:50], small[:, 50:51]
        t_ssq, t_scale = small[:, 16:24], small[:, 24:32]
        t_var = [small[:, 32 + 8 * i:40 + 8 * i] for i in range(2)]
        t_root = [small[:, 8 * i:8 + 8 * i] for i in range(2)]
        t_nm = [small[:, 52 + 2 * i:54 + 2 * i] for i in range(4)]
        t_den = [small[:, 60 + 2 * i:62 + 2 * i] for i in range(4)]
        t_r = [small[:, 68 + 2 * i:70 + 2 * i] for i in range(4)]
        o_ssq, o_var, o_root, o_scale = ([small[:, 76 + 4 * i + 2 * hh:78 + 4 * i + 2 * hh] for hh in range(2)]
                                         for i in range(4))

        def att_groups(eng, fl, first, group):
            first()
            with fl.loop(eng, 3, 4 * UNITS, 4) as g:
                group(g, False)
            return group(3, True)

        def pe_att(pe, fl):
            def turn(g, n):
                pe.wait_ge(at["rows"], g * 2 + n + 1)
                if n:
                    pe.wait_ge(at["copied"], g * 2 + 1)
                for q in range(4):
                    for t in range(NT):
                        m = pe.transpose(bank(2 + q // 2, (q % 2) * T + t * P, P), t_raws[n][:, t, q * P:q * P + P],
                                         ident)
                m.then_inc(at["turned"], 1)

            def scores(g, n):
                if n == 0:
                    pe.wait_ge(at["copied"], g * 2 + 2)
                if n >= 2:
                    pe.wait_ge(at["read"], g * 4 + n - 1)
                pe.matmul(bank(n % 2, 0, T), t_q[:, n, P:T], t_k[:, n, :], start=True, stop=True)
                pe.matmul(bank(n % 2, T, P), t_q[:, n, 0:P], t_k[:, n, 0:P], start=True, stop=True).then_inc(
                    at["scores"], 1)

            def turn_probs(g, hh):
                pe.wait_ge(at["mixed"], g * 2 + hh + 1)
                for b in range(3):
                    m = pe.transpose(bank(2 - 2 * hh, b * P, P), t_a[hh][:, b * P:b * P + P], ident)
                m.then_inc(at["pturned"], 1)

            def outputs(g, hh):
                pe.wait_ge(at["pcopied"], g * 2 + hh + 1)
                ch = slice(hh * T, hh * T + T)
                pt, b = t_pt[hh], 3 - 2 * hh
                pe.matmul(bank(b, T, T), pt[:, 0:P], t_v[:, 0, ch], start=True, stop=False)
                pe.matmul(bank(b, T, T), pt[:, P:T], t_v[:, 1, ch], start=False, stop=True)
                pe.matmul(bank(b, 0, T), pt[:, T:SCORE], t_v[:, 0, ch], start=True, stop=True).then_inc(at["o"], 1)

            def turn_y(g, hh):
                pe.wait_ge(at["y"], g * 2 + hh + 1)
                for q in range(2):
                    for t in range(NT):
                        m = pe.transpose(bank(2 - 2 * hh, q * T + t * P, P), t_ys[hh][:, t, q * P:q * P + P], ident)
                m.then_inc(at["yturned"], 1)

            def group(g, last):
                product(pe, fl, x_parts, hooks={6: lambda: turn(g, 0)})
                product(pe, fl, x_parts, hooks={6: lambda: turn(g, 1)})
                product(pe, fl, x_parts, hooks={1: lambda: scores(g, 0), 2: lambda: scores(g, 1),
                                                4: lambda: scores(g, 2), 5: lambda: scores(g, 3)})
                tail = {1: lambda: turn_probs(g, 0), 2: lambda: outputs(g, 0), 3: lambda: turn_probs(g, 1),
                        4: lambda: outputs(g, 1), 5: lambda: turn_y(g, 0), 7: lambda: turn_y(g, 1)}
                if last:
                    tail[6] = lambda: (turn_y(g, 1), pe.wait_ge(at["ylow"], g * 2 + 2))
                    del tail[7]
                    return tail
                product(pe, fl, x_parts, hooks=tail)
                pe.wait_ge(at["ylow"], g * 2 + 2)

            return att_groups(pe, fl, lambda: product(pe, fl, x_parts, hooks=norm_hooks(pe, norms["att"])), group)

        def act_att(act, fl):
            act.wait_ge(at["lam"], 1)
            act.activation(lam2, lam2, ACT.Exp).then_inc(at["lamexp"], 1)

            def head_rows(g, n):
                chunk_done(act, fl)
                if n:
                    act.wait_ge(at["var"], g * 2 + 1)
                act.activation(t_raws[n], chunk_ps(fl)[:], ACT.Copy)
                act.activation(t_sq, chunk_ps(fl)[:], ACT.Square).then_inc(out_free, 1)
                act.drain().then_inc(at["sq"], 1)

            def head_root(g, n):
                act.wait_ge(at["var"], g * 2 + n + 1)
                act.activation(t_root[n], t_var[n], ACT.Sqrt).then_inc(at["root"], 1)

            def copy_turned(g, n):
                act.wait_ge(at["turned"], g * 2 + n + 1)
                act.activation((t_q, t_k)[n], mix[:, 2:4, :].rearrange("p a (n t) -> p (a n) t", t=T),
                               ACT.Copy).then_inc(at["copied"], 1)

            def v_out(g):
                chunk_done(act, fl)
                act.activation(t_v, chunk_ps(fl)[:], ACT.Copy).then_inc(out_free, 1)

            def s_out(g):
                chunk_done(act, fl)
                act.activation(t_s, chunk_ps(fl)[:], ACT.Silu).then_inc(out_free, 1)
                act.drain().then_inc(at["s"], 1)

            def exps(g, n):
                act.wait_ge(at["max"], g * 4 + n + 1)
                act.activation(t_p[n][:, 0:T], t_p[n][:, 0:T], ACT.Exp, bias=t_nm[n][:, 1:2],
                               accum_out=t_den[n][:, 1:2])
                act.activation(t_p[n][:, T:SCORE], t_p[n][:, T:SCORE], ACT.Exp, bias=t_nm[n][:, 0:1],
                               accum_out=t_den[n][:, 0:1]).then_inc(at["exp"], 1)

            def copy_probs(g, hh):
                act.wait_ge(at["pturned"], g * 2 + hh + 1)
                act.activation(t_pt[hh], bank(2 - 2 * hh, 0, SCORE), ACT.Copy).then_inc(at["pcopied"], 1)

            def out_squares(g, hh):
                act.wait_ge(at["o"], g * 2 + hh + 1)
                for t in range(NT):
                    act.activation(t_sq[:, t, 0:T], bank(3 - 2 * hh, t * T, T), ACT.Square,
                                   accum_out=o_ssq[hh][:, t:t + 1])
                act.drain().then_inc(at["osq"], 1)

            def out_root(g, hh):
                act.wait_ge(at["ovar"], g * 2 + hh + 1)
                act.activation(o_root[hh], o_var[hh], ACT.Sqrt).then_inc(at["oroot"], 1)

            def y_high(g, hh):
                act.wait_ge(at["yturned"], g * 2 + hh + 1)
                act.activation(y_hi[:, bass.ds(g * 4 + 2 * hh, 2), :],
                               bank(2 - 2 * hh).rearrange("p (n t) -> p n t", t=T), ACT.Copy).then_inc(at["yhigh"], 1)

            def group(g, last):
                splits(high, act, fl, hooks={0: lambda: head_rows(g, 0), 2: lambda: head_root(g, 0),
                                             7: lambda: copy_turned(g, 0)})
                splits(high, act, fl, hooks={0: lambda: head_rows(g, 1), 2: lambda: head_root(g, 1),
                                             7: lambda: copy_turned(g, 1)})
                splits(high, act, fl, hooks={0: lambda: v_out(g), 3: lambda: exps(g, 0), 4: lambda: exps(g, 1),
                                             6: lambda: exps(g, 2), 7: lambda: exps(g, 3)})
                tail = {0: lambda: s_out(g), 2: lambda: copy_probs(g, 0), 3: lambda: out_squares(g, 0),
                        4: lambda: (copy_probs(g, 1), out_root(g, 0)), 5: lambda: out_squares(g, 1),
                        6: lambda: (y_high(g, 0), out_root(g, 1))}
                if last:
                    tail[6] = lambda: (y_high(g, 0), out_root(g, 1), y_high(g, 1))
                    return tail
                splits(high, act, fl, hooks=tail)
                y_high(g, 1)

            return att_groups(act, fl, lambda: splits(high, act, fl), group)

        def dve_att(dve, fl):
            dr = dve.drain
            dve.wait_ge(at["loads"], 32)
            lr = lam_rows.rearrange("p (a b d) -> p a b d", a=2, b=2)
            pr = wk(0, 256).rearrange("p (a d) -> p a d", a=2)
            dve.tensor_tensor(pr, lr[:, :, 0, :], lr[:, :, 1, :], ALU.mult)
            dr()
            dve.tensor_reduce(lam2, pr, AX.X, ALU.add)
            dve.drain().then_inc(at["lam"], 1)
            dve.wait_ge(at["lamexp"], 1)
            dve.tensor_tensor(lam, lam2[:, 1:2], lam2[:, 0:1], ALU.subtract)
            dr()
            dve.tensor_scalar(lam, lam, -LAM_INIT, None, ALU.add)
            dr()
            cos, sin = (kept(n).rearrange("p (t a) -> p t a", t=NT) for n in ("cos", "sin"))
            def head_scale(g, n):
                dve.wait_ge(at["sq"], g * 2 + n + 1)
                dve.tensor_reduce(t_ssq.rearrange("p (t n) -> p t n", t=NT),
                                  t_sq.rearrange("p t (n d) -> p t n d", d=P), AX.X, ALU.add)
                dr()
                dve.tensor_scalar(t_var[n], t_ssq, 1.0 / P, EPS, ALU.mult, ALU.add).then_inc(at["var"], 1)

            def head_norm(g, n):
                gain = (q_gain, k_gain)[n]
                dve.wait_ge(at["root"], g * 2 + n + 1)
                dve.reciprocal(t_scale, t_root[n])
                dr()
                for t in range(NT):
                    v = t_raws[n][:, t, :].rearrange("p (n d) -> p n d", d=P)
                    dve.tensor_tensor(v, v, bc(t_scale[:, 4 * t:4 * t + 4], P), ALU.mult)
                dr()
                for t in range(NT):
                    v = t_raws[n][:, t, :].rearrange("p (n d) -> p n d", d=P)
                    dve.tensor_tensor(v, v, gain.unsqueeze(1).to_broadcast([P, 4, P]), ALU.mult)
                dr()
                for t in range(NT):
                    v = t_raws[n][:, t, :].rearrange("p (n d) -> p n d", d=P)
                    x1, x2 = v[:, :, 0:HALF], v[:, :, HALF:ROPE]
                    cc, ss = (a[:, t, :].unsqueeze(1).to_broadcast([P, 4, HALF]) for a in (cos, sin))
                    r4 = [a[:, 4 * t:4 * t + 4, :] for a in rope_t]
                    dve.tensor_tensor(r4[0], x1, cc, ALU.mult)
                    dve.tensor_tensor(r4[1], x2, ss, ALU.mult)
                    dve.tensor_tensor(r4[2], x2, cc, ALU.mult)
                    dve.tensor_tensor(r4[3], x1, ss, ALU.mult)
                dr()
                for t in range(NT):
                    v = t_raws[n][:, t, :].rearrange("p (n d) -> p n d", d=P)
                    r4 = [a[:, 4 * t:4 * t + 4, :] for a in rope_t]
                    dve.tensor_tensor(v[:, :, 0:HALF], r4[0], r4[1], ALU.subtract)
                    dve.tensor_tensor(v[:, :, HALF:ROPE], r4[2], r4[3], ALU.add)
                dve.drain().then_inc(at["rows"], 1)

            def gate_rows(g):
                dve.wait_ge(at["s"], g + 1)
                for t in range(NT):
                    v = t_s[:, t, :].rearrange("p (a d) -> p a d", d=2 * P)
                    dve.scalar_tensor_tensor(v, v, 1.0 - LAM_INIT, sub_gain.unsqueeze(1).to_broadcast([P, 2, 2 * P]),
                                             ALU.mult, ALU.mult)

            def maxima(g, n):
                dve.wait_ge(at["scores"], g * 4 + n + 1)
                dve.scalar_tensor_tensor(t_p[n], bank(n % 2, 0, SCORE), float(P) ** -0.5, t_mask, ALU.mult,
                                         ALU.add).then_inc(at["read"], 1)
                dr()
                dve.tensor_reduce(t_nm[n][:, 1:2], t_p[n][:, 0:T], AX.X, ALU.max)
                dve.tensor_reduce(t_nm[n][:, 0:1], t_p[n][:, T:SCORE], AX.X, ALU.max)
                dr()
                dve.tensor_scalar(t_nm[n], t_nm[n], -1.0, None, ALU.mult)
                dve.drain().then_inc(at["max"], 1)

            def mixed(g, hh):
                dve.wait_ge(at["exp"], g * 4 + 2 * hh + 2)
                n0, n1 = 2 * hh, 2 * hh + 1
                dve.reciprocal(t_r[n0], t_den[n0])
                dve.reciprocal(t_r[n1], t_den[n1])
                dr()
                dve.tensor_scalar(t_r[n1], t_r[n1], lam, None, ALU.mult)
                for t, (a, b) in enumerate(((T, SCORE), (0, T))):
                    dve.tensor_scalar(t_a[hh][:, a:b], t_p[n0][:, a:b], t_r[n0][:, t:t + 1], None, ALU.mult)
                dr()
                for t, (a, b) in enumerate(((T, SCORE), (0, T))):
                    dve.scalar_tensor_tensor(t_a[hh][:, a:b], t_p[n1][:, a:b], t_r[n1][:, t:t + 1],
                                             t_a[hh][:, a:b], ALU.mult, ALU.add)
                dve.drain().then_inc(at["mixed"], 1)

            def out_var(g, hh):
                dve.wait_ge(at["osq"], g * 2 + hh + 1)
                dve.tensor_scalar(o_var[hh], o_ssq[hh], 1.0 / (2 * P), 1e-5, ALU.mult, ALU.add).then_inc(at["ovar"], 1)

            def y_rows(g, hh):
                dve.wait_ge(at["oroot"], g * 2 + hh + 1)
                dve.reciprocal(o_scale[hh], o_root[hh])
                dr()
                for t in range(NT):
                    m = dve.scalar_tensor_tensor(t_ys[hh][:, t, :], bank(3 - 2 * hh, t * T, T), o_scale[hh][:, t:t + 1],
                                                 t_s[:, t, hh * T:hh * T + T], ALU.mult, ALU.mult)
                m.then_inc(at["y"], 1)

            def y_low(g, hh):
                dve.wait_ge(at["yhigh"], g * 2 + hh + 1)
                ys = bass.ds(g * 4 + 2 * hh, 2)
                dve.tensor_tensor(y_lo[:, ys, :], bank(2 - 2 * hh).rearrange("p (n t) -> p n t", t=T), y_hi[:, ys, :],
                                  ALU.subtract).then_inc(at["ylow"], 1)

            def group(g, last):
                splits(low, dve, fl, hooks={1: lambda: head_scale(g, 0), 3: lambda: head_norm(g, 0)})
                splits(low, dve, fl, hooks={1: lambda: head_scale(g, 1), 3: lambda: head_norm(g, 1)})
                splits(low, dve, fl, hooks={2: lambda: maxima(g, 0), 3: lambda: maxima(g, 1),
                                            5: lambda: maxima(g, 2), 6: lambda: maxima(g, 3)})
                tail = {0: lambda: mixed(g, 0), 1: lambda: gate_rows(g), 2: lambda: mixed(g, 1),
                        4: lambda: (out_var(g, 0), y_rows(g, 0)),
                        6: lambda: (out_var(g, 1), y_rows(g, 1), y_low(g, 0))}
                if last:
                    tail[6] = lambda: (out_var(g, 1), y_rows(g, 1), y_low(g, 0), y_low(g, 1))
                    return tail
                splits(low, dve, fl, hooks=tail)
                y_low(g, 1)

            return att_groups(dve, fl, lambda: splits(low, dve, fl), group)

        def sp_att(sp, fl):
            w = d["att_w_in_2"][0]

            def group(g, last):
                for n in range(1, 4):
                    load_chunk(sp, fl, w, 0, g * W + n * D)
                if not last:
                    load_chunk(sp, fl, w, 0, g * W + W)

            att_groups(sp, fl, lambda: load_chunk(sp, fl, w, 0, 0), group)

        def sum_pe(pe, fl, head=None):
            for c in range(D // W):
                product(pe, fl, y_parts, hooks=None if c else head)

        def sum_act(act, fl, head=None, last=False):
            for c in range(D // W):
                splits(high, act, fl, hooks=None if c else head, last=last and c == D // W - 1)

        def sum_dve(dve, fl, head=None, last=False):
            for c in range(D // W):
                splits(low, dve, fl, last=last and c == D // W - 1,
                       hooks={0: lambda: add_to_h(dve, fl, c - 1, last)} if c else head)
            add_to_h(dve, fl, D // W - 1, last)

        def sum_sp(sp, fl, wt, row):
            for c in range(D // W):
                load_chunk(sp, fl, wt, row, c * W)

        fin_ready = sem("h_ready")
        fin_sum = sem("stored")
        block = ctx.enter_context(nc.Block())

        @block.sync
        def _(sp):
            fl = Flow()
            sp.dma_start(h[:], d["x"][0].rearrange("(t p) n -> p t n", p=P)).then_inc(start_loads, 16)
            sp.dma_start(keep[:], d["tables"][:, 0:keep_n]).then_inc(start_loads, 16)
            vrows = wk(9000, 2 * P).rearrange("p (a b) -> p a b", a=2)
            for i, n in enumerate(vec_names):
                sp.dma_start(vrows[16 * i:16 * i + 16, 0, :], d[n].rearrange("a (k p) -> (a k) p", p=P)).then_inc(
                    start_loads, 16)
            sp.dma_start(vrows[0:64, 1, :], d["rg_conv_w_2"][0].rearrange("t (k p) -> (t k) p", p=P)).then_inc(
                start_loads, 16)
            sp.dma_start(vrows[64:80, 1, :], d["rg_conv_b_2"].rearrange("a (k p) -> (a k) p", p=P)).then_inc(
                start_loads, 16)
            w = d["w_in"][0]
            for name, column in W_IN:
                load_chunk(sp, fl, w, 0, column * W, n=256 if name == "kvb" else W)
            sum_sp(sp, fl, d["w_out"][0], 0)
            with fl.loop(sp, N_GROUPS, MOE_UNITS, MOE_CHUNKS) as g:
                moe_sp(sp, fl, g)
            sp.wait_ge(r_done, 1)
            flag = sp.value_load(ovf[0:1, 0:1], min_val=0, max_val=1)
            over = sp.value_load(ovf[0:1, 1:2], min_val=0, max_val=N_GROUPS - 1)
            with fl.optional(sp, flag, MOE_UNITS, MOE_CHUNKS):
                moe_sp(sp, fl, over)
            for c in range(D // W):
                load_chunk(sp, fl, d["w_ple"][0], 0, c * W, units=1)
            sum_sp(sp, fl, d["w_ple_gate"][0], 0)
            sp_rg(sp, fl)
            sum_sp(sp, fl, d["rec_w_out_2"][0], 0)
            sp_hg(sp, fl)
            sum_sp(sp, fl, d["rec_w_out_2"][0], D)
            sp_att(sp, fl)
            sum_sp(sp, fl, d["att_w_out_2"][0], 0)
            for c in range(D // W):
                sp.wait_ge(fin_ready, c + 1)
                sp.dma_start(out[0].rearrange("(t p) n -> p t n", p=P)[:, :, c * W:(c + 1) * W],
                             h[:, :, c * W:(c + 1) * W]).then_inc(fin_sum, 16)
            sp.wait_ge(fin_sum, 16 * D // W)

        @block.gpsimd
        def _(pool):
            pool.dma_start(sinks, d["sinks"][0].partition_broadcast(P)).then_inc(row_loads, 16)
            pool.dma_start(route_b[:, 0:N_GROUPS], d["b_grp"][0].partition_broadcast(P)).then_inc(row_loads, 16)
            pool.dma_start(route_b[:, N_GROUPS:], d["b_exp"][0].rearrange("g e -> (g e)").partition_broadcast(P)
                           ).then_inc(row_loads, 16)
            for dst, n in ((hg_gain, "hg_out_norm_2"), (q_gain, "att_q_norm_2"), (k_gain, "att_k_norm_2"),
                           (sub_gain, "att_sub_norm_2")):
                pool.dma_start(dst, d[n][0].partition_broadcast(P)).then_inc(row_loads, 16)
            a = tab_at["delta"][0]
            pool.wait_ge(vecs_turned, 1)
            pool.dma_start(bias_tabs, d["tables"][:, a:a + 3 * SCORE]).then_inc(row_loads, 16)
            pool.wait_ge(p1_copied, PROJ["kvb"])
            pool.dma_start(kb[B_DIM:P, 0, :], kb[0:B_DIM, 0, :]).then_inc(keys_doubled, 16)
            pool.dma_start(kb[0:B_DIM, 1, :], kb[B_DIM:P, 1, :]).then_inc(keys_doubled, 16)
            pool.wait_ge(region_free, 1)
            pool.dma_start(gain_row, d["g_moe"][0].partition_broadcast(P)).then_inc(moe_loads, 16)
            with nc.allow_non_contiguous_dma(reason="router weights have short rows"):
                pool.dma_start(route_raw[:, :, 0:N_GROUPS],
                               d["w_grp"][0].rearrange("(k p) g -> p k g", p=P)).then_inc(moe_loads, 16)
                pool.dma_start(route_raw[:, :, N_GROUPS:],
                               d["w_exp"][0].rearrange("(k p) g e -> p k (g e)", p=P)).then_inc(moe_loads, 16)
            pool.wait_ge(moe_memory_free, 1)
            pool.dma_start(p_rows, d["p"][0, 0].rearrange("(t p) n -> p t n", p=P)).then_inc(ple_loads, 16)
            pool.dma_start(final_gain, d["g_final"].partition_broadcast(P)).then_inc(ple_loads, 16)
            pool.wait_ge(hg["free"], 1)
            a = tab_at["level1"][0]
            pool.dma_start(masks, d["tables"][:, a:a + n_masks * P]).then_inc(hg["loads"], 16)
            a = tab_at["reset"][0]
            pool.dma_start(reset, d["tables"][:, a:a + 1024]).then_inc(hg["loads"], 16)
            pool.wait_ge(at["free"], 1)
            a = tab_at["causal"][0]
            pool.dma_start(t_mask, d["tables"][:, a:a + SCORE]).then_inc(at["loads"], 16)
            pool.dma_start(lam_rows, d["att_lambda_2"][0].rearrange("a d -> (a d)").partition_broadcast(P)).then_inc(
                at["loads"], 16)

        vrows2 = wk(9000, 2 * P).rearrange("p (a b) -> p a b", a=2)

        @block.tensor
        def _(pe):
            fl = Flow()
            pe.nop().then_inc(unit_used, RING)
            pe.wait_ge(start_loads, 16 * 12)
            pe.transpose(bank(3, 0, P), vrows2[:, 0, :], ident)
            pe.transpose(bank(3, P, 80), vrows2[0:80, 1, :], ident[0:80, 0:80]).then_inc(vecs_turned, 1)
            pe.wait_ge(vecs_ready, 1)
            norm_pe(pe, norms["mix"], fills=FIRST_FILLS)
            def keys_and_values():
                ps = out_ps[fl.c % 2]
                pe.wait_ge(out_free, fl.chunk() + 1)
                for j in range(UNITS):
                    slot = (fl.u + j) % RING
                    pe.wait_ge(low_ready, fl.unit(j) + 1 + RING)
                    for r in range(UNIT_K):
                        k = UNIT_K * j + r
                        keys = slice(0, P)
                        for q, (wp, xp) in enumerate(((w_hi, x_hi), (w_hi, x_lo), (w_lo, x_hi))):
                            pe.matmul(ps[:, 0, 0:T], wp[:, slot, r, keys], xp[:, k, :], start=k == 0 and q == 0,
                                      stop=k == KD - 1 and q == 2, skip_group_check=True)
                        for t in range(NT):
                            for q, (xp, wp) in enumerate(((x_hi, w_hi), (x_hi, w_lo), (x_lo, w_hi))):
                                m = pe.matmul(ps[:, 1, t * P:t * P + P], xp[:, k, t * P:t * P + P],
                                              wp[:, slot, r, P:2 * P], start=k == 0 and t == 0 and q == 0,
                                              stop=k == KD - 1 and q == 2, skip_group_check=True)
                    m.then_inc(unit_used, 1)
                fl.next(UNITS)

            step_a, step_b = pe_attn_a(pe), pe_attn_b(pe)
            for n, (name, _) in enumerate(W_IN):
                if name == "kvb":
                    keys_and_values()
                else:
                    hooks = attn_hooks(n, None, step_a, step_b) if n else norm_hooks(pe, norms["mix"])
                    product(pe, fl, x_parts, by_channel=name[0] != "v", hooks=hooks)
            attn_rest(step_a, step_b)
            pe.wait_ge(s_ol, KD)
            sum_pe(pe, fl)
            norm_pe(pe, norms["moe"], rows=m_rows)
            route_pe(pe)
            pe.wait_ge(r_done, 1)
            flag = pe.value_load(ovf[0:1, 0:1], min_val=0, max_val=1)
            for f in range(8):
                gather_pe(pe, 0, f)
            with fl.loop(pe, N_GROUPS, MOE_UNITS, MOE_CHUNKS) as g:
                moe_pe(pe, fl, g)
            with fl.optional(pe, flag, MOE_UNITS, MOE_CHUNKS):
                moe_pe(pe, fl, N_GROUPS)
            norm_pe(pe, norms["ple"])
            pe.wait_ge(ple_loads, 32)
            for k in range(2):
                for t in range(NT):
                    m = pe.transpose(bank(0, k * T + t * P, P), p_rows[:, t, k * P:k * P + P], ident)
            m.then_inc(pt_turned, 1)
            pe.wait_ge(pt_low, 1)
            for _ in range(D // W):
                product(pe, fl, tokens_of(pt_hi, pt_lo), units=1)
            for _ in range(D // W):
                product(pe, fl, x_parts)
            norm_pe(pe, norms["rec"], fills=FIRST_FILLS)
            pe_rg(pe, fl)
            sum_pe(pe, fl, {6: lambda: pe.wait_ge(rg["ylow"], 4)})
            sum_pe(pe, fl, pe_hg(pe, fl))
            norm_pe(pe, norms["att"], fills=FIRST_FILLS)
            sum_pe(pe, fl, pe_att(pe, fl))

        @block.scalar
        def _(act):
            fl = Flow()
            act.wait_ge(vecs_turned, 1)
            act.activation(cols[:], bank(3, 0, 208), ACT.Copy)
            act.drain().then_inc(vecs_ready, 1)
            for j in range(RING):
                high(act, fl, j)
            norm_act(act, norms["mix"])

            def proj_out(name):
                chunk_done(act, fl)
                half = int(name[-1]) if name[-1].isdigit() else 0
                if name == "kvb":
                    for g in range(2):
                        lo_, hi_ = g * B_DIM, (g + 1) * B_DIM
                        act.activation(kb[lo_:hi_, g, :], chunk_ps(fl)[lo_:hi_, 0, 0:T], ACT.Copy)
                    dst, src = vb.rearrange("p n t -> p (n t)"), chunk_ps(fl)[:, 1, 0:T]
                elif name[0] == "v":
                    dst, src = va[:, :, half * W:half * W + W], chunk_ps(fl)[:]
                else:
                    at_, n = {"qa": (qk, 0), "ka": (qk, A_HEADS), "qb": (qb, 0)}[name[:2]]
                    dst, src = at_[:, n + 4 * half:n + 4 * half + 4, :], by_channel(fl)
                act.activation(dst, src, ACT.Copy).then_inc(p1_copied, 1)
                act.drain().then_inc(out_free, 1)

            step_a, step_b = act_attn_a(act), act_attn_b(act)
            for n in range(len(W_IN)):
                first = (lambda n=n: proj_out(W_IN[n - 1][0])) if n else None
                splits(high, act, fl, hooks=attn_hooks(n, first, step_a, step_b))
                if n == 1:
                    act.wait_ge(row_loads, 16 * 8)
            proj_out(W_IN[-1][0])
            attn_rest(step_a, step_b)
            sum_act(act, fl)
            act.wait_ge(moe_loads, 48)
            act.activation(route_hi, route_raw, ACT.Copy).then_inc(r_whi, 1)
            nm = norms["moe"]
            norm_stats_act(act, nm)
            act.wait_ge(m_rows, 1)
            act.activation(m_hi, xn, ACT.Copy).then_inc(m_split_hi, 1)
            for f in range(KD // 2):
                act.wait_ge(norm_s["turned"], nm.turns + f + 1)
                act.activation(x_hi[:, 2 * f:2 * f + 2, :], bank(f % 4).rearrange("p (n t) -> p n t", t=T),
                               ACT.Copy).then_inc(norm_s["high"], 1)
            route_act(act)
            act.wait_ge(r_done, 1)
            flag = act.value_load(ovf[0:1, 0:1], min_val=0, max_val=1)
            for b in range(4):
                gather_act(act, 0, b)
            with fl.loop(act, N_GROUPS, MOE_UNITS, MOE_CHUNKS) as g:
                moe_act(act, fl, g)
            with fl.optional(act, flag, MOE_UNITS, MOE_CHUNKS):
                moe_act(act, fl, N_GROUPS)
            norm_act(act, norms["ple"])
            act.wait_ge(pt_turned, 1)
            act.activation(pt_hi, bank(0).rearrange("p (n t) -> p n t", t=T), ACT.Copy).then_inc(pt_high, 1)

            def pp_out(c):
                chunk_done(act, fl)
                act.activation(pp[:, :, c * W:(c + 1) * W], chunk_ps(fl)[:], ACT.Copy)
                act.drain().then_inc(out_free, 1)

            def sig_out(c):
                chunk_done(act, fl)
                if c:
                    act.wait_ge(ple_used, c)
                act.activation(sig, chunk_ps(fl)[:], ACT.Sigmoid).then_inc(ple_sig, 1)
                act.drain().then_inc(out_free, 1)

            for c in range(D // W):
                splits(high, act, fl, units=1)
                pp_out(c)
            for c in range(D // W):
                splits(high, act, fl, hooks={0: lambda c=c: sig_out(c - 1)} if c else None)
            sig_out(D // W - 1)
            norm_stats_act(act, norms["final"])
            act.wait_ge(vecs_ready, 1)
            act.activation(sp_t[0], col["rg_lambda_2"], ACT.Abs)
            act.drain()
            act.activation(sp_t[0], sp_t[0], ACT.Exp, scale=-1.0).then_inc(rg["lam"], 1)
            norm_act(act, norms["rec"])
            sum_act(act, fl, act_rg(act, fl))
            sum_act(act, fl, act_hg(act, fl))
            norm_act(act, norms["att"])
            sum_act(act, fl, act_att(act, fl), last=True)

        @block.vector
        def _(dve):
            fl = Flow()
            dve.nop().then_inc(low_ready, RING)
            dve.nop().then_inc(out_free, 2)
            dve.nop().then_inc(hid_lo, 1)
            dve.nop().then_inc(sc_add, 1)
            dve.wait_ge(start_loads, 16 * 12)
            dve.wait_ge(vecs_ready, 1)
            for j in range(RING):
                low(dve, fl, j)
            norm_dve(dve, norms["mix"])
            dve.wait_ge(row_loads, 16 * 8)
            step_a, step_b = dve_attn_a(dve), dve_attn_b(dve)
            for n in range(len(W_IN)):
                splits(low, dve, fl, hooks=attn_hooks(n, None, step_a, step_b))
            attn_rest(step_a, step_b)
            dve.drain().then_inc(region_free, 1)
            sum_dve(dve, fl)
            dve.wait_ge(moe_loads, 48)
            dve.wait_ge(r_whi, 1)
            dve.tensor_tensor(route_lo, route_raw, route_hi, ALU.subtract).then_inc(r_wlo, 1)
            nm = norms["moe"]
            norm_stats_dve(dve, nm)
            dve.wait_ge(norm_s["scale"], nm.n + 1)
            for t in range(NT):
                dve.scalar_tensor_tensor(xn[:, t, :], h[:, t, :], scale[:, t:t + 1], gain_row, ALU.mult, ALU.mult)
            dve.drain().then_inc(m_rows, 1)
            dve.wait_ge(m_split_hi, 1)
            dve.tensor_tensor(m_lo, xn, m_hi, ALU.subtract)
            norm_low(dve, nm)
            route_dve(dve)
            flag = dve.value_load(ovf[0:1, 0:1], min_val=0, max_val=1)
            select_dve(dve, 0)
            for b in range(4):
                gather_dve(dve, 0, b)
            with fl.loop(dve, N_GROUPS, MOE_UNITS, MOE_CHUNKS) as g:
                moe_dve(dve, fl, g)
            with fl.optional(dve, flag, MOE_UNITS, MOE_CHUNKS):
                moe_dve(dve, fl, N_GROUPS)
            dve.drain().then_inc(moe_memory_free, 1)
            norm_dve(dve, norms["ple"])
            dve.wait_ge(pt_high, 1)
            dve.tensor_tensor(pt_lo, bank(0).rearrange("p (n t) -> p n t", t=T), pt_hi, ALU.subtract).then_inc(pt_low, 1)

            def gate_out(c):
                dve.wait_ge(ple_sig, c + 1)
                at_ = slice(c * W, (c + 1) * W)
                dve.tensor_tensor(sig2, sig, pp[:, :, at_], ALU.mult).then_inc(ple_used, 1)
                dve.drain()
                dve.tensor_tensor(h[:, :, at_], h[:, :, at_], sig2, ALU.add)

            for c in range(D // W):
                splits(low, dve, fl, units=1)
            for c in range(D // W):
                splits(low, dve, fl, hooks={0: lambda c=c: gate_out(c - 1)} if c else None)
            gate_out(D // W - 1)
            norm_stats_dve(dve, norms["final"])
            dve.wait_ge(norm_s["scale"], norms["final"].n + 1)
            dve.wait_ge(ple_loads, 32)
            for t in range(NT):
                dve.scalar_tensor_tensor(h[:, t, :], h[:, t, :], scale[:, t:t + 1], final_gain, ALU.mult, ALU.mult)
            dve.wait_ge(rg["lam"], 1)
            x_, z_, s_ = sp_t
            dve.tensor_scalar(z_, x_, 2.0, None, ALU.add)
            dve.drain()
            dve.reciprocal(s_, z_)
            dve.drain()
            dve.tensor_tensor(z_, x_, s_, ALU.mult)
            dve.drain()
            dve.tensor_tensor(x_, z_, z_, ALU.mult)
            dve.memset(s_, 1.0 / 17)
            dve.drain()
            for n in range(15, 0, -2):
                dve.tensor_tensor(s_, s_, x_, ALU.mult)
                dve.drain()
                dve.tensor_scalar(s_, s_, 1.0 / n, None, ALU.add)
                dve.drain()
            dve.tensor_tensor(s_, s_, z_, ALU.mult)
            dve.tensor_scalar(x_, col["rg_lambda_2"], -1.0, 0.0, ALU.mult, ALU.max)
            dve.drain()
            dve.scalar_tensor_tensor(s_, s_, 2.0, x_, ALU.mult, ALU.add)
            dve.drain()
            dve.tensor_scalar(decay, s_, 8.0, None, ALU.mult)
            norm_dve(dve, norms["rec"])
            head = dve_rg(dve, fl)
            dve.drain().then_inc(hg["free"], 1)
            sum_dve(dve, fl, head)
            sum_dve(dve, fl, dve_hg(dve, fl))
            dve.drain().then_inc(at["free"], 1)
            norm_dve(dve, norms["att"])
            sum_dve(dve, fl, dve_att(dve, fl), last=True)


_IN = ["x", "p", "w_in", "w_out", "sinks", "g_mix", "g_moe", "g_ple", "g_final", "w_grp", "b_grp", "w_exp", "b_exp",
       "w_gate", "w_up", "w_down", "w_ple", "w_ple_gate", "rec_norm_2", "rec_w_in_2", "rg_conv_w_2", "rg_conv_b_2",
       "rg_w_gate_a_2", "rg_b_gate_a_2", "rg_w_gate_x_2", "rg_b_gate_x_2", "rg_lambda_2", "hg_out_norm_2",
       "rec_w_out_2", "att_norm_2", "att_w_in_2", "att_q_norm_2", "att_k_norm_2", "att_lambda_2", "att_sub_norm_2",
       "att_w_out_2"]


def kernel(**inputs):
    import concourse.bacc as bacc
    from concourse.bass_utils import run_bass_kernel_spmd

    nc = bacc.Bacc("TRN2", target_bir_lowering=False, num_devices=1)
    table, tab_at = tables()
    arrays = {n: np.ascontiguousarray(inputs[n]) for n in _IN}
    arrays["tables"] = table
    d = {n: nc.dram_tensor(n, a.shape, F32, kind="ExternalInput").ap() for n, a in arrays.items()}
    out = nc.dram_tensor("out", (1, T, D), F32, kind="ExternalOutput").ap()
    program(nc, d, tab_at, out)
    r = run_bass_kernel_spmd(nc, [arrays], core_ids=[0])
    return r.results[0]["out"]
```
